# Optimizing a Trainium2 kernel written in Bass

```python
import math
import jax, jax.numpy as jnp
from jax import lax
import numpy as np

D_MODEL = 1024
BATCH = 1
SEQ = 2048
DEPTH = 1

N_MIXERS = 3
D_FF = 4 * D_MODEL
RMS_EPS = 1e-6
NEG_INF = -1e30
NUM_BUCKETS = 32
REL_MAX_DISTANCE = 2048
DA_HEAD_DIM = 64
DA_HEADS = D_MODEL // (2 * DA_HEAD_DIM)
DA_Q_BLOCK = 128
LRU_WIDTH = D_MODEL
LRU_BLOCK_WIDTH = 256
LRU_BLOCKS = LRU_WIDTH // LRU_BLOCK_WIDTH
CONV_WIDTH = 4
LRU_C = 8.0
DIL_HEAD_DIM = 64
DIL_HEADS = D_MODEL // DIL_HEAD_DIM
DIL_PATTERNS = ((128, 1), (512, 4), (2048, 16))
DIL_GROUPS = len(DIL_PATTERNS)
BAND_BLOCK = 128
N_BIAS_COLS = 2 * DA_HEADS

kernel_name = 'hybrid_diffattn_rglru_dilated_adaln'

def rms_norm(x, gain):
    xf = x.astype(jnp.float32)
    y = xf * lax.rsqrt(jnp.mean(xf * xf, axis=-1, keepdims=True) + RMS_EPS)
    return (y * gain.astype(jnp.float32)).astype(x.dtype)

def modulate(h, shift, scale):
    return h * (1.0 + scale[:, None, :]) + shift[:, None, :]

def t5_bucket(dist):
    n = jnp.maximum(dist, 0)
    max_exact = NUM_BUCKETS // 2
    nf = jnp.maximum(n, max_exact).astype(jnp.float32)
    large = max_exact + (jnp.log(nf / max_exact) / math.log(REL_MAX_DISTANCE / max_exact)
                         * (NUM_BUCKETS - max_exact)).astype(jnp.int32)
    large = jnp.minimum(large, NUM_BUCKETS - 1)
    return jnp.where(n < max_exact, n, large)

def differential_attention(h, w_qkv, w_o, q_gain, k_gain, lam_q1, lam_k1, lam_q2, lam_k2,
                           sub_gain, rel_bias, lambda_init):
    B, S, _ = h.shape
    q, k, v = jnp.split(h @ w_qkv, 3, axis=-1)
    q = rms_norm(q.reshape(B, S, DA_HEADS, 2, DA_HEAD_DIM), q_gain) * (DA_HEAD_DIM ** -0.5)
    k = rms_norm(k.reshape(B, S, DA_HEADS, 2, DA_HEAD_DIM), k_gain)
    v = v.reshape(B, S, DA_HEADS, 2 * DA_HEAD_DIM)
    lam = (jnp.exp(jnp.sum(lam_q1.astype(jnp.float32) * lam_k1.astype(jnp.float32)))
           - jnp.exp(jnp.sum(lam_q2.astype(jnp.float32) * lam_k2.astype(jnp.float32)))
           + lambda_init)
    bq = min(DA_Q_BLOCK, S)
    outs = []
    for j in range(S // bq):
        q0, kv_len = j * bq, (j + 1) * bq
        s = jnp.einsum('bqhmd,bkhmd->bhmqk', q[:, q0:kv_len], k[:, :kv_len]).astype(jnp.float32)
        dist = jnp.arange(q0, kv_len)[:, None] - jnp.arange(kv_len)[None, :]
        bias = rel_bias[t5_bucket(dist)].reshape(bq, kv_len, DA_HEADS, 2).transpose(2, 3, 0, 1)
        s = jnp.where(dist >= 0, s + bias.astype(jnp.float32), NEG_INF)
        p = jax.nn.softmax(s, axis=-1)
        p = p[:, :, 0] - lam * p[:, :, 1]
        outs.append(jnp.einsum('bhqk,bkhe->bqhe', p.astype(v.dtype), v[:, :kv_len]))
    o = jnp.concatenate(outs, axis=1)
    o = rms_norm(o, sub_gain) * (1.0 - lambda_init)
    return o.reshape(B, S, D_MODEL) @ w_o

def rglru_block(h, w_in, conv_w, conv_b, w_x, b_x, w_a, b_a, a_param, w_out):
    B, S, _ = h.shape
    y, u = jnp.split(h @ w_in, 2, axis=-1)
    u_pad = jnp.pad(u, ((0, 0), (CONV_WIDTH - 1, 0), (0, 0)))
    conv = conv_b
    for tap in range(CONV_WIDTH):
        start = CONV_WIDTH - 1 - tap
        conv = conv + u_pad[:, start:start + S] * conv_w[tap]
    u = conv
    ub = u.reshape(B, S, LRU_BLOCKS, LRU_BLOCK_WIDTH)
    gate_x = jax.nn.sigmoid((jnp.einsum('bsni,nij->bsnj', ub, w_x).reshape(B, S, LRU_WIDTH) + b_x).astype(jnp.float32))
    gate_a = jax.nn.sigmoid((jnp.einsum('bsni,nij->bsnj', ub, w_a).reshape(B, S, LRU_WIDTH) + b_a).astype(jnp.float32))
    log_a = -LRU_C * gate_a * jax.nn.softplus(-a_param.astype(jnp.float32))
    a = jnp.exp(log_a)
    b = jnp.sqrt(-jnp.expm1(2.0 * log_a)) * (gate_x * u.astype(jnp.float32))

    def combine(left, right):
        a_l, b_l = left
        a_r, b_r = right
        return a_l * a_r, a_r * b_l + b_r

    _, hs = lax.associative_scan(combine, (a, b), axis=1)
    out = hs.astype(h.dtype) * jax.nn.gelu(y, approximate=True)
    return out @ w_out

def dilated_branch(q, k, v, dilation, sub_window, rel_bias):
    B, S, H, d = q.shape
    L = S // dilation
    bq = min(BAND_BLOCK, L)
    nb = -(-L // bq)
    pad = nb * bq - L

    def to_blocks(t):
        t = t.reshape(B, L, dilation, H, d)
        t = jnp.pad(t, ((0, 0), (0, pad), (0, 0), (0, 0), (0, 0)))
        t = t.reshape(B, nb, bq, dilation, H, d).transpose(1, 0, 3, 4, 2, 5)
        return t.reshape(nb, B * dilation, H, bq, d)

    def with_prev(t):
        prev = jnp.concatenate([jnp.zeros_like(t[:1]), t[:-1]], axis=0)
        return jnp.concatenate([prev, t], axis=3)

    qb = to_blocks(q)
    kb = with_prev(to_blocks(k))
    vb = with_prev(to_blocks(v))
    rel = jnp.arange(bq)[:, None] + bq - jnp.arange(2 * bq)[None, :]
    band = (rel >= 0) & (rel <= sub_window)
    bias = rel_bias[t5_bucket(rel * dilation)].transpose(2, 0, 1).astype(jnp.float32)
    in_current = jnp.arange(2 * bq) >= bq

    def block_step(args):
        j, qj, kj, vj = args
        s = jnp.einsum('nhqd,nhkd->nhqk', qj, kj).astype(jnp.float32) + bias
        mask = band & ((j > 0) | in_current)[None, :]
        s = jnp.where(mask, s, NEG_INF)
        m = jnp.max(s, axis=-1, keepdims=True)
        p = jnp.exp(s - m)
        den = jnp.sum(p, axis=-1)
        o = jnp.einsum('nhqk,nhkd->nhqd', (p / den[..., None]).astype(vj.dtype), vj).astype(jnp.float32)
        return o, m[..., 0] + jnp.log(den)

    o, lse = lax.map(block_step, (jnp.arange(nb), qb, kb, vb))
    o = o.reshape(nb, B, dilation, H, bq, d).transpose(1, 0, 4, 2, 3, 5)
    o = o.reshape(B, nb * bq, dilation, H, d)[:, :L].reshape(B, S, H, d)
    lse = lse.reshape(nb, B, dilation, H, bq).transpose(1, 0, 4, 2, 3)
    lse = lse.reshape(B, nb * bq, dilation, H)[:, :L].reshape(B, S, H)
    return o, lse

def dilated_attention(h, w_qkv, w_o, q_gain, k_gain, rel_bias):
    B, S, _ = h.shape
    o_acc, lse_acc = None, None
    for g, (window, dilation) in enumerate(DIL_PATTERNS):
        cols = w_qkv[:, g * 3 * D_MODEL:(g + 1) * 3 * D_MODEL]
        q, k, v = jnp.split(h @ cols, 3, axis=-1)
        q = rms_norm(q.reshape(B, S, DIL_HEADS, DIL_HEAD_DIM), q_gain) * (DIL_HEAD_DIM ** -0.5)
        k = rms_norm(k.reshape(B, S, DIL_HEADS, DIL_HEAD_DIM), k_gain)
        v = v.reshape(B, S, DIL_HEADS, DIL_HEAD_DIM)
        o_g, lse_g = dilated_branch(q, k, v, dilation, window // dilation, rel_bias)
        if o_acc is None:
            o_acc, lse_acc = o_g, lse_g
        else:
            lse_new = jnp.logaddexp(lse_acc, lse_g)
            o_acc = (o_acc * jnp.exp(lse_acc - lse_new)[..., None]
                     + o_g * jnp.exp(lse_g - lse_new)[..., None])
            lse_acc = lse_new
    return o_acc.astype(h.dtype).reshape(B, S, D_MODEL) @ w_o

def squared_relu_mlp(h, w1, w2):
    return jnp.square(jax.nn.relu(h @ w1)) @ w2

def setup_inputs(seed: int = 0) -> dict:
    key = jax.random.key(seed)
    ks = iter(jax.random.split(key, 40))
    n_a = len(range(0, DEPTH, N_MIXERS))
    n_b = len(range(1, DEPTH, N_MIXERS))
    n_c = len(range(2, DEPTH, N_MIXERS))
    D, W = D_MODEL, LRU_WIDTH

    def nrm(shape, scale):
        return jax.random.normal(next(ks), shape, jnp.float32) * scale

    def gain(shape):
        return 1.0 + nrm(shape, 0.05)

    inp = {}
    inp['x'] = nrm((BATCH, SEQ, D), 1.0)
    inp['c'] = nrm((BATCH, D), 1.0)
    inp['rel_bias'] = nrm((NUM_BUCKETS, N_BIAS_COLS), 0.5)
    inp['w_ada'] = nrm((DEPTH, D, 6 * D), 0.5 * D ** -0.5)
    inp['b_ada'] = nrm((DEPTH, 6 * D), 0.02)
    inp['norm_mix'] = gain((DEPTH, D))
    inp['norm_mlp'] = gain((DEPTH, D))
    inp['mlp_w1'] = nrm((DEPTH, D, D_FF), D ** -0.5)
    inp['mlp_w2'] = nrm((DEPTH, D_FF, D), D_FF ** -0.5)
    inp['da_w_qkv'] = nrm((n_a, D, 3 * D), D ** -0.5)
    inp['da_w_o'] = nrm((n_a, D, D), D ** -0.5)
    inp['da_q_gain'] = gain((n_a, DA_HEAD_DIM))
    inp['da_k_gain'] = gain((n_a, DA_HEAD_DIM))
    inp['da_lam_q1'] = nrm((n_a, DA_HEAD_DIM), 0.1)
    inp['da_lam_k1'] = nrm((n_a, DA_HEAD_DIM), 0.1)
    inp['da_lam_q2'] = nrm((n_a, DA_HEAD_DIM), 0.1)
    inp['da_lam_k2'] = nrm((n_a, DA_HEAD_DIM), 0.1)
    inp['da_sub_gain'] = gain((n_a, 2 * DA_HEAD_DIM))
    inp['lru_w_in'] = nrm((n_b, D, 2 * W), D ** -0.5)
    inp['lru_conv_w'] = nrm((n_b, CONV_WIDTH, W), CONV_WIDTH ** -0.5)
    inp['lru_conv_b'] = nrm((n_b, W), 0.02)
    inp['lru_w_x'] = nrm((n_b, LRU_BLOCKS, LRU_BLOCK_WIDTH, LRU_BLOCK_WIDTH), LRU_BLOCK_WIDTH ** -0.5)
    inp['lru_b_x'] = nrm((n_b, W), 0.02)
    inp['lru_w_a'] = nrm((n_b, LRU_BLOCKS, LRU_BLOCK_WIDTH, LRU_BLOCK_WIDTH), LRU_BLOCK_WIDTH ** -0.5)
    inp['lru_b_a'] = nrm((n_b, W), 0.02)
    a_c = jax.random.uniform(next(ks), (n_b, W), jnp.float32, minval=0.9, maxval=0.999)
    a0 = a_c ** (1.0 / LRU_C)
    inp['lru_a_param'] = jnp.log(a0) - jnp.log1p(-a0)
    inp['lru_w_out'] = nrm((n_b, W, D), W ** -0.5)
    inp['dil_w_qkv'] = nrm((n_c, D, DIL_GROUPS * 3 * D), D ** -0.5)
    inp['dil_w_o'] = nrm((n_c, D, D), D ** -0.5)
    inp['dil_q_gain'] = gain((n_c, DIL_HEAD_DIM))
    inp['dil_k_gain'] = gain((n_c, DIL_HEAD_DIM))
    return inp

def reference(x, c, rel_bias, w_ada, b_ada, norm_mix, norm_mlp, mlp_w1, mlp_w2,
              da_w_qkv, da_w_o, da_q_gain, da_k_gain, da_lam_q1, da_lam_k1, da_lam_q2, da_lam_k2, da_sub_gain,
              lru_w_in, lru_conv_w, lru_conv_b, lru_w_x, lru_b_x, lru_w_a, lru_b_a, lru_a_param, lru_w_out,
              dil_w_qkv, dil_w_o, dil_q_gain, dil_k_gain):
    mod = jnp.einsum('bd,ldk->lbk', jax.nn.silu(c), w_ada) + b_ada[:, None, :]
    for i in range(DEPTH):
        shift1, scale1, gate1, shift2, scale2, gate2 = jnp.split(mod[i], 6, axis=-1)
        h = modulate(rms_norm(x, norm_mix[i]), shift1, scale1)
        kind, slot = i % N_MIXERS, i // N_MIXERS
        if kind == 0:
            lambda_init = 0.8 - 0.6 * math.exp(-0.3 * i)
            y = differential_attention(h, da_w_qkv[slot], da_w_o[slot], da_q_gain[slot], da_k_gain[slot],
                                       da_lam_q1[slot], da_lam_k1[slot], da_lam_q2[slot], da_lam_k2[slot],
                                       da_sub_gain[slot], rel_bias, lambda_init)
        elif kind == 1:
            y = rglru_block(h, lru_w_in[slot], lru_conv_w[slot], lru_conv_b[slot], lru_w_x[slot], lru_b_x[slot],
                            lru_w_a[slot], lru_b_a[slot], lru_a_param[slot], lru_w_out[slot])
        else:
            y = dilated_attention(h, dil_w_qkv[slot], dil_w_o[slot], dil_q_gain[slot], dil_k_gain[slot], rel_bias)
        x = x + gate1[:, None, :] * y
        h = modulate(rms_norm(x, norm_mlp[i]), shift2, scale2)
        x = x + gate2[:, None, :] * squared_relu_mlp(h, mlp_w1[i], mlp_w2[i])
    return x


_drawn_inputs = setup_inputs


def setup_inputs(seed=0):
    import zlib

    import numpy as np

    out = dict(_drawn_inputs(seed))
    spreads = {}
    factors = {'norm_mix': 8.0,
     'da_q_gain': 8.0,
     'da_k_gain': 8.0,
     'da_lam_q1': 8.0,
     'da_lam_k1': 28.46,
     'da_lam_q2': 8.0,
     'da_lam_k2': 8.0,
     'da_sub_gain': 4.732,
     'norm_mlp': 3.26}
    for name, (base, spread) in spreads.items():
        noise = np.random.default_rng([zlib.crc32(name.encode()), seed]).standard_normal(out[name].shape)
        drawn = base * np.exp(spread * noise) if base else spread * noise
        out[name] = __import__('jax').numpy.asarray(drawn.astype(out[name].dtype))
    for name, factor in factors.items():
        out[name] = (out[name] * factor).astype(out[name].dtype)
    return out
```

```python
import math
from contextlib import ExitStack

import concourse.bass as bass
import numpy as np
from concourse import mybir

F32 = mybir.dt.float32
F32R = mybir.dt.float32r
ALU = mybir.AluOpType
ACT = mybir.ActivationFunctionType
AX_X = mybir.AxisListType.X

P = 128
D = 1024
S = 2048
F = 4 * D
DB = D // P
TB = S // P
HD = 64
HEADS = D // (2 * HD)
BANK = 512
SUPER = S // BANK
EPS = 1e-6
LAMBDA_INIT = 0.8 - 0.6 * math.exp(-0.3 * 0)
BUCKETS = 32
REL_MAX = 2048
MASK = 1e30
DIAG = S + P
FAR = 3.0e38


def bucket_table():
    dist = S - 1 - np.arange(DIAG)
    n = np.maximum(dist, 0)
    exact = BUCKETS // 2
    nf = np.maximum(n, exact).astype(np.float32)
    steps = np.log(nf / np.float32(exact)) / np.float32(math.log(REL_MAX / exact)) * np.float32(BUCKETS - exact)
    large = np.minimum(exact + steps.astype(np.int32), BUCKETS - 1)
    bucket = np.where(n < exact, n, large)
    bucket = np.where(dist < 0, BUCKETS, bucket)
    return (np.arange(BUCKETS + 1)[:, None] == bucket[None, :]).astype(np.float32)


class Scratch:

    def __init__(self, nc):
        def dram(name, shape):
            return nc.dram_tensor(name, shape, F32, kind="Internal").ap()

        self.bias_row = dram("bias_row", (2 * HEADS, DIAG))
        self.bias_skew = dram("bias_skew", (2 * HEADS, P * (DIAG + 1)))
        self.qk_hi = dram("qk_hi", (2 * HEADS, P, S))
        self.qk_lo = dram("qk_lo", (2 * HEADS, P, S))
        self.v_hi = dram("v_hi", (HEADS, P, TB, P))
        self.v_lo = dram("v_lo", (HEADS, P, TB, P))
        self.o_t = dram("o_t", (HEADS, P, S))
        self.l_sum = dram("l_sum", (P, TB, HEADS))
        self.x1 = dram("x1", (S, D))
        self.h2_hi = dram("h2_hi", (P, DB, S))
        self.h2_lo = dram("h2_lo", (P, DB, S))


def f32(ap):
    return ap.bitcast(F32)


def settle(eng, passed):
    eng.sem_inc(passed, 1)


class Persist:

    def __init__(self, nc, ctx):
        def sb(name, shape, dt=F32):
            return ctx.enter_context(nc.sbuf_tensor(name, shape, dt))

        self.ident = sb("ident", [P, P])
        self.mod = sb("mod", [P, 6 * DB])
        self.affine = sb("affine", [P, 2, DB])
        self.neg_lambda = sb("neg_lambda", [P, 1])
        self.qk_gain = sb("qk_gain", [P, 4])
        self.sub_gain = sb("sub_gain", [P, 1])
        self.eps = sb("eps", [P, 1])
        self.passed = ctx.enter_context(nc.semaphore("passed"))


def modulate(nc, ins, keep, scr, ht_hi, ht_lo):
    ADA_N = 512
    CHUNKS = 6 * D // ADA_N
    CJ = ADA_N // P
    with ExitStack() as ctx:
        def sb(name, shape, dt=F32):
            return ctx.enter_context(nc.sbuf_tensor(name, shape, dt))

        def pb(name, shape):
            return ctx.enter_context(nc.psum_tensor(name, shape, F32))

        def sem(name):
            return ctx.enter_context(nc.semaphore(name))

        ada = sb("ada", [P, 2, DB, ADA_N])
        xg = sb("xg", [P, 4, D])
        sq = sb("sq_a", [P, D])
        tmp = sb("tmp_a", [P, 2, BANK])
        ccol = sb("ccol", [P, 2, DB])
        bcol = sb("bcol", [P, 6 * DB])
        ncol = sb("ncol", [P, 2, DB])
        lam = sb("lam", [P, 4, HD])
        lam_s = sb("lam_s", [P, 4])
        stat = sb("stat_a", [P, 2, TB])
        rel = sb("rel", [BUCKETS + 1, 2 * HEADS])
        hot = sb("hot", [BUCKETS + 1, DIAG])
        row = sb("row", [2 * HEADS, DIAG])
        ps_mod = pb("ps_mod", [P, 6 * DB])
        ps_row = pb("ps_row", [2 * HEADS, BANK])
        ps_t = [pb(f"ps_t{i}", [P, BANK]) for i in range(4)]

        small_in = sem("small_in")
        ada_in = [sem(f"ada_in{i}") for i in range(2)]
        x_in = sem("x_in")
        ident_ok = sem("ident_ok")
        pool_ok = sem("pool_ok")
        silu_a = sem("silu_a")
        silu_d = sem("silu_d")
        mod_part = sem("mod_part")
        mod_ok_d = sem("mod_ok_d")
        mod_ok = sem("mod_ok")
        lam_d = sem("lam_d")
        lam_a = sem("lam_a")
        rel_ok = sem("rel_ok")
        row_mm = sem("row_mm")
        row_ok = sem("row_ok")
        row_out = sem("row_out")
        skew_out = sem("skew_out")
        x_sq = sem("x_sq")
        x_sd = sem("x_sd")
        x_ri = sem("x_ri")
        x_n = sem("x_n")
        x_t = sem("x_t")
        h_f = sem("h_f")
        h_hi = sem("h_hi")
        h_lo = sem("h_lo")
        SMALL = 17

        ada_v = ins["w_ada"][0].rearrange("(b p) n -> p b n", p=P)
        x_v = ins["x"][0].rearrange("(t p) d -> p t d", p=P)

        with nc.Block() as block:
            @block.sync
            def _(sp):
                with nc.allow_non_contiguous_dma(reason="columns of small vectors"):
                    col = lambda a: a.rearrange("(b p) -> p b", p=P)
                    loads = [(ccol[:, 0, :], col(ins["c"][0])), (bcol[:], col(ins["b_ada"][0])),
                             (ncol[:, 0, :], col(ins["norm_mix"][0])), (ncol[:, 1, :], col(ins["norm_mlp"][0])),
                             (keep.sub_gain[:], col(ins["da_sub_gain"][0]))]
                    for half in range(2):
                        at = slice(half * HD, half * HD + HD)
                        for g, name in ((0, "da_q_gain"), (1, "da_q_gain"), (2, "da_k_gain"), (3, "da_k_gain")):
                            loads.append((keep.qk_gain[at, g:g + 1], ins[name][0].rearrange("(p b) -> p b", b=1)))
                    for n, name in enumerate(("da_lam_q1", "da_lam_k1", "da_lam_q2", "da_lam_k2")):
                        loads.append((lam[:, n, :], ins[name].to_broadcast([P, HD])))
                    assert len(loads) == SMALL
                    for to, src in loads:
                        sp.dma_start(to, src).then_inc(small_in, 16)
                sp.dma_start(rel[0:BUCKETS, :], ins["rel_bias"]).then_inc(small_in, 16)
                sp.dma_start(hot[:], ins["buckets"]).then_inc(small_in, 16)
                for n in range(CHUNKS):
                    if n >= 2:
                        sp.wait_ge(mod_part, n - 1)
                    sp.dma_start(ada[:, n % 2], ada_v[:, :, n * ADA_N:(n + 1) * ADA_N]).then_inc(ada_in[n % 2], 16)
                sp.wait_ge(row_ok, -(-DIAG // BANK))
                sp.dma_start(scr.bias_row, row[:]).then_inc(row_out, 16)
                sp.wait_ge(row_out, 16)
                for m in range(2 * HEADS):
                    sp.dma_start(scr.bias_skew[m].rearrange("(p y) -> p y", p=P)[:, 0:DIAG],
                                 scr.bias_row[m:m + 1, :].to_broadcast([P, DIAG])).then_inc(skew_out, 16)
                sp.wait_ge(skew_out, 16 * 2 * HEADS)

            @block.gpsimd
            def _(pool):
                nc.gpsimd.memset(keep.ident[:], 0.0).then_inc(pool_ok, 1)
                pool.wait_ge(pool_ok, 1)
                nc.gpsimd.affine_select(out=keep.ident[:], in_=keep.ident[:], compare_op=ALU.not_equal, fill=1.0,
                                        base=0, pattern=[[-1, P]], channel_multiplier=1).then_inc(ident_ok, 1)

            @block.scalar
            def _(act):
                for t in range(4):
                    act.dma_start(xg[:, t], x_v[:, t]).then_inc(x_in, 16)
                act.wait_ge(small_in, 16 * (SMALL + 2))
                nc.scalar.activation(ccol[:, 1, :], ccol[:, 0, :], ACT.Exp, scale=-1.0).then_inc(silu_a, 1)
                act.wait_ge(lam_d, 2)
                nc.scalar.activation(lam_s[:, 2:4], lam_s[:, 0:2], ACT.Exp).then_inc(lam_a, 1)
                act.wait_ge(silu_d, 1)
                for g in range(SUPER):
                    if g:
                        for t in range(4):
                            act.wait_ge(x_t, 8 * g)
                            act.dma_start(xg[:, t], x_v[:, 4 * g + t]).then_inc(x_in, 16)
                    for t in range(4 * g, 4 * g + 4):
                        act.wait_ge(x_in, 64 * (g + 1))
                        if t:
                            act.wait_ge(x_sq, t)
                        nc.scalar.activation(sq[:], xg[:, t % 4], ACT.Square,
                                             accum_out=stat[:, 0, t:t + 1]).then_inc(x_sq, 1)
                    act.wait_ge(x_sq, 4 * g + 4)
                    nc.scalar.activation(stat[:, 1, 4 * g:4 * g + 4], stat[:, 0, 4 * g:4 * g + 4], ACT.Sqrt,
                                         bias=keep.eps[:], scale=1.0 / D).then_inc(x_sd, 1)
                    for d in range(DB):
                        n = DB * g + d
                        act.wait_ge(x_t, n + 1)
                        act.wait_ge(mod_ok, 1)
                        if n >= 2:
                            act.wait_ge(h_lo, n - 1)
                        nc.scalar.activation(tmp[:, n % 2], ps_t[n % 4][:], ACT.Identity,
                                             bias=keep.mod[:, d:d + 1],
                                             scale=keep.affine[:, 0, d:d + 1]).then_inc(h_f, 1)

            @block.vector
            def _(dve):
                nc.vector.memset(keep.eps[:], EPS)
                nc.vector.memset(rel[BUCKETS:BUCKETS + 1, :], MASK).then_inc(silu_d, 1)
                dve.wait_ge(small_in, 16 * (SMALL + 2))
                nc.vector.tensor_scalar(rel[0:BUCKETS, :], rel[0:BUCKETS, :], -1.0, None, ALU.mult).then_inc(rel_ok, 1)
                for n in range(2):
                    nc.vector.tensor_tensor_reduce(lam[:, 2 * n], lam[:, 2 * n], lam[:, 2 * n + 1], 1.0, 0.0,
                                                   ALU.mult, ALU.add, lam_s[:, n:n + 1]).then_inc(lam_d, 1)
                nc.vector.tensor_scalar(keep.qk_gain[:, 0:2], keep.qk_gain[:, 0:2], -(HD ** -0.5), None, ALU.mult)
                nc.vector.tensor_scalar(keep.sub_gain[:], keep.sub_gain[:], 1.0 - LAMBDA_INIT, None, ALU.mult)
                dve.wait_ge(silu_a, 1)
                nc.vector.tensor_scalar(ccol[:, 1, :], ccol[:, 1, :], 1.0, None, ALU.add).then_inc(silu_d, 1)
                dve.wait_ge(silu_d, 2)
                nc.vector.reciprocal(ccol[:, 1, :], ccol[:, 1, :]).then_inc(silu_d, 1)
                dve.wait_ge(silu_d, 3)
                nc.vector.tensor_tensor(ccol[:, 0, :], ccol[:, 0, :], ccol[:, 1, :], ALU.mult).then_inc(silu_d, 1)
                dve.wait_ge(lam_a, 1)
                nc.vector.scalar_tensor_tensor(out=keep.neg_lambda[:], in0=lam_s[:, 3:4], scalar=-LAMBDA_INIT,
                                               in1=lam_s[:, 2:3], op0=ALU.add, op1=ALU.subtract)
                for n in range(-(-DIAG // BANK)):
                    w = min(BANK, DIAG - n * BANK)
                    dve.wait_ge(row_mm, n + 1)
                    nc.vector.tensor_copy(row[:, n * BANK:n * BANK + w], ps_row[:, 0:w]).then_inc(row_ok, 1)

                def scale_rows(g):
                    dve.wait_ge(x_sd, g + 1)
                    nc.vector.reciprocal(stat[:, 1, 4 * g:4 * g + 4], stat[:, 1, 4 * g:4 * g + 4]).then_inc(x_ri, 1)
                    dve.wait_ge(x_ri, g + 1)
                    for t in range(4):
                        nc.vector.tensor_scalar(xg[:, t], xg[:, t], stat[:, 1, 4 * g + t:4 * g + t + 1], None,
                                                ALU.mult).then_inc(x_n, 1)

                def columns(part, n0, n1):
                    dve.wait_ge(mod_part, n1)
                    a, b = n0 * CJ, n1 * CJ
                    nc.vector.tensor_tensor(keep.mod[:, a:b], ps_mod[:, a:b], bcol[:, a:b], ALU.add).then_inc(mod_ok_d, 1)
                    dve.wait_ge(mod_ok_d, part + 1)
                    sc = DB if part == 0 else 4 * DB
                    nc.vector.scalar_tensor_tensor(out=keep.affine[:, part, :], in0=keep.mod[:, sc:sc + DB], scalar=1.0,
                                                   in1=ncol[:, part, :], op0=ALU.add, op1=ALU.mult).then_inc(mod_ok, 1)

                scale_rows(0)
                columns(0, 0, 4)
                for g in range(SUPER):
                    if g:
                        scale_rows(g)
                    for d in range(DB):
                        n = DB * g + d
                        at = slice(g * BANK, (g + 1) * BANK)
                        dve.wait_ge(h_f, n + 1)
                        nc.vector.tensor_copy(ht_hi[:, d, at], tmp[:, n % 2]).then_inc(h_hi, 1)
                        dve.wait_ge(h_hi, n + 1)
                        nc.vector.tensor_tensor(ht_lo[:, d, at], tmp[:, n % 2], f32(ht_hi[:, d, at]),
                                                ALU.subtract).then_inc(h_lo, 1)
                columns(1, 4, CHUNKS)

            @block.tensor
            def _(pe):
                def ada_chunk(n):
                    pe.wait_ge(ada_in[n % 2], 16 * (n // 2 + 1))
                    for j in range(CJ):
                        for b in range(DB):
                            mm = nc.tensor.matmul(ps_mod[:, n * CJ + j:n * CJ + j + 1], ada[:, n % 2, b, j * P:(j + 1) * P],
                                                  ccol[:, 0, b:b + 1], start=(b == 0), stop=(b == DB - 1))
                    mm.then_inc(mod_part, 1)

                def transposes(g):
                    pe.wait_ge(x_n, 4 * g + 4)
                    for d in range(DB):
                        n = DB * g + d
                        if n >= 4:
                            pe.wait_ge(h_f, n - 3)
                        for t in range(4):
                            mm = nc.tensor.transpose(ps_t[n % 4][:, t * P:(t + 1) * P], xg[:, t, d * P:(d + 1) * P],
                                                     keep.ident[:])
                        mm.then_inc(x_t, 1)

                pe.wait_ge(rel_ok, 1)
                pe.wait_ge(silu_d, 1)
                for n in range(-(-DIAG // BANK)):
                    w = min(BANK, DIAG - n * BANK)
                    if n:
                        pe.wait_ge(row_ok, n)
                    nc.tensor.matmul(ps_row[:, 0:w], rel[:], hot[:, n * BANK:n * BANK + w], start=True,
                                     stop=True).then_inc(row_mm, 1)
                pe.wait_ge(silu_d, 4)
                for n in range(4):
                    ada_chunk(n)
                pe.wait_ge(ident_ok, 1)
                for g in range(SUPER):
                    transposes(g)
                    ada_chunk(4 + 2 * g)
                    ada_chunk(5 + 2 * g)


def project(nc, ins, keep, scr, ht_hi, ht_lo):
    with ExitStack() as ctx:
        def sb(name, shape, dt=F32):
            return ctx.enter_context(nc.sbuf_tensor(name, shape, dt))

        def pb(name, shape):
            return ctx.enter_context(nc.psum_tensor(name, shape, F32))

        def sem(name):
            return ctx.enter_context(nc.semaphore(name))

        w_raw = sb("w_raw", [P, DB, BANK])
        w_hi = sb("w_hi", [P, DB, BANK], F32R)
        w_lo = sb("w_lo", [P, DB, BANK], F32R)
        sq = sb("sq_b", [P, 2, BANK])
        st = sb("st_b", [P, 2, 2, 8])
        qn = sb("qn", [P, 2, BANK])
        qt = sb("qt", [P, 2, BANK])
        p_hi = sb("p_hi", [P, 2, BANK], F32R)
        p_lo = sb("p_lo", [P, 2, BANK], F32R)
        ps = [pb(f"ps_p{i}", [P, BANK]) for i in range(4)]
        pst = [pb(f"ps_q{i}", [P, BANK]) for i in range(2)]

        w_in = [sem(f"w_in{b}") for b in range(DB)]
        w_hi_ok = sem("w_hi_ok")
        w_lo_ok = sem("w_lo_ok")
        w_free = sem("w_free")
        mm_ok = sem("mm_ok")
        sq_ok = sem("sq_ok")
        ss_ok = sem("ss_ok")
        sd_ok = sem("sd_ok")
        ri_ok = sem("ri_ok")
        ps_free = sem("ps_free")
        t_ok = sem("t_ok")
        qt_ok = sem("qt_ok")
        hi_ok = sem("hi_ok")
        lo_ok = sem("lo_ok")
        v_hi_ok = sem("v_hi_ok")
        stored = [sem(f"stored{i}") for i in range(2)]

        QK, V = 4, 2
        w_v = ins["da_w_qkv"][0].rearrange("(b p) n -> p b n", p=P)
        qkh = scr.qk_hi.rearrange("i p s -> p i s")
        qkl = scr.qk_lo.rearrange("i p s -> p i s")
        vh = scr.v_hi.rearrange("h p t e -> p h t e")
        vl = scr.v_lo.rearrange("h p t e -> p h t e")

        with nc.Block() as block:
            def split_hi(act, c, first=False):
                for b in range(DB):
                    act.wait_ge(w_in[b], c * 16 + 16)
                    if not first and b < DB - 1:
                        act.wait_ge(w_free, (c - 1) * (DB - 1) + b + 1)
                    elif not first:
                        act.wait_ge(mm_ok, c * TB)
                    nc.scalar.copy(w_hi[:, b], w_raw[:, b]).then_inc(w_hi_ok, 1)

            def split_lo(dve, c):
                for b in range(DB):
                    dve.wait_ge(w_hi_ok, c * DB + b + 1)
                    nc.vector.tensor_tensor(w_lo[:, b], w_raw[:, b], f32(w_hi[:, b]),
                                            ALU.subtract).then_inc(w_lo_ok, 1)

            heads = lambda a: f32(a).rearrange("p (h n) -> p h n", h=4)

            @block.sync
            def _(sp):
                def load(c):
                    for b in range(DB):
                        sp.dma_start(w_raw[:, b], w_v[:, b, bass.ds(c * BANK, BANK)]).then_inc(w_in[b], 16)

                def load_next(c):
                    sp.wait_ge(w_hi_ok, c * DB + DB)
                    sp.wait_ge(w_lo_ok, c * DB + DB)
                    settle(sp, keep.passed)
                    load(c + 1)

                sp.sem_inc(ps_free, 4)
                sp.sem_inc(t_ok, 2)
                sp.sem_inc(qt_ok, 2)
                sp.sem_inc(lo_ok, 2)
                for parity in range(2):
                    sp.sem_inc(stored[parity], 32)
                load(0)
                with sp.Fori(0, QK) as c:
                    load_next(c)
                    for t in range(TB):
                        sp.wait_ge(hi_ok, c * TB + t + 1)
                        settle(sp, keep.passed)
                        sp.dma_start(qkh[:, bass.ds(c * 4, 4), t * P:(t + 1) * P], heads(p_hi[:, t % 2])).then_inc(
                            stored[t % 2], 16)
                        sp.wait_ge(lo_ok, c * TB + t + 3)
                        settle(sp, keep.passed)
                        sp.dma_start(qkl[:, bass.ds(c * 4, 4), t * P:(t + 1) * P], heads(p_lo[:, t % 2])).then_inc(
                            stored[t % 2], 16)
                for v in range(V):
                    if v < V - 1:
                        load_next(QK + v)
                    for t in range(TB):
                        sp.wait_ge(v_hi_ok, v * TB + t + 1)
                        sp.dma_start(vh[:, 4 * v:4 * v + 4, t], heads(p_hi[:, t % 2])).then_inc(stored[t % 2], 16)
                        sp.wait_ge(ps_free, (QK + v) * TB + t + 5)
                        sp.dma_start(vl[:, 4 * v:4 * v + 4, t], heads(p_lo[:, t % 2])).then_inc(stored[t % 2], 16)
                for parity in range(2):
                    sp.wait_ge(stored[parity], 32 * (1 + (QK + V) * TB // 2))

            @block.gpsimd
            def _(pool):
                with pool.Fori(0, QK) as c:
                    for t in range(TB):
                        n = c * TB + t
                        pool.wait_ge(qt_ok, n + 3)
                        pool.wait_ge(stored[t % 2], (c * (TB // 2) + t // 2 + 1) * 32)
                        settle(pool, keep.passed)
                        nc.gpsimd.tensor_copy(p_hi[:, t % 2], qt[:, t % 2]).then_inc(hi_ok, 1)
                        pool.wait_ge(hi_ok, n + 1)
                        nc.gpsimd.tensor_tensor(p_lo[:, t % 2], qt[:, t % 2], f32(p_hi[:, t % 2]),
                                                ALU.subtract).then_inc(lo_ok, 1)

            @block.scalar
            def _(act):
                split_hi(act, 0, first=True)
                with act.Fori(0, QK) as c:
                    for t in range(TB):
                        n = c * TB + t
                        act.wait_ge(mm_ok, n + 1)
                        nc.scalar.activation(sq[:, t % 2], ps[t % 4][:], ACT.Square).then_inc(sq_ok, 1)
                        act.wait_ge(ss_ok, n + 1)
                        nc.scalar.activation(st[:, t % 2, 1], st[:, t % 2, 0], ACT.Sqrt, bias=keep.eps[:],
                                             scale=1.0 / HD).then_inc(sd_ok, 1)
                        if t == TB - 2:
                            split_hi(act, c + 1)
                        act.wait_ge(t_ok, n + 3)
                        act.wait_ge(lo_ok, n + 1)
                        settle(act, keep.passed)
                        nc.scalar.activation(qt[:, t % 2], pst[t % 2][:], ACT.Copy,
                                             scale=keep.qk_gain[:, bass.ds(c, 1)]).then_inc(qt_ok, 1)
                for v in range(V):
                    for t in range(TB):
                        if v < V - 1 and t == TB - 1:
                            split_hi(act, QK + v + 1)
                        act.wait_ge(mm_ok, (QK + v) * TB + t + 1)
                        act.wait_ge(stored[t % 2], 32 * (QK * TB // 2 + (v * TB + t) // 2 + 1))
                        nc.scalar.copy(p_hi[:, t % 2], ps[t % 4][:]).then_inc(v_hi_ok, 1)

            @block.vector
            def _(dve):
                split_lo(dve, 0)
                with dve.Fori(0, QK) as c:
                    for t in range(TB):
                        n = c * TB + t
                        if t == TB - 1:
                            split_lo(dve, c + 1)
                        dve.wait_ge(sq_ok, n + 1)
                        nc.vector.tensor_reduce(st[:, t % 2, 0], sq[:, t % 2].rearrange("p (g d) -> p g d", d=HD), AX_X,
                                                ALU.add).then_inc(ss_ok, 1)
                        dve.wait_ge(sd_ok, n + 1)
                        nc.vector.reciprocal(st[:, t % 2, 1], st[:, t % 2, 1]).then_inc(ri_ok, 1)
                        dve.wait_ge(ri_ok, n + 1)
                        dve.wait_ge(t_ok, n + 1)
                        nc.vector.tensor_tensor(qn[:, t % 2].rearrange("p (g d) -> p g d", d=HD),
                                                ps[t % 4][:].rearrange("p (g d) -> p g d", d=HD),
                                                st[:, t % 2, 1].rearrange("p (g b) -> p g b", b=1).to_broadcast([P, 8, HD]),
                                                ALU.mult).then_inc(ps_free, 1)
                for v in range(V):
                    for t in range(TB):
                        if v < V - 1 and t == TB - 1:
                            split_lo(dve, QK + v + 1)
                        dve.wait_ge(v_hi_ok, v * TB + t + 1)
                        nc.vector.tensor_tensor(p_lo[:, t % 2], ps[t % 4][:], f32(p_hi[:, t % 2]),
                                                ALU.subtract).then_inc(ps_free, 1)

            @block.tensor
            def _(pe):
                def product(c, t):
                    n = c * TB + t
                    pe.wait_ge(ps_free, n + 1)
                    tok = slice(t * P, (t + 1) * P)
                    for b in range(DB):
                        if t == 0:
                            pe.wait_ge(w_lo_ok, c * DB + b + 1)
                        nc.tensor.matmul(ps[t % 4][:], ht_hi[:, b, tok], w_hi[:, b], start=(b == 0), stop=False)
                        nc.tensor.matmul(ps[t % 4][:], ht_hi[:, b, tok], w_lo[:, b], start=False, stop=False)
                        mm = nc.tensor.matmul(ps[t % 4][:], ht_lo[:, b, tok], w_hi[:, b], start=False, stop=(b == DB - 1))
                        if t == TB - 1 and b < DB - 1:
                            mm.then_inc(w_free, 1)
                    mm.then_inc(mm_ok, 1)

                def transposes(c, t):
                    n = c * TB + t
                    pe.wait_ge(ps_free, n + 5)
                    pe.wait_ge(qt_ok, n + 1)
                    for k in range(4):
                        mm = nc.tensor.transpose(pst[t % 2][:, k * P:(k + 1) * P], qn[:, t % 2, k * P:(k + 1) * P],
                                                 keep.ident[:])
                    mm.then_inc(t_ok, 1)

                product(0, 0)
                with pe.Fori(0, QK) as c:
                    for t in range(1, TB):
                        product(c, t)
                        transposes(c, t - 1)
                    product(c + 1, 0)
                    transposes(c, TB - 1)
                for v in range(V):
                    for t in range(1 if v == 0 else 0, TB):
                        product(QK + v, t)


def attend(nc, keep, scr):
    UNIT = 2 * BANK
    STEPS = TB

    def keys(i):
        return (STEPS - i) * P

    def units(i):
        return -(-keys(i) // UNIT)

    def groups(i):
        return -(-keys(i) // BANK)

    def units_before(i):
        return sum(2 * units(k) for k in range(i))

    def groups_before(i):
        return sum(groups(k) for k in range(i))

    UNITS, GROUPS = units_before(STEPS), groups_before(STEPS)
    PV_GROUPS = sum(range(1, SUPER + 1))

    def pv_before(q):
        return sum(SUPER - k for k in range(q))

    def pt_view(t, i, g, w):
        c = (STEPS - 1 - i) % 4
        return t[:, 4 * g:4 * g + w // P, c * P:(c + 1) * P]

    with ExitStack() as ctx:
        def sb(name, shape, dt=F32):
            return ctx.enter_context(nc.sbuf_tensor(name, shape, dt))

        def pb(name, shape):
            return ctx.enter_context(nc.psum_tensor(name, shape, F32))

        def sem(name):
            return ctx.enter_context(nc.semaphore(name))

        q_st = sb("q_st", [P, 2, S], F32R)
        k_hi = sb("k_hi", [P, 2, S], F32R)
        k_lo = sb("k_lo", [P, 2, S], F32R)
        v_hi = sb("v_hi_sb", [P, TB, P], F32R)
        v_lo = sb("v_lo_sb", [P, TB, P], F32R)
        bias = sb("bias", [P, 2, S])
        sc = sb("sc", [P, 2, 2, S])
        p_hi = sb("pt_hi", [P, TB, BANK], F32R)
        p_lo = sb("pt_lo", [P, TB, BANK], F32R)
        o_sb = sb("o_sb", [P, 2, BANK])
        low = sb("low", [P, 2, 2, 2])
        den = sb("den", [P, 2, TB])
        coef = sb("coef", [P, 2])
        dens = sb("dens", [P, TB, HEADS])
        ps_s = pb("ps_s", [P, 2, UNIT])
        ps_t = [pb(f"ps_u{i}", [P, BANK]) for i in range(2)]
        ps_o = pb("ps_o", [P, BANK])

        qk_in = [sem(f"qk_in{c}") for c in range(SUPER)]
        v_in = [sem(f"v_in{c}") for c in range(SUPER)]
        b_in = [sem(f"b_in{c}") for c in range(SUPER)]
        s_ok = sem("s_ok")
        a_ok = sem("a_ok")
        e_ok = sem("e_ok")
        rec_ok = sem("rec_ok")
        coef_ok = sem("coef_ok")
        c_ok = sem("c_ok")
        t_ok = sem("tt_ok")
        hi_ok = sem("thi_ok")
        lo_ok = sem("tlo_ok")
        pv_ok = sem("pv_ok")
        o_ok = sem("o_ok")
        o_out = [sem(f"o_out{i}") for i in range(2)]
        d_ok = sem("d_ok")
        d_out = sem("d_out")

        with nc.Block() as block:
            @block.sync
            def _(sp):
                halves = (slice(0, HD), slice(HD, P))

                def load_chunk(h, c):
                    cols = slice(c * BANK, (c + 1) * BANK)

                    def part(src, i):
                        return src[bass.ds(i, 1)].rearrange("i (m d) s -> d (i m) s", m=2)[:, :, cols]

                    moves = [(q_st[halves[0], :, cols], part(scr.qk_hi, h)), (q_st[halves[1], :, cols], part(scr.qk_lo, h))]
                    for half in halves:
                        moves.append((k_hi[half, :, cols], part(scr.qk_hi, h + HEADS)))
                        moves.append((k_lo[half, :, cols], part(scr.qk_lo, h + HEADS)))
                    for to, src in moves:
                        sp.dma_start(f32(to), src).then_inc(qk_in[c], 16)

                def load_v(h, c):
                    at = slice(4 * c, 4 * c + 4)
                    for to, src in ((v_hi, scr.v_hi), (v_lo, scr.v_lo)):
                        sp.dma_start(f32(to[:, at]), src[bass.ds(h, 1)].rearrange("i p t e -> p (i t) e")[:, at]).then_inc(
                            v_in[c], 16)

                def load_bias(h, x):
                    src = scr.bias_skew[bass.ds(h * 2, 2)][:, 0:P * DIAG].rearrange("m (p y) -> p m y", p=P)
                    sp.dma_start(bias[:, :, x * BANK:(x + 1) * BANK],
                                 src[:, :, P - 1 + x * BANK:P - 1 + (x + 1) * BANK]).then_inc(b_in[x], 16)

                def store_o(h, q):
                    n = h * SUPER + q
                    cols = slice((SUPER - 1 - q) * BANK, (SUPER - q) * BANK)
                    sp.wait_ge(o_ok, n + 2)
                    settle(sp, keep.passed)
                    sp.dma_start(scr.o_t[bass.ds(h, 1)].rearrange("i p s -> p (i s)")[:, cols], o_sb[:, q % 2]).then_inc(
                        o_out[q % 2], 16)

                def next_head(h, last=False):
                    for q in range(SUPER):
                        c = SUPER - 1 - q
                        if not last:
                            sp.wait_ge(s_ok, h * UNITS + units_before(4 * q + 4))
                            settle(sp, keep.passed)
                            load_chunk(h + 1, c)
                            sp.wait_ge(a_ok, h * UNITS + units_before(4 * q + 4) + 2)
                            settle(sp, keep.passed)
                            load_bias(h + 1, q)
                            sp.wait_ge(pv_ok, h * PV_GROUPS + pv_before(q + 1))
                            settle(sp, keep.passed)
                            load_v(h + 1, c)
                        store_o(h, q)

                sp.sem_inc(a_ok, 2)
                sp.sem_inc(lo_ok, 2)
                sp.sem_inc(o_ok, 1)
                for i in range(2):
                    sp.sem_inc(o_out[i], 16)
                for c in reversed(range(SUPER)):
                    load_chunk(0, c)
                    load_bias(0, SUPER - 1 - c)
                for c in range(SUPER):
                    load_v(0, c)
                with sp.Fori(0, HEADS - 1) as h:
                    next_head(h)
                next_head(HEADS - 1, last=True)
                sp.wait_ge(d_ok, HEADS)
                sp.dma_start(scr.l_sum, dens[:]).then_inc(d_out, 16)
                sp.wait_ge(d_out, 16)
                for i in range(2):
                    sp.wait_ge(o_out[i], 16 * (1 + HEADS * SUPER // 2))

            @block.tensor
            def _(pe):
                with pe.Fori(0, HEADS) as h:
                    def scores(i, m, u):
                        n = units_before(i) + m * units(i) + u
                        pe.wait_ge(a_ok, h * UNITS + n + 1)
                        q_cols = slice((STEPS - 1 - i) * P, (STEPS - i) * P)
                        for b in range(2 * u, min(2 * u + 2, groups(i))):
                            w = min(BANK, keys(i) - b * BANK)
                            if i == 0:
                                pe.wait_ge(qk_in[b], (h + 1) * 96)
                                pe.wait_ge(qk_in[SUPER - 1], (h + 1) * 96)
                            out = ps_s[:, n % 2, (b % 2) * BANK:(b % 2) * BANK + w]
                            for k in (k_hi, k_lo):
                                mm = nc.tensor.matmul(out, q_st[:, m, q_cols], k[:, m, b * BANK:b * BANK + w],
                                                      start=(k is k_hi), stop=(k is k_lo))
                        mm.then_inc(s_ok, 1)

                    def transposes(i, g):
                        n = groups_before(i) + g
                        if g == 0:
                            pe.wait_ge(c_ok, h * STEPS + i + 1)
                        pe.wait_ge(lo_ok, h * GROUPS + n + 1)
                        w = min(BANK, keys(i) - g * BANK)
                        for k in range(w // P):
                            at = g * BANK + k * P
                            mm = nc.tensor.transpose(ps_t[n % 2][:, k * P:(k + 1) * P], sc[:, i % 2, 0, at:at + P],
                                                     keep.ident[:])
                        mm.then_inc(t_ok, 1)

                    def pv(q, g):
                        s = SUPER - 1 - q
                        last_step = 4 * q + 3
                        n = groups_before(last_step) + g
                        pe.wait_ge(lo_ok, h * GROUPS + n + 3)
                        pe.wait_ge(v_in[g], (h + 1) * 32)
                        if g == 0:
                            pe.wait_ge(o_ok, h * SUPER + q + 1)
                        for kb in range(4 * g, 4 * g + 4):
                            c0 = max(kb - 4 * s, 0) * P
                            for v, p in ((v_hi, p_lo), (v_lo, p_hi), (v_hi, p_hi)):
                                mm = nc.tensor.matmul(ps_o[:, c0:BANK], v[:, kb], p[:, kb, c0:BANK],
                                                      start=(kb == 0 and p is p_lo), stop=(kb == 4 * s + 3 and v is v_hi and p is p_hi))
                        mm.then_inc(pv_ok, 1)

                    def groups_of(i, rest):
                        q = i // 4 - 1
                        for g in range(groups(i)):
                            if i % 4 == 0 and q >= 0:
                                pv(q, g)
                            transposes(i, g)
                            if rest:
                                scores(*rest.pop(0))
                        if i % 4 == 0 and q >= 0:
                            pv(q, groups(i))

                    for i in range(STEPS):
                        first = [(i, m, u) for m in range(2) for u in range(units(i))]
                        for x in first[:2]:
                            scores(*x)
                        rest = first[2:]
                        if i:
                            groups_of(i - 1, rest)
                        for x in rest:
                            scores(*x)
                    groups_of(STEPS - 1, [])
                    pv(SUPER - 1, 0)

            @block.scalar
            def _(act):
                with act.Fori(0, HEADS) as h:
                    def exponentials(i, m):
                        u = units_before(i) + (m + 1) * units(i)
                        act.wait_ge(a_ok, h * UNITS + u + 2)
                        s = sc[:, i % 2, m, 0:keys(i)]
                        nc.scalar.activation(s, s, ACT.Exp, bias=low[:, i % 2, m, units(i) - 1:units(i)], scale=-1.0,
                                             accum_out=den[:, m, i:i + 1]).then_inc(e_ok, 1)

                    def split_hi(i, g):
                        n = groups_before(i) + g
                        act.wait_ge(t_ok, h * GROUPS + n + 1)
                        w = min(BANK, keys(i) - g * BANK)
                        q = i // 4 - 1
                        if i % 4 == 0 and q >= 0:
                            act.wait_ge(pv_ok, h * PV_GROUPS + pv_before(q) + g + 1)
                        nc.scalar.copy(pt_view(p_hi, i, g, w), ps_t[n % 2][:, 0:w].rearrange("p (k c) -> p k c", c=P)
                                       ).then_inc(hi_ok, 1)

                    def out_super(q):
                        act.wait_ge(pv_ok, h * PV_GROUPS + pv_before(q + 1))
                        act.wait_ge(o_out[q % 2], 16 * (h * (SUPER // 2) + q // 2 + 1))
                        nc.scalar.copy(o_sb[:, q % 2], ps_o[:]).then_inc(o_ok, 1)

                    for i in range(STEPS):
                        gs = list(range(groups(i - 1))) if i else []
                        exponentials(i, 0)
                        for g in gs[:2]:
                            split_hi(i - 1, g)
                        exponentials(i, 1)
                        for g in gs[2:]:
                            split_hi(i - 1, g)
                        if i >= 5 and (i - 1) % 4 == 0:
                            out_super((i - 1) // 4 - 1)
                    split_hi(STEPS - 1, 0)
                    out_super(SUPER - 1)

            @block.vector
            def _(dve):
                with dve.Fori(0, HEADS) as h:
                    def add_bias(i, m, u):
                        n = units_before(i) + m * units(i) + u
                        dve.wait_ge(s_ok, h * UNITS + n + 1)
                        w = min(UNIT, keys(i) - u * UNIT)
                        x0 = S - P - (STEPS - 1 - i) * P + u * UNIT
                        if i == 0 and m == 0:
                            for x in (2 * u, 2 * u + 1):
                                dve.wait_ge(b_in[x], (h + 1) * 16)
                        if u:
                            dve.wait_ge(a_ok, h * UNITS + n + 2)
                        settle(dve, keep.passed)
                        nc.vector.tensor_tensor_reduce(sc[:, i % 2, m, u * UNIT:u * UNIT + w], ps_s[:, n % 2, 0:w],
                                                       bias[:, m, x0:x0 + w], 1.0,
                                                       low[:, i % 2, m, 0:1] if u else FAR, ALU.add, ALU.min,
                                                       low[:, i % 2, m, u:u + 1]).then_inc(a_ok, 1)

                    def combine(i):
                        n = h * STEPS + i
                        dve.wait_ge(e_ok, 2 * n + 2)
                        nc.vector.reciprocal(coef[:, 0:1], den[:, 1, i:i + 1]).then_inc(rec_ok, 1)
                        dve.wait_ge(rec_ok, n + 1)
                        nc.vector.scalar_tensor_tensor(out=coef[:, 1:2], in0=den[:, 0, i:i + 1], scalar=keep.neg_lambda[:],
                                                       in1=coef[:, 0:1], op0=ALU.mult, op1=ALU.mult).then_inc(coef_ok, 1)
                        dve.wait_ge(coef_ok, n + 1)
                        a, b = sc[:, i % 2, 0, 0:keys(i)], sc[:, i % 2, 1, 0:keys(i)]
                        nc.vector.scalar_tensor_tensor(out=a, in0=b, scalar=coef[:, 1:2], in1=a, op0=ALU.mult,
                                                       op1=ALU.add).then_inc(c_ok, 1)

                    def split_lo(i, g):
                        n = groups_before(i) + g
                        dve.wait_ge(hi_ok, h * GROUPS + n + 1)
                        w = min(BANK, keys(i) - g * BANK)
                        nc.vector.tensor_tensor(pt_view(p_lo, i, g, w), ps_t[n % 2][:, 0:w].rearrange("p (k c) -> p k c", c=P),
                                                f32(pt_view(p_hi, i, g, w)), ALU.subtract).then_inc(lo_ok, 1)

                    for i in range(STEPS):
                        before = [(i - 2, g) for g in range(2, groups(i - 2))] if i >= 2 else []
                        for u in range(units(i)):
                            if i >= 2:
                                dve.wait_ge(t_ok, h * GROUPS + groups_before(i - 1))
                            add_bias(i, 0, u)
                            if before:
                                split_lo(*before.pop(0))
                        while before:
                            split_lo(*before.pop(0))
                        if i:
                            combine(i - 1)
                        after = [(i - 1, g) for g in range(min(2, groups(i - 1)))] if i else []
                        for u in range(units(i)):
                            add_bias(i, 1, u)
                            if after:
                                split_lo(*after.pop(0))
                        while after:
                            split_lo(*after.pop(0))
                    combine(STEPS - 1)
                    for g in range(2, groups(STEPS - 2)):
                        split_lo(STEPS - 2, g)
                    split_lo(STEPS - 1, 0)
                    nc.vector.tensor_copy(dens[:, :, bass.ds(h, 1)], den[:, 0, :].rearrange("p (t b) -> p t b", b=1)
                                          ).then_inc(d_ok, 1)


def mix(nc, ins, keep, scr):
    with ExitStack() as ctx:
        def sb(name, shape, dt=F32):
            return ctx.enter_context(nc.sbuf_tensor(name, shape, dt))

        def pb(name, shape):
            return ctx.enter_context(nc.psum_tensor(name, shape, F32))

        def sem(name):
            return ctx.enter_context(nc.semaphore(name))

        wo_raw = sb("wo_raw", [P, 2, D])
        wo_hi = sb("wo_hi", [P, HEADS, D], F32R)
        wo_lo = sb("wo_lo", [P, HEADS, D], F32R)
        gate = sb("gate_m", [P, D])
        diag = sb("diag_m", [P, P])
        ones = sb("ones_m", [P, P])
        ot = sb("ot", [P, 2, HEADS, P])
        xr = sb("xr", [P, 2, D])
        den = sb("den_m", [P, TB, HEADS])
        sq = sb("sq_m", [P, D])
        st = sb("st_m", [P, 2, HEADS])
        on = sb("on", [P, D])
        of = sb("of", [P, D])
        o_hi = sb("o_hi", [P, 2, D], F32R)
        o_lo = sb("o_lo", [P, 2, D], F32R)
        x1 = sb("x1_m", [P, 2, D])
        sq2 = sb("sq2_m", [P, D])
        st2 = sb("st2_m", [P, 2])
        xn = sb("xn_m", [P, D])
        hf = sb("hf", [P, 2, D])
        h_hi = sb("h_hi_m", [P, 2, D], F32R)
        h_lo = sb("h_lo_m", [P, 2, D], F32R)
        ps_a = pb("ps_a", [P, D])
        ps_b = pb("ps_b", [P, D])
        ps_y = pb("ps_y", [P, D])
        ps_d = pb("ps_d", [P, D])

        wo_in = [sem(f"wo_in{i}") for i in range(2)]
        wo_hi_ok = sem("wo_hi_ok")
        wo_lo_ok = sem("wo_lo_ok")
        gate_d = sem("gate_d")
        gate_m = sem("gate_mm")
        gate_ok = sem("gate_ok")
        den_in = sem("den_in")
        den_ok = sem("den_ok")
        o_in = [sem(f"o_in{i}") for i in range(2)]
        x_in = [sem(f"xm_in{i}") for i in range(2)]
        ta_ok = sem("ta_ok")
        sq_ok = sem("sqm_ok")
        ss_ok = sem("ssm_ok")
        var_ok = sem("var_ok")
        sd_ok = sem("sdm_ok")
        ri_ok = sem("rim_ok")
        on_ok = sem("on_ok")
        tb_ok = sem("tb_ok")
        of_ok = sem("of_ok")
        ohi_ok = sem("ohi_ok")
        olo_ok = sem("olo_ok")
        y_ok = sem("y_ok")
        gy_ok = sem("gy_ok")
        x1_ok = sem("x1_ok")
        sq2_ok = sem("sq2_ok")
        sd2_ok = sem("sd2_ok")
        ri2_ok = sem("ri2_ok")
        xn_ok = sem("xn_ok")
        td_ok = sem("td_ok")
        hf_ok = sem("hf_ok")
        hhi_ok = sem("hhi_ok")
        hlo_ok = sem("hlo_ok")
        x1_out = [sem(f"x1_out{i}") for i in range(2)]
        h_out = [sem(f"h_out{i}") for i in range(2)]

        x_v = ins["x"][0].rearrange("(t p) d -> t p d", p=P)
        x1_v = scr.x1.rearrange("(t p) d -> t p d", p=P)
        wo_v = ins["da_w_o"][0].rearrange("(h p) n -> h p n", p=P)
        ot_v = scr.o_t.rearrange("h p s -> p h s")
        blocks = lambda a: a.rearrange("p (b n) -> p b n", n=P)
        wide = lambda a: a.rearrange("p (b n) -> p b n", n=1).to_broadcast([P, HEADS, P])

        with nc.Block() as block:
            @block.sync
            def _(sp):
                def loads(t):
                    if t >= 2:
                        sp.wait_ge(ta_ok, t - 1)
                        sp.wait_ge(x1_ok, t - 1)
                    sp.dma_start(ot[:, t % 2], ot_v[:, :, t * P:(t + 1) * P]).then_inc(o_in[t % 2], 16)
                    sp.dma_start(xr[:, t % 2], x_v[t]).then_inc(x_in[t % 2], 16)

                sp.dma_start(den[:], scr.l_sum).then_inc(den_in, 16)
                loads(0)
                loads(1)
                for hh in range(HEADS):
                    if hh >= 2:
                        sp.wait_ge(wo_lo_ok, hh - 1)
                    sp.dma_start(wo_raw[:, hh % 2], wo_v[hh]).then_inc(wo_in[hh % 2], 16)
                for t in range(TB):
                    if t + 2 < TB:
                        loads(t + 2)
                    sp.wait_ge(x1_ok, t + 1)
                    sp.dma_start(x1_v[t], x1[:, t % 2]).then_inc(x1_out[t % 2], 16)
                    sp.wait_ge(hhi_ok, t + 1)
                    sp.dma_start(scr.h2_hi[:, :, t * P:(t + 1) * P], f32(blocks(h_hi[:, t % 2]))).then_inc(h_out[t % 2], 16)
                    sp.wait_ge(hlo_ok, t + 1)
                    sp.dma_start(scr.h2_lo[:, :, t * P:(t + 1) * P], f32(blocks(h_lo[:, t % 2]))).then_inc(h_out[t % 2], 16)
                for i in range(2):
                    sp.wait_ge(x1_out[i], 16 * TB // 2)
                    sp.wait_ge(h_out[i], 32 * TB // 2)

            @block.gpsimd
            def _(pool):
                for t in range(TB):
                    pool.wait_ge(of_ok, t + 1)
                    if t >= 2:
                        pool.wait_ge(y_ok, 2 * (t - 1))
                    nc.gpsimd.tensor_copy(o_hi[:, t % 2], of[:]).then_inc(ohi_ok, 1)
                    pool.wait_ge(ohi_ok, t + 1)
                    nc.gpsimd.tensor_tensor(o_lo[:, t % 2], of[:], f32(o_hi[:, t % 2]), ALU.subtract).then_inc(olo_ok, 1)

            @block.scalar
            def _(act):
                def norm_stats(t):
                    act.wait_ge(ta_ok, t + 1)
                    if t:
                        act.wait_ge(ss_ok, t)
                    nc.scalar.activation(sq[:], ps_a[:], ACT.Square).then_inc(sq_ok, 1)
                    act.wait_ge(var_ok, t + 1)
                    nc.scalar.activation(st[:, 1], st[:, 0], ACT.Sqrt).then_inc(sd_ok, 1)

                def head_gain(t):
                    act.wait_ge(tb_ok, t + 1)
                    if t:
                        act.wait_ge(olo_ok, t)
                    nc.scalar.activation(of[:], ps_b[:], ACT.Copy, scale=keep.sub_gain[:]).then_inc(of_ok, 1)

                def second_norm(t):
                    act.wait_ge(x1_ok, t + 1)
                    nc.scalar.activation(sq2[:], x1[:, t % 2], ACT.Square, accum_out=st2[:, 0:1]).then_inc(sq2_ok, 1)
                    act.wait_ge(sq2_ok, t + 1)
                    nc.scalar.activation(st2[:, 1:2], st2[:, 0:1], ACT.Sqrt, bias=keep.eps[:],
                                         scale=1.0 / D).then_inc(sd2_ok, 1)

                def second_affine(t):
                    act.wait_ge(td_ok, t + 1)
                    if t >= 2:
                        act.wait_ge(hlo_ok, t - 1)
                    for d in range(DB):
                        at = slice(d * P, (d + 1) * P)
                        a = nc.scalar.activation(hf[:, t % 2, at], ps_d[:, at], ACT.Identity,
                                                 bias=keep.mod[:, 3 * DB + d:3 * DB + d + 1],
                                                 scale=keep.affine[:, 1, d:d + 1])
                    a.then_inc(hf_ok, 1)
                    act.wait_ge(hf_ok, t + 1)
                    if t >= 2:
                        act.wait_ge(h_out[t % 2], 32 * (t // 2))
                    nc.scalar.copy(h_hi[:, t % 2], hf[:, t % 2]).then_inc(hhi_ok, 1)

                for hh in range(HEADS):
                    act.wait_ge(wo_in[hh % 2], 16 * (hh // 2 + 1))
                    nc.scalar.copy(wo_hi[:, hh], wo_raw[:, hh % 2]).then_inc(wo_hi_ok, 1)
                norm_stats(0)
                for t in range(TB):
                    head_gain(t)
                    if t + 1 < TB:
                        norm_stats(t + 1)
                    if t:
                        second_affine(t - 1)
                    second_norm(t)
                second_affine(TB - 1)

            @block.vector
            def _(dve):
                def gate_row(first, j):
                    if j:
                        dve.wait_ge(gate_m, j)
                    nc.vector.tensor_scalar(diag[:], keep.ident[:], keep.mod[:, first + j:first + j + 1], None,
                                            ALU.mult).then_inc(gate_d, 1)

                def head_rows(t):
                    dve.wait_ge(sq_ok, t + 1)
                    if t:
                        dve.wait_ge(sd_ok, t)
                    nc.vector.tensor_reduce(st[:, 0], blocks(sq[:]), AX_X, ALU.add).then_inc(ss_ok, 1)
                    dve.wait_ge(ss_ok, t + 1)
                    nc.vector.scalar_tensor_tensor(out=st[:, 0], in0=st[:, 0], scalar=1.0 / P, in1=den[:, TB - 1 - t],
                                                   op0=ALU.mult, op1=ALU.add).then_inc(var_ok, 1)
                    dve.wait_ge(sd_ok, t + 1)
                    nc.vector.reciprocal(st[:, 1], st[:, 1]).then_inc(ri_ok, 1)
                    dve.wait_ge(ri_ok, t + 1)
                    if t:
                        dve.wait_ge(tb_ok, t)
                    nc.vector.tensor_tensor(blocks(on[:]), blocks(ps_a[:]), wide(st[:, 1]), ALU.mult).then_inc(on_ok, 1)

                def residual(t):
                    for n in range(2):
                        at = slice(n * BANK, (n + 1) * BANK)
                        dve.wait_ge(y_ok, 2 * t + n + 1)
                        if t >= 2 and n == 0:
                            dve.wait_ge(x1_out[t % 2], 16 * (t // 2))
                            dve.wait_ge(sq2_ok, t - 1)
                        nc.vector.tensor_tensor(x1[:, t % 2, at], ps_y[:, at], gate[:, at], ALU.mult).then_inc(gy_ok, 1)
                    dve.wait_ge(gy_ok, 2 * t + 2)
                    dve.wait_ge(x_in[t % 2], 16 * (t // 2 + 1))
                    nc.vector.tensor_tensor(x1[:, t % 2], x1[:, t % 2], xr[:, t % 2], ALU.add).then_inc(x1_ok, 1)

                def second_rows(t):
                    dve.wait_ge(sd2_ok, t + 1)
                    nc.vector.reciprocal(st2[:, 1:2], st2[:, 1:2]).then_inc(ri2_ok, 1)
                    dve.wait_ge(ri2_ok, t + 1)
                    if t:
                        dve.wait_ge(td_ok, t)
                    nc.vector.tensor_scalar(xn[:], x1[:, t % 2], st2[:, 1:2], None, ALU.mult).then_inc(xn_ok, 1)

                def second_lo(t):
                    dve.wait_ge(hhi_ok, t + 1)
                    nc.vector.tensor_tensor(h_lo[:, t % 2], hf[:, t % 2], f32(h_hi[:, t % 2]), ALU.subtract).then_inc(hlo_ok, 1)

                nc.vector.memset(ones[:], 1.0)
                for j in range(DB):
                    gate_row(2 * DB, j)
                dve.wait_ge(gate_m, DB)
                nc.vector.tensor_copy(gate[:], ps_y[:]).then_inc(gate_ok, 1)
                dve.wait_ge(den_in, 16)
                nc.vector.scalar_tensor_tensor(out=den[:], in0=den[:], scalar=EPS, in1=den[:], op0=ALU.mult,
                                               op1=ALU.mult).then_inc(den_ok, 1)
                dve.wait_ge(den_ok, 1)
                for hh in range(HEADS):
                    dve.wait_ge(wo_hi_ok, hh + 1)
                    nc.vector.tensor_tensor(wo_lo[:, hh], wo_raw[:, hh % 2], f32(wo_hi[:, hh]), ALU.subtract).then_inc(wo_lo_ok, 1)
                head_rows(0)
                for t in range(TB):
                    if t + 1 < TB:
                        head_rows(t + 1)
                    if t:
                        second_lo(t - 1)
                    residual(t)
                    second_rows(t)
                second_lo(TB - 1)

            @block.tensor
            def _(pe):
                def transposes_a(t):
                    pe.wait_ge(o_in[t % 2], 16 * (t // 2 + 1))
                    if t:
                        pe.wait_ge(on_ok, t)
                    for hh in range(HEADS):
                        mm = nc.tensor.transpose(ps_a[:, hh * P:(hh + 1) * P], ot[:, t % 2, hh], keep.ident[:])
                    mm.then_inc(ta_ok, 1)

                def transposes_b(t):
                    pe.wait_ge(on_ok, t + 1)
                    if t:
                        pe.wait_ge(of_ok, t)
                    for hh in range(HEADS):
                        mm = nc.tensor.transpose(ps_b[:, hh * P:(hh + 1) * P], on[:, hh * P:(hh + 1) * P], keep.ident[:])
                    mm.then_inc(tb_ok, 1)

                def product(t, n):
                    pe.wait_ge(olo_ok, t + 1)
                    if t:
                        pe.wait_ge(gy_ok, 2 * t - 1 + n)
                    else:
                        pe.wait_ge(gate_ok, 1)
                    at = slice(n * BANK, (n + 1) * BANK)
                    for hh in range(HEADS):
                        if t == 0:
                            pe.wait_ge(wo_lo_ok, hh + 1)
                        hs = slice(hh * P, (hh + 1) * P)
                        nc.tensor.matmul(ps_y[:, at], o_hi[:, t % 2, hs], wo_hi[:, hh, at], start=(hh == 0), stop=False)
                        nc.tensor.matmul(ps_y[:, at], o_hi[:, t % 2, hs], wo_lo[:, hh, at], start=False, stop=False)
                        mm = nc.tensor.matmul(ps_y[:, at], o_lo[:, t % 2, hs], wo_hi[:, hh, at], start=False,
                                              stop=(hh == HEADS - 1))
                    mm.then_inc(y_ok, 1)

                def transposes_d(t):
                    pe.wait_ge(xn_ok, t + 1)
                    if t:
                        pe.wait_ge(hf_ok, t)
                    for d in range(DB):
                        mm = nc.tensor.transpose(ps_d[:, d * P:(d + 1) * P], xn[:, d * P:(d + 1) * P], keep.ident[:])
                    mm.then_inc(td_ok, 1)

                for j in range(DB):
                    pe.wait_ge(gate_d, j + 1)
                    nc.tensor.matmul(ps_y[:, j * P:(j + 1) * P], ones[:], diag[:], start=True, stop=True).then_inc(gate_m, 1)
                transposes_a(0)
                transposes_b(0)
                for t in range(TB):
                    if t + 1 < TB:
                        transposes_a(t + 1)
                    product(t, 0)
                    if t + 1 < TB:
                        transposes_b(t + 1)
                    if t:
                        transposes_d(t - 1)
                    product(t, 1)
                transposes_d(TB - 1)


def mlp(nc, ins, keep, scr, out):
    HALVES = 2
    HT = S // HALVES
    FC = 256
    CHUNKS = F // FC
    FB = FC // P
    TG = HT // BANK
    HB = HT // P
    UB = BANK // P
    NB = D // BANK
    with ExitStack() as ctx:
        def sb(name, shape, dt=F32):
            return ctx.enter_context(nc.sbuf_tensor(name, shape, dt))

        def pb(name, shape):
            return ctx.enter_context(nc.psum_tensor(name, shape, F32))

        def sem(name):
            return ctx.enter_context(nc.semaphore(name))

        h_hi = sb("h_hi_f", [P, DB, HT], F32R)
        h_lo = sb("h_lo_f", [P, DB, HT], F32R)
        acc = sb("acc", [P, HB, D])
        w_raw = sb("wf_raw", [P, 2, DB * FC])
        w1_hi = sb("w1_hi", [P, 2, DB, FC], F32R)
        w1_lo = sb("w1_lo", [P, 2, DB, FC], F32R)
        w2_hi = sb("w2_hi", [P, 2, FB, D], F32R)
        w2_lo = sb("w2_lo", [P, 2, FB, D], F32R)
        r = sb("r", [P, 2, BANK])
        g_hi = sb("g_hi", [P, TG, FB, BANK], F32R)
        g_lo = sb("g_lo", [P, TG, FB, BANK], F32R)
        gate = sb("gate_f", [P, D])
        diag = sb("diag_f", [P, P])
        ones = sb("ones_f", [P, P])
        ps_h = [pb(f"ps_h{i}", [P, BANK]) for i in range(4)]
        ps_y = [pb(f"ps_y{i}", [P, BANK]) for i in range(4)]

        h_in = [sem(f"h_in{g}") for g in range(TG)]
        acc_in = [sem(f"acc_in{t}") for t in range(HB)]
        acc_out = [sem(f"acc_out{t}") for t in range(HB)]
        w_in = [sem(f"wf_in{i}") for i in range(2)]
        w_hi_ok = [sem(f"wfhi_ok{i}") for i in range(2)]
        w_lo_ok = [sem(f"wflo_ok{i}") for i in range(2)]
        w2g_ok = sem("w2g_ok")
        gate_d = sem("gatef_d")
        gate_m = sem("gatef_m")
        gate_ok = sem("gatef_ok")
        mh_ok = sem("mh_ok")
        r_ok = sem("r_ok")
        g_ok = sem("g_ok")
        ghi_ok = sem("ghi_ok")
        glo_ok = sem("glo_ok")
        y_ok = sem("yf_ok")
        add_ok = sem("add_ok")

        YB = UB * NB
        w1_v = ins["mlp_w1"][0].rearrange("(b p) f -> p b f", p=P)
        w2_v = ins["mlp_w2"][0].rearrange("(b p) n -> p b n", p=P)
        x1_v = scr.x1.rearrange("(t p) d -> t p d", p=P)
        out_v = out[0].rearrange("(t p) d -> t p d", p=P)
        raw = [w_raw[:, 0].rearrange("p (b f) -> p b f", b=DB), w_raw[:, 1].rearrange("p (b n) -> p b n", b=FB)]
        hi = [w1_hi, w2_hi]
        lo = [w1_lo, w2_lo]

        def rounds(eng, head, body):
            with eng.Fori(0, HALVES) as half:
                i0 = half * CHUNKS
                head(half, i0)
                with eng.Fori(0, CHUNKS // 2 - 1) as pair:
                    for e in range(2):
                        body(half, i0 + pair * 2 + e, e, False)
                body(half, i0 + (CHUNKS - 2), 0, False)
                body(half, i0 + (CHUNKS - 1), 1, True)

        with nc.Block() as block:
            @block.sync
            def _(sp):
                def load_w(i, f):
                    sp.wait_ge(w_lo_ok[0], i + 1)
                    settle(sp, keep.passed)
                    sp.dma_start(raw[0], w1_v[:, :, bass.ds(f * FC, FC)]).then_inc(w_in[0], 16)
                    sp.wait_ge(w_lo_ok[1], i + 1)
                    settle(sp, keep.passed)
                    sp.dma_start(raw[1], w2_v[:, bass.ds(f * FB, FB)]).then_inc(w_in[1], 16)

                def load_h(half, g):
                    if half:
                        sp.wait_ge(mh_ok, (half * CHUNKS - 1) * TG * FB + (g + 1) * FB)
                    at = half * HT + g * BANK
                    for to, src in ((h_hi, scr.h2_hi), (h_lo, scr.h2_lo)):
                        sp.dma_start(f32(to[:, :, g * BANK:(g + 1) * BANK]), src[:, :, at:at + BANK]).then_inc(h_in[g], 16)

                sp.sem_inc(w_lo_ok[0], 1)
                sp.sem_inc(w_lo_ok[1], 1)
                sp.sem_inc(g_ok, 4)
                sp.sem_inc(glo_ok, 2)
                sp.sem_inc(add_ok, 4)
                sp.sem_inc(y_ok, 2 * YB)
                for half in range(HALVES):
                    load_h(half, 0)
                    load_w(half * CHUNKS, 0)
                    load_h(half, 1)
                    for t in range(HB):
                        if half:
                            sp.wait_ge(acc_out[t], 16)
                        sp.dma_start(acc[:, t], x1_v[half * HB + t]).then_inc(acc_in[t], 16)
                    with sp.Fori(1, CHUNKS) as f:
                        load_w(half * CHUNKS + f, f)
                    for t in range(HB):
                        unit = ((half + 1) * CHUNKS - 1) * TG + t // UB
                        sp.wait_ge(add_ok, unit * YB + (t % UB + 1) * NB + 4)
                        sp.dma_start(out_v[half * HB + t], acc[:, t]).then_inc(acc_out[t], 16)
                for t in range(HB):
                    sp.wait_ge(acc_out[t], 16 * HALVES)

            @block.gpsimd
            def _(pool):
                def w2_gate(i):
                    pool.wait_ge(w_in[1], i * 16 + 16)
                    for b in range(FB):
                        g = nc.gpsimd.tensor_tensor(raw[1][:, b], raw[1][:, b], gate[:], ALU.mult)
                    g.then_inc(w2g_ok, 1)

                def unit_lo(i, g):
                    for fb in range(FB):
                        b = (i * TG + g) * FB + fb
                        pool.wait_ge(ghi_ok, b + 1)
                        nc.gpsimd.tensor_tensor(g_lo[:, g, fb], r[:, fb], f32(g_hi[:, g, fb]), ALU.subtract).then_inc(glo_ok, 1)

                def head(half, i):
                    w2_gate(i)
                    unit_lo(i, 0)

                def body(half, i, parity, last):
                    if not last:
                        w2_gate(i + 1)
                    unit_lo(i, 1)
                    if not last:
                        unit_lo(i + 1, 0)

                pool.wait_ge(gate_ok, NB)
                rounds(pool, head, body)

            @block.scalar
            def _(act):
                def split(i, parity, more=0):
                    act.wait_ge(y_ok, i * (TG * YB) + more)
                    for m in range(2):
                        if m == 0:
                            act.wait_ge(w_in[0], i * 16 + 16)
                        else:
                            act.wait_ge(w2g_ok, i + 1)
                        nc.scalar.copy(hi[m][:, parity], raw[m]).then_inc(w_hi_ok[m], 1)

                def unit(i, g):
                    for fb in range(FB):
                        b = (i * TG + g) * FB + fb
                        act.wait_ge(mh_ok, b + 1)
                        act.wait_ge(glo_ok, b + 1)
                        nc.scalar.activation(r[:, fb], ps_h[g * FB + fb][:], ACT.Relu).then_inc(r_ok, 1)
                        act.wait_ge(g_ok, b + 5)
                        act.wait_ge(y_ok, (i * TG + g + 1) * YB)
                        nc.scalar.copy(g_hi[:, g, fb], r[:, fb]).then_inc(ghi_ok, 1)

                def head(half, i):
                    split(i, 0, more=1)
                    unit(i, 0)

                def body(half, i, parity, last):
                    if not last:
                        split(i + 1, 1 - parity)
                    unit(i, 1)
                    if not last:
                        unit(i + 1, 0)

                rounds(act, head, body)

            @block.vector
            def _(dve):
                def split(i, parity):
                    for m in range(2):
                        dve.wait_ge(w_hi_ok[m], i + 1)
                        nc.vector.tensor_tensor(lo[m][:, parity], raw[m], f32(hi[m][:, parity]), ALU.subtract).then_inc(
                            w_lo_ok[m], 1)

                def squares(i, g):
                    for fb in range(FB):
                        b = (i * TG + g) * FB + fb
                        dve.wait_ge(r_ok, b + 1)
                        nc.vector.scalar_tensor_tensor(out=r[:, fb], in0=ps_h[g * FB + fb][:], scalar=0.0, in1=r[:, fb],
                                                       op0=ALU.max, op1=ALU.mult).then_inc(g_ok, 1)

                def adds(half, i, g):
                    for k in range(YB):
                        n = (i * TG + g) * YB + k
                        t = g * UB + k // NB
                        at = slice((k % NB) * BANK, (k % NB + 1) * BANK)
                        if k % NB == 0:
                            dve.wait_ge(acc_in[t], half * 16 + 16)
                        dve.wait_ge(y_ok, n + 2 * YB + 1)
                        nc.vector.tensor_tensor(acc[:, t, at], ps_y[k % 4][:], acc[:, t, at], ALU.add).then_inc(add_ok, 1)

                def head(half, i):
                    split(i, 0)
                    squares(i, 0)

                def body(half, i, parity, last):
                    if not last:
                        split(i + 1, 1 - parity)
                    squares(i, 1)
                    adds(half, i, 0)
                    if not last:
                        squares(i + 1, 0)
                    adds(half, i, 1)

                nc.vector.memset(ones[:], 1.0)
                for j in range(DB):
                    if j:
                        dve.wait_ge(gate_m, j)
                    nc.vector.tensor_scalar(diag[:], keep.ident[:], keep.mod[:, 5 * DB + j:5 * DB + j + 1], None,
                                            ALU.mult).then_inc(gate_d, 1)
                dve.wait_ge(gate_m, DB)
                for n in range(NB):
                    nc.vector.tensor_copy(gate[:, n * BANK:(n + 1) * BANK], ps_y[n][:]).then_inc(gate_ok, 1)
                rounds(dve, head, body)

            @block.tensor
            def _(pe):
                def hidden(half, i, g, parity):
                    if g == 0:
                        pe.wait_ge(w_lo_ok[0], i + 2)
                    pe.wait_ge(h_in[g], half * 32 + 32)
                    at = slice(g * BANK, (g + 1) * BANK)
                    for fb in range(FB):
                        b = (i * TG + g) * FB + fb
                        pe.wait_ge(g_ok, b + 1)
                        ps = ps_h[g * FB + fb][:]
                        fs = slice(fb * P, (fb + 1) * P)
                        for d in range(DB):
                            nc.tensor.matmul(ps, w1_hi[:, parity, d, fs], h_hi[:, d, at], start=(d == 0), stop=False)
                            nc.tensor.matmul(ps, w1_hi[:, parity, d, fs], h_lo[:, d, at], start=False, stop=False)
                            mm = nc.tensor.matmul(ps, w1_lo[:, parity, d, fs], h_hi[:, d, at], start=False, stop=(d == DB - 1))
                        mm.then_inc(mh_ok, 1)

                def products(i, g, parity):
                    if g == 0:
                        pe.wait_ge(w_lo_ok[1], i + 2)
                    pe.wait_ge(glo_ok, (i * TG + g) * FB + FB + 2)
                    for k in range(YB):
                        n = (i * TG + g) * YB + k
                        pe.wait_ge(add_ok, n + 1)
                        ts = slice((k // NB) * P, (k // NB + 1) * P)
                        at = slice((k % NB) * BANK, (k % NB + 1) * BANK)
                        for fb in range(FB):
                            nc.tensor.matmul(ps_y[k % 4][:], g_hi[:, g, fb, ts], w2_hi[:, parity, fb, at], start=(fb == 0), stop=False)
                            nc.tensor.matmul(ps_y[k % 4][:], g_hi[:, g, fb, ts], w2_lo[:, parity, fb, at], start=False, stop=False)
                            mm = nc.tensor.matmul(ps_y[k % 4][:], g_lo[:, g, fb, ts], w2_hi[:, parity, fb, at], start=False,
                                                  stop=(fb == FB - 1))
                        mm.then_inc(y_ok, 1)

                def head(half, i):
                    hidden(half, i, 0, 0)

                def body(half, i, parity, last):
                    hidden(half, i, 1, parity)
                    products(i, 0, parity)
                    if not last:
                        hidden(half, i + 1, 0, 1 - parity)
                    products(i, 1, parity)

                for j in range(DB):
                    pe.wait_ge(gate_d, j + 1)
                    nc.tensor.matmul(ps_y[j // 4][:, (j % 4) * P:(j % 4 + 1) * P], ones[:], diag[:], start=True,
                                     stop=True).then_inc(gate_m, 1)
                pe.wait_ge(gate_ok, NB)
                rounds(pe, head, body)


def decoder_layer(nc, ins, out):
    scr = Scratch(nc)
    with ExitStack() as ctx:
        keep = Persist(nc, ctx)
        with ExitStack() as both:
            ht_hi = both.enter_context(nc.sbuf_tensor("ht_hi", [P, DB, S], F32R))
            ht_lo = both.enter_context(nc.sbuf_tensor("ht_lo", [P, DB, S], F32R))
            modulate(nc, ins, keep, scr, ht_hi, ht_lo)
            project(nc, ins, keep, scr, ht_hi, ht_lo)
        attend(nc, keep, scr)
        mix(nc, ins, keep, scr)
        mlp(nc, ins, keep, scr, out)


_INS = ["x", "c", "rel_bias", "w_ada", "b_ada", "norm_mix", "norm_mlp", "mlp_w1", "mlp_w2", "da_w_qkv", "da_w_o",
        "da_q_gain", "da_k_gain", "da_lam_q1", "da_lam_k1", "da_lam_q2", "da_lam_k2", "da_sub_gain"]


def kernel(**inputs):
    import concourse.bacc as bacc
    from concourse.bass_utils import run_bass_kernel_spmd

    nc = bacc.Bacc("TRN2", target_bir_lowering=False, num_devices=1)
    arrays, ins = {}, {}
    for name in _INS:
        a = np.ascontiguousarray(inputs[name])
        arrays[f"in_{name}"] = a
        ins[name] = nc.dram_tensor(f"in_{name}", a.shape, mybir.dt.from_np(a.dtype), kind="ExternalInput").ap()
    table = bucket_table()
    arrays["in_buckets"] = table
    ins["buckets"] = nc.dram_tensor("in_buckets", table.shape, F32, kind="ExternalInput").ap()
    out = nc.dram_tensor("out", (1, S, D), F32, kind="ExternalOutput").ap()
    decoder_layer(nc, ins, out)
    r = run_bass_kernel_spmd(nc, [arrays], core_ids=[0])
    return r.results[0]["out"]
```

```python
import math
from contextlib import ExitStack

import concourse.bass as bass
import numpy as np
from concourse import mybir

F32 = mybir.dt.float32
F32R = mybir.dt.float32r
ALU = mybir.AluOpType
ACT = mybir.ActivationFunctionType
AX_X = mybir.AxisListType.X

P = 128
D = 1024
S = 2048
F = 4 * D
DB = D // P
TB = S // P
HD = 64
HEADS = D // (2 * HD)
BANK = 512
SUPER = S // BANK
EPS = 1e-6
LAMBDA_INIT = 0.8 - 0.6 * math.exp(-0.3 * 0)
BUCKETS = 32
REL_MAX = 2048
MASK = 1e30
DIAG = S + P
FAR = 3.0e38


def bucket_table():
    dist = S - 1 - np.arange(DIAG)
    n = np.maximum(dist, 0)
    exact = BUCKETS // 2
    nf = np.maximum(n, exact).astype(np.float32)
    steps = np.log(nf / np.float32(exact)) / np.float32(math.log(REL_MAX / exact)) * np.float32(BUCKETS - exact)
    large = np.minimum(exact + steps.astype(np.int32), BUCKETS - 1)
    bucket = np.where(n < exact, n, large)
    bucket = np.where(dist < 0, BUCKETS, bucket)
    return (np.arange(BUCKETS + 1)[:, None] == bucket[None, :]).astype(np.float32)


class Scratch:

    def __init__(self, nc):
        def dram(name, shape):
            return nc.dram_tensor(name, shape, F32, kind="Internal").ap()

        self.bias_row = dram("bias_row", (2 * HEADS, DIAG))
        self.qk_hi = dram("qk_hi", (2 * HEADS, P, S))
        self.qk_lo = dram("qk_lo", (2 * HEADS, P, S))
        self.v_hi = dram("v_hi", (HEADS, P, TB, P))
        self.v_lo = dram("v_lo", (HEADS, P, TB, P))
        self.o_t = dram("o_t", (HEADS, P, S))
        self.l_sum = dram("l_sum", (P, TB, HEADS))
        self.x1 = dram("x1", (S, D))
        self.h2_hi = dram("h2_hi", (P, DB, S))
        self.h2_lo = dram("h2_lo", (P, DB, S))


def f32(ap):
    return ap.bitcast(F32)


def settle(eng, passed):
    eng.sem_inc(passed, 1)


class Persist:

    def __init__(self, nc, ctx):
        def sb(name, shape, dt=F32):
            return ctx.enter_context(nc.sbuf_tensor(name, shape, dt))

        self.ident = sb("ident", [P, P])
        self.mirror = sb("mirror", [P, P])
        self.mod = sb("mod", [P, 6 * DB])
        self.affine = sb("affine", [P, 2, DB])
        self.c_silu = sb("c_silu", [P, DB])
        self.one = sb("one", [P, 1])
        self.b_ada = sb("b_ada", [P, 6 * DB])
        self.norm_gain = sb("norm_gain", [P, 2, DB])
        self.neg_lambda = sb("neg_lambda", [P, 1])
        self.qk_gain = sb("qk_gain", [P, 4])
        self.sub_gain = sb("sub_gain", [P, 1])
        self.eps = sb("eps", [P, 1])
        self.passed = ctx.enter_context(nc.semaphore("passed"))


class Handover:

    def __init__(self, nc, ctx):
        self.ht_hi = ctx.enter_context(nc.sbuf_tensor("ht_hi", [P, DB, S], F32R))
        self.ht_lo = ctx.enter_context(nc.sbuf_tensor("ht_lo", [P, DB, S], F32R))
        self.w_raw = ctx.enter_context(nc.sbuf_tensor("w_raw", [P, DB, BANK], F32))
        self.w_in = [ctx.enter_context(nc.semaphore(f"w_in{b}")) for b in range(DB)]


def weighted_rows(nc, dve, keep, acc, w, acc_ok, n):
    for b in range(DB):
        c = keep.c_silu[:, b:b + 1]
        if b == 0:
            a = nc.vector.tensor_scalar(acc, w[:, b], c, None, ALU.mult)
        else:
            dve.wait_ge(acc_ok, n * DB + b)
            a = nc.vector.scalar_tensor_tensor(out=acc, in0=w[:, b], scalar=c, in1=acc, op0=ALU.mult, op1=ALU.add)
        a.then_inc(acc_ok, 1)


def load_qkv_weights(sp, ins, over, cols):
    w_v = ins["da_w_qkv"][0].rearrange("(b p) n -> p b n", p=P)
    for b in range(DB):
        sp.dma_start(over.w_raw[:, b], w_v[:, b, cols]).then_inc(over.w_in[b], 16)


def modulate(nc, ins, keep, scr, over):
    ADA_N = 256
    CHUNKS = 2 * D // ADA_N
    CJ = ADA_N // P
    ht_hi, ht_lo = over.ht_hi, over.ht_lo
    with ExitStack() as ctx:
        def sb(name, shape, dt=F32):
            return ctx.enter_context(nc.sbuf_tensor(name, shape, dt))

        def pb(name, shape):
            return ctx.enter_context(nc.psum_tensor(name, shape, F32))

        def sem(name):
            return ctx.enter_context(nc.semaphore(name))

        ada = sb("ada", [P, 2, DB, ADA_N])
        acc = sb("acc_a", [P, 2, ADA_N])
        xg = sb("xg", [P, 4, D])
        sq = sb("sq_a", [P, D])
        tmp = sb("tmp_a", [P, 2, BANK])
        ccol = sb("ccol", [P, 2, DB])
        lam = sb("lam", [P, 4, HD])
        lam_s = sb("lam_s", [P, 4])
        stat = sb("stat_a", [P, 2, TB])
        rel = sb("rel", [BUCKETS + 1, 2 * HEADS])
        hot = sb("hot", [BUCKETS + 1, DIAG])
        row = sb("row", [2 * HEADS, DIAG])
        ps_mod = pb("ps_mod", [P, 2 * DB])
        ps_row = pb("ps_row", [2 * HEADS, BANK])
        ps_t = [pb(f"ps_t{i}", [P, BANK]) for i in range(4)]

        small_in = sem("small_in")
        ada_in = [sem(f"ada_in{i}") for i in range(2)]
        x_in = [sem(f"x_in{i}") for i in range(2)]
        ident_ok = sem("ident_ok")
        pool_ok = sem("pool_ok")
        silu_a = sem("silu_a")
        silu_d = sem("silu_d")
        acc_ok = sem("acc_a_ok")
        mod_part = sem("mod_part")
        mod_ok_d = sem("mod_ok_d")
        mod_ok = sem("mod_ok")
        lam_d = sem("lam_d")
        lam_a = sem("lam_a")
        rel_ok = sem("rel_ok")
        row_mm = sem("row_mm")
        row_ok = sem("row_ok")
        row_out = sem("row_out")
        x_sq = sem("x_sq")
        x_sd = sem("x_sd")
        x_ri = sem("x_ri")
        x_n = sem("x_n")
        x_t = sem("x_t")
        h_f = sem("h_f")
        h_hi = sem("h_hi")
        h_lo = sem("h_lo")
        SMALL = 17

        ada_v = ins["w_ada"][0].rearrange("(b p) n -> p b n", p=P)
        x_v = ins["x"][0].rearrange("(t p) d -> p t d", p=P)
        x_of = [xg[:], ada[:].rearrange("p i (k b) n -> p (i k) (b n)", k=2)]

        with nc.Block() as block:
            @block.sync
            def _(sp):
                with nc.allow_non_contiguous_dma(reason="columns of small vectors"):
                    col = lambda a: a.rearrange("(b p) -> p b", p=P)
                    loads = [(ccol[:, 0, :], col(ins["c"][0])), (keep.b_ada[:], col(ins["b_ada"][0])),
                             (keep.norm_gain[:, 0, :], col(ins["norm_mix"][0])), (keep.norm_gain[:, 1, :], col(ins["norm_mlp"][0])),
                             (keep.sub_gain[:], col(ins["da_sub_gain"][0]))]
                    for half in range(2):
                        at = slice(half * HD, half * HD + HD)
                        for g, name in ((0, "da_q_gain"), (1, "da_q_gain"), (2, "da_k_gain"), (3, "da_k_gain")):
                            loads.append((keep.qk_gain[at, g:g + 1], ins[name][0].rearrange("(p b) -> p b", b=1)))
                    for n, name in enumerate(("da_lam_q1", "da_lam_k1", "da_lam_q2", "da_lam_k2")):
                        loads.append((lam[:, n, :], ins[name].to_broadcast([P, HD])))
                    assert len(loads) == SMALL
                    for to, src in loads:
                        sp.dma_start(to, src).then_inc(small_in, 16)
                sp.dma_start(rel[0:BUCKETS, :], ins["rel_bias"]).then_inc(small_in, 16)
                sp.dma_start(hot[:], ins["buckets"]).then_inc(small_in, 16)
                for n in range(CHUNKS):
                    if n >= 2:
                        sp.wait_ge(acc_ok, (n - 1) * DB)
                    sp.dma_start(ada[:, n % 2], ada_v[:, :, n * ADA_N:(n + 1) * ADA_N]).then_inc(ada_in[n % 2], 16)
                load_qkv_weights(sp, ins, over, slice(0, BANK))
                sp.wait_ge(row_ok, -(-DIAG // BANK))
                sp.dma_start(scr.bias_row, row[:]).then_inc(row_out, 16)
                sp.wait_ge(row_out, 16)

            @block.gpsimd
            def _(pool):
                nc.gpsimd.memset(keep.ident[:], 0.0).then_inc(pool_ok, 1)
                pool.wait_ge(pool_ok, 1)
                nc.gpsimd.affine_select(out=keep.ident[:], in_=keep.ident[:], compare_op=ALU.not_equal, fill=1.0,
                                        base=0, pattern=[[-1, P]], channel_multiplier=1).then_inc(ident_ok, 1)
                nc.gpsimd.memset(keep.mirror[:], 0.0).then_inc(pool_ok, 1)
                pool.wait_ge(pool_ok, 2)
                nc.gpsimd.affine_select(out=keep.mirror[:], in_=keep.mirror[:], compare_op=ALU.not_equal, fill=1.0,
                                        base=1 - P, pattern=[[1, P]], channel_multiplier=1)

            @block.scalar
            def _(act):
                def load_x(g):
                    for t in range(4):
                        act.dma_start(x_of[g % 2][:, t], x_v[:, 4 * g + t]).then_inc(x_in[g % 2], 16)

                def stats(g):
                    act.wait_ge(x_in[g % 2], 64 * (g // 2 + 1))
                    for t in range(4 * g, 4 * g + 4):
                        if t:
                            act.wait_ge(x_sq, t)
                        nc.scalar.activation(sq[:], x_of[g % 2][:, t % 4], ACT.Square,
                                             accum_out=stat[:, 0, t:t + 1]).then_inc(x_sq, 1)
                    act.wait_ge(x_sq, 4 * g + 4)
                    nc.scalar.activation(stat[:, 1, 4 * g:4 * g + 4], stat[:, 0, 4 * g:4 * g + 4], ACT.Sqrt,
                                         bias=keep.eps[:], scale=1.0 / D).then_inc(x_sd, 1)

                load_x(0)
                act.wait_ge(small_in, 16 * (SMALL + 2))
                nc.scalar.activation(ccol[:, 1, :], ccol[:, 0, :], ACT.Exp, scale=-1.0).then_inc(silu_a, 1)
                act.wait_ge(lam_d, 2)
                nc.scalar.activation(lam_s[:, 2:4], lam_s[:, 0:2], ACT.Exp).then_inc(lam_a, 1)
                act.wait_ge(silu_d, 1)
                stats(0)
                act.wait_ge(acc_ok, CHUNKS * DB)
                load_x(1)
                act.wait_ge(mod_ok, 1)
                for g in range(SUPER):
                    for d in range(DB):
                        if d == DB // 2 and g + 1 < SUPER:
                            stats(g + 1)
                        n = DB * g + d
                        act.wait_ge(x_t, n + 1)
                        if d % 2 == 0:
                            nc.scalar.activation(ht_hi[:, d, g * BANK:(g + 1) * BANK], ps_t[n % 4][:], ACT.Identity,
                                                 bias=keep.mod[:, d:d + 1], scale=keep.affine[:, 0, d:d + 1])
                        if n >= 2:
                            act.wait_ge(h_lo, n - 1)
                        nc.scalar.activation(tmp[:, n % 2], ps_t[n % 4][:], ACT.Identity,
                                             bias=keep.mod[:, d:d + 1],
                                             scale=keep.affine[:, 0, d:d + 1]).then_inc(h_f, 1)
                    if g + 2 < SUPER:
                        load_x(g + 2)

            @block.vector
            def _(dve):
                nc.vector.memset(keep.eps[:], EPS)
                nc.vector.memset(keep.one[:], 1.0)
                nc.vector.memset(rel[BUCKETS:BUCKETS + 1, :], MASK).then_inc(silu_d, 1)
                dve.wait_ge(small_in, 16 * (SMALL + 2))
                nc.vector.tensor_scalar(rel[0:BUCKETS, :], rel[0:BUCKETS, :], -1.0, None, ALU.mult).then_inc(rel_ok, 1)
                for n in range(2):
                    nc.vector.tensor_tensor_reduce(lam[:, 2 * n], lam[:, 2 * n], lam[:, 2 * n + 1], 1.0, 0.0,
                                                   ALU.mult, ALU.add, lam_s[:, n:n + 1]).then_inc(lam_d, 1)
                nc.vector.tensor_scalar(keep.qk_gain[:, 0:2], keep.qk_gain[:, 0:2], -(HD ** -0.5), None, ALU.mult)
                nc.vector.tensor_scalar(keep.sub_gain[:], keep.sub_gain[:], 1.0 - LAMBDA_INIT, None, ALU.mult)
                dve.wait_ge(silu_a, 1)
                nc.vector.tensor_scalar(ccol[:, 1, :], ccol[:, 1, :], 1.0, None, ALU.add).then_inc(silu_d, 1)
                dve.wait_ge(silu_d, 2)
                nc.vector.reciprocal(ccol[:, 1, :], ccol[:, 1, :]).then_inc(silu_d, 1)
                dve.wait_ge(silu_d, 3)
                nc.vector.tensor_tensor(keep.c_silu[:], ccol[:, 0, :], ccol[:, 1, :], ALU.mult).then_inc(silu_d, 1)
                dve.wait_ge(lam_a, 1)
                nc.vector.scalar_tensor_tensor(out=keep.neg_lambda[:], in0=lam_s[:, 3:4], scalar=-LAMBDA_INIT,
                                               in1=lam_s[:, 2:3], op0=ALU.add, op1=ALU.subtract)
                for n in range(-(-DIAG // BANK)):
                    w = min(BANK, DIAG - n * BANK)
                    dve.wait_ge(row_mm, n + 1)
                    nc.vector.tensor_copy(row[:, n * BANK:n * BANK + w], ps_row[:, 0:w]).then_inc(row_ok, 1)

                def scale_rows(g):
                    dve.wait_ge(x_sd, g + 1)
                    nc.vector.reciprocal(stat[:, 1, 4 * g:4 * g + 4], stat[:, 1, 4 * g:4 * g + 4]).then_inc(x_ri, 1)
                    dve.wait_ge(x_ri, g + 1)
                    for t in range(4):
                        x = x_of[g % 2][:, t]
                        nc.vector.tensor_scalar(x, x, stat[:, 1, 4 * g + t:4 * g + t + 1], None, ALU.mult).then_inc(x_n, 1)

                dve.wait_ge(silu_d, 4)
                for n in range(CHUNKS):
                    if n == CHUNKS // 2:
                        scale_rows(0)
                    dve.wait_ge(ada_in[n % 2], 16 * (n // 2 + 1))
                    if n >= 2:
                        dve.wait_ge(mod_part, n - 1)
                    weighted_rows(nc, dve, keep, acc[:, n % 2], ada[:, n % 2], acc_ok, n)
                dve.wait_ge(mod_part, CHUNKS)
                nc.vector.tensor_tensor(keep.mod[:, 0:2 * DB], ps_mod[:], keep.b_ada[:, 0:2 * DB], ALU.add).then_inc(mod_ok_d, 1)
                dve.wait_ge(mod_ok_d, 1)
                nc.vector.scalar_tensor_tensor(out=keep.affine[:, 0, :], in0=keep.mod[:, DB:2 * DB], scalar=1.0,
                                               in1=keep.norm_gain[:, 0, :], op0=ALU.add, op1=ALU.mult).then_inc(mod_ok, 1)
                for g in range(SUPER):
                    for d in range(DB):
                        if d == DB // 2 and g + 1 < SUPER:
                            scale_rows(g + 1)
                        n = DB * g + d
                        at = slice(g * BANK, (g + 1) * BANK)
                        dve.wait_ge(h_f, n + 1)
                        if d % 2:
                            nc.vector.tensor_copy(ht_hi[:, d, at], tmp[:, n % 2]).then_inc(h_hi, 1)
                            dve.wait_ge(h_hi, n // 2 + 1)
                        nc.vector.tensor_tensor(ht_lo[:, d, at], tmp[:, n % 2], f32(ht_hi[:, d, at]),
                                                ALU.subtract).then_inc(h_lo, 1)

            @block.tensor
            def _(pe):
                def ada_chunk(n):
                    pe.wait_ge(acc_ok, (n + 1) * DB)
                    for j in range(CJ):
                        mm = nc.tensor.matmul(ps_mod[:, n * CJ + j:n * CJ + j + 1], acc[:, n % 2, j * P:(j + 1) * P],
                                              keep.one[:], start=True, stop=True)
                    mm.then_inc(mod_part, 1)

                def transposes(g):
                    pe.wait_ge(x_n, 4 * g + 4)
                    for d in range(DB):
                        n = DB * g + d
                        if n >= 4:
                            pe.wait_ge(h_f, n - 3)
                        for t in range(4):
                            mm = nc.tensor.transpose(ps_t[n % 4][:, t * P:(t + 1) * P], x_of[g % 2][:, t, d * P:(d + 1) * P],
                                                     keep.ident[:])
                        mm.then_inc(x_t, 1)

                pe.wait_ge(rel_ok, 1)
                pe.wait_ge(silu_d, 1)
                for n in range(-(-DIAG // BANK)):
                    w = min(BANK, DIAG - n * BANK)
                    if n:
                        pe.wait_ge(row_ok, n)
                    nc.tensor.matmul(ps_row[:, 0:w], rel[:], hot[:, n * BANK:n * BANK + w], start=True,
                                     stop=True).then_inc(row_mm, 1)
                pe.wait_ge(silu_d, 4)
                for n in range(CHUNKS):
                    ada_chunk(n)
                pe.wait_ge(ident_ok, 1)
                for g in range(SUPER):
                    transposes(g)


def project(nc, ins, keep, scr, over):
    ht_hi, ht_lo, w_raw, w_in = over.ht_hi, over.ht_lo, over.w_raw, over.w_in
    ADA0 = 2 * DB
    with ExitStack() as ctx:
        def sb(name, shape, dt=F32):
            return ctx.enter_context(nc.sbuf_tensor(name, shape, dt))

        def pb(name, shape):
            return ctx.enter_context(nc.psum_tensor(name, shape, F32))

        def sem(name):
            return ctx.enter_context(nc.semaphore(name))

        ada = sb("ada_b", [P, 2, DB, P])
        w_hi = sb("w_hi", [P, DB, BANK], F32R)
        w_lo = sb("w_lo", [P, DB, BANK], F32R)
        sq = sb("sq_b", [P, 2, BANK])
        st = sb("st_b", [P, 2, 2, 8])
        qn = sb("qn", [P, 2, BANK])
        qt = sb("qt", [P, 2, BANK])
        p_hi = sb("p_hi", [P, 2, BANK], F32R)
        p_lo = sb("p_lo", [P, 2, BANK], F32R)
        ps = [pb(f"ps_p{i}", [P, BANK]) for i in range(4)]
        pst = [pb(f"ps_q{i}", [P, BANK]) for i in range(2)]
        ps_mod = pb("ps_mod_b", [P, 4 * DB])
        acc = sb("acc_b", [P, 2, P])

        ada_in = [sem(f"adab_in{i}") for i in range(2)]
        acc_ok = sem("acc_b_ok")
        ada_part = sem("ada_part")
        mod_ok = sem("modb_ok")
        w_hi_ok = sem("w_hi_ok")
        w_lo_ok = sem("w_lo_ok")
        w_free = sem("w_free")
        mm_ok = sem("mm_ok")
        sq_ok = sem("sq_ok")
        ss_ok = sem("ss_ok")
        sd_ok = sem("sd_ok")
        ri_ok = sem("ri_ok")
        ps_free = sem("ps_free")
        t_ok = sem("t_ok")
        qt_ok = sem("qt_ok")
        hi_ok = sem("hi_ok")
        lo_ok = sem("lo_ok")
        v_hi_ok = sem("v_hi_ok")
        stored = [sem(f"stored{i}") for i in range(2)]

        QK, V = 4, 2
        ada_v = ins["w_ada"][0].rearrange("(b p) n -> p b n", p=P)
        assert V * TB == 4 * DB
        qkh = scr.qk_hi.rearrange("i p s -> p i s")
        qkl = scr.qk_lo.rearrange("i p s -> p i s")
        vh = scr.v_hi.rearrange("h p t e -> p h t e")
        vl = scr.v_lo.rearrange("h p t e -> p h t e")

        with nc.Block() as block:
            def split_hi(act, c, first=False):
                for b in range(DB):
                    act.wait_ge(w_in[b], c * 16 + 16)
                    if not first and b < DB - 1:
                        act.wait_ge(w_free, (c - 1) * (DB - 1) + b + 1)
                    elif not first:
                        act.wait_ge(mm_ok, c * TB)
                    nc.scalar.copy(w_hi[:, b], w_raw[:, b]).then_inc(w_hi_ok, 1)

            def split_lo(dve, c):
                for b in range(DB):
                    dve.wait_ge(w_hi_ok, c * DB + b + 1)
                    nc.vector.tensor_tensor(w_lo[:, b], w_raw[:, b], f32(w_hi[:, b]),
                                            ALU.subtract).then_inc(w_lo_ok, 1)

            heads = lambda a: f32(a).rearrange("p (h n) -> p h n", h=4)

            @block.sync
            def _(sp):
                def load_ada(j):
                    if j >= 2:
                        sp.wait_ge(acc_ok, (j - 1) * DB)
                    sp.dma_start(ada[:, j % 2], ada_v[:, :, (ADA0 + j) * P:(ADA0 + j + 1) * P]).then_inc(ada_in[j % 2], 16)

                def load_next(c):
                    sp.wait_ge(w_hi_ok, c * DB + DB)
                    sp.wait_ge(w_lo_ok, c * DB + DB)
                    settle(sp, keep.passed)
                    load_qkv_weights(sp, ins, over, bass.ds((c + 1) * BANK, BANK))

                sp.sem_inc(ps_free, 4)
                sp.sem_inc(t_ok, 2)
                sp.sem_inc(qt_ok, 2)
                sp.sem_inc(lo_ok, 2)
                for parity in range(2):
                    sp.sem_inc(stored[parity], 32)
                for j in range(2):
                    load_ada(j)
                with sp.Fori(0, QK) as c:
                    load_next(c)
                    for t in range(TB):
                        sp.wait_ge(hi_ok, c * TB + t + 1)
                        settle(sp, keep.passed)
                        sp.dma_start(qkh[:, bass.ds(c * 4, 4), t * P:(t + 1) * P], heads(p_hi[:, t % 2])).then_inc(
                            stored[t % 2], 16)
                        sp.wait_ge(lo_ok, c * TB + t + 3)
                        settle(sp, keep.passed)
                        sp.dma_start(qkl[:, bass.ds(c * 4, 4), t * P:(t + 1) * P], heads(p_lo[:, t % 2])).then_inc(
                            stored[t % 2], 16)
                for v in range(V):
                    if v < V - 1:
                        load_next(QK + v)
                    for t in range(TB):
                        sp.wait_ge(v_hi_ok, v * TB + t + 1)
                        sp.dma_start(vh[:, 4 * v:4 * v + 4, t], heads(p_hi[:, t % 2])).then_inc(stored[t % 2], 16)
                        sp.wait_ge(ps_free, (QK + v) * TB + t + 5)
                        sp.dma_start(vl[:, 4 * v:4 * v + 4, t], heads(p_lo[:, t % 2])).then_inc(stored[t % 2], 16)
                        if v * TB + t + 2 < V * TB:
                            load_ada(v * TB + t + 2)
                for parity in range(2):
                    sp.wait_ge(stored[parity], 32 * (1 + (QK + V) * TB // 2))

            @block.gpsimd
            def _(pool):
                with pool.Fori(0, QK) as c:
                    for t in range(TB):
                        n = c * TB + t
                        pool.wait_ge(qt_ok, n + 3)
                        pool.wait_ge(stored[t % 2], (c * (TB // 2) + t // 2 + 1) * 32)
                        settle(pool, keep.passed)
                        nc.gpsimd.tensor_copy(p_hi[:, t % 2], qt[:, t % 2]).then_inc(hi_ok, 1)
                        pool.wait_ge(hi_ok, n + 1)
                        nc.gpsimd.tensor_tensor(p_lo[:, t % 2], qt[:, t % 2], f32(p_hi[:, t % 2]),
                                                ALU.subtract).then_inc(lo_ok, 1)

            @block.scalar
            def _(act):
                split_hi(act, 0, first=True)
                with act.Fori(0, QK) as c:
                    for t in range(TB):
                        n = c * TB + t
                        act.wait_ge(mm_ok, n + 1)
                        nc.scalar.activation(sq[:, t % 2], ps[t % 4][:], ACT.Square).then_inc(sq_ok, 1)
                        act.wait_ge(ss_ok, n + 1)
                        nc.scalar.activation(st[:, t % 2, 1], st[:, t % 2, 0], ACT.Sqrt, bias=keep.eps[:],
                                             scale=1.0 / HD).then_inc(sd_ok, 1)
                        if t == TB - 2:
                            split_hi(act, c + 1)
                        act.wait_ge(t_ok, n + 3)
                        act.wait_ge(lo_ok, n + 1)
                        settle(act, keep.passed)
                        nc.scalar.activation(qt[:, t % 2], pst[t % 2][:], ACT.Copy,
                                             scale=keep.qk_gain[:, bass.ds(c, 1)]).then_inc(qt_ok, 1)
                for v in range(V):
                    for t in range(TB):
                        if v < V - 1 and t == TB - 1:
                            split_hi(act, QK + v + 1)
                        act.wait_ge(mm_ok, (QK + v) * TB + t + 1)
                        act.wait_ge(stored[t % 2], 32 * (QK * TB // 2 + (v * TB + t) // 2 + 1))
                        nc.scalar.copy(p_hi[:, t % 2], ps[t % 4][:]).then_inc(v_hi_ok, 1)

            @block.vector
            def _(dve):
                split_lo(dve, 0)
                with dve.Fori(0, QK) as c:
                    for t in range(TB):
                        n = c * TB + t
                        if t == TB - 1:
                            split_lo(dve, c + 1)
                        dve.wait_ge(sq_ok, n + 1)
                        nc.vector.tensor_reduce(st[:, t % 2, 0], sq[:, t % 2].rearrange("p (g d) -> p g d", d=HD), AX_X,
                                                ALU.add).then_inc(ss_ok, 1)
                        dve.wait_ge(sd_ok, n + 1)
                        nc.vector.reciprocal(st[:, t % 2, 1], st[:, t % 2, 1]).then_inc(ri_ok, 1)
                        dve.wait_ge(ri_ok, n + 1)
                        dve.wait_ge(t_ok, n + 1)
                        nc.vector.tensor_tensor(qn[:, t % 2].rearrange("p (g d) -> p g d", d=HD),
                                                ps[t % 4][:].rearrange("p (g d) -> p g d", d=HD),
                                                st[:, t % 2, 1].rearrange("p (g b) -> p g b", b=1).to_broadcast([P, 8, HD]),
                                                ALU.mult).then_inc(ps_free, 1)
                for v in range(V):
                    for t in range(TB):
                        if v < V - 1 and t == TB - 1:
                            split_lo(dve, QK + v + 1)
                        j = v * TB + t
                        dve.wait_ge(ada_in[j % 2], 16 * (j // 2 + 1))
                        if j >= 2:
                            dve.wait_ge(ada_part, j - 1)
                        weighted_rows(nc, dve, keep, acc[:, j % 2], ada[:, j % 2], acc_ok, j)
                        dve.wait_ge(v_hi_ok, v * TB + t + 1)
                        nc.vector.tensor_tensor(p_lo[:, t % 2], ps[t % 4][:], f32(p_hi[:, t % 2]),
                                                ALU.subtract).then_inc(ps_free, 1)
                dve.wait_ge(ada_part, V * TB)
                nc.vector.tensor_tensor(keep.mod[:, ADA0:6 * DB], ps_mod[:], keep.b_ada[:, ADA0:6 * DB], ALU.add
                                        ).then_inc(mod_ok, 1)
                dve.wait_ge(mod_ok, 1)
                nc.vector.scalar_tensor_tensor(out=keep.affine[:, 1, :], in0=keep.mod[:, 4 * DB:5 * DB], scalar=1.0,
                                               in1=keep.norm_gain[:, 1, :], op0=ALU.add, op1=ALU.mult)

            @block.tensor
            def _(pe):
                def product(c, t):
                    n = c * TB + t
                    pe.wait_ge(ps_free, n + 1)
                    tok = slice(t * P, (t + 1) * P)
                    for b in range(DB):
                        if t == 0:
                            pe.wait_ge(w_lo_ok, c * DB + b + 1)
                        nc.tensor.matmul(ps[t % 4][:], ht_hi[:, b, tok], w_hi[:, b], start=(b == 0), stop=False)
                        nc.tensor.matmul(ps[t % 4][:], ht_hi[:, b, tok], w_lo[:, b], start=False, stop=False)
                        mm = nc.tensor.matmul(ps[t % 4][:], ht_lo[:, b, tok], w_hi[:, b], start=False, stop=(b == DB - 1))
                        if t == TB - 1 and b < DB - 1:
                            mm.then_inc(w_free, 1)
                    mm.then_inc(mm_ok, 1)

                def transposes(c, t, order):
                    n = c * TB + t
                    pe.wait_ge(ps_free, n + 5)
                    pe.wait_ge(qt_ok, n + 1)
                    for k in range(4):
                        mm = nc.tensor.transpose(pst[t % 2][:, k * P:(k + 1) * P], qn[:, t % 2, k * P:(k + 1) * P],
                                                 order[:])
                    mm.then_inc(t_ok, 1)

                product(0, 0)
                for first, order in ((0, keep.mirror), (QK // 2, keep.ident)):
                    with pe.Fori(first, first + QK // 2) as c:
                        for t in range(1, TB):
                            product(c, t)
                            transposes(c, t - 1, order)
                        product(c + 1, 0)
                        transposes(c, TB - 1, order)
                for n in range(V * TB):
                    if n:
                        product(QK + n // TB, n % TB)
                    pe.wait_ge(acc_ok, (n + 1) * DB)
                    nc.tensor.matmul(ps_mod[:, n:n + 1], acc[:, n % 2], keep.one[:], start=True, stop=True).then_inc(ada_part, 1)


def attend(nc, keep, scr):
    UNIT = 2 * BANK
    STEPS = TB
    SLOTS = 5
    WAYS = 2

    def keys(i):
        return (STEPS - i) * P

    def units(i):
        return -(-keys(i) // UNIT)

    def groups(i):
        return -(-keys(i) // BANK)

    def units_before(i):
        return sum(2 * units(k) for k in range(i))

    def groups_before(i):
        return sum(groups(k) for k in range(i))

    def pv_before(q):
        return sum(SUPER - k for k in range(q))

    UNITS, GROUPS, PV_GROUPS = units_before(STEPS), groups_before(STEPS), pv_before(SUPER)
    EACH = GROUPS // WAYS
    assert GROUPS % (2 * WAYS) == 0 and PV_GROUPS % SLOTS == 0 and UNITS % 2 == 0
    PV_AT = {4: [(0, 0), (0, 1)], 5: [(0, 2)], 6: [(0, 3)], 8: [(1, 0)], 9: [(1, 1)], 10: [(1, 2)],
             12: [(2, 0)], 13: [(2, 1)]}
    OUT_AT = {7: 0, 11: 1, 14: 2}

    def bank_of(n):
        return 2 if n % 2 else n // 2 % 2

    def slot_view(t, i, g, w):
        c = (STEPS - 1 - i) % 4
        slot = (pv_before(i // 4) + g) % SLOTS
        return t[:, slot, 0:w // P, c * P:(c + 1) * P]

    with ExitStack() as ctx:
        def sb(name, shape, dt=F32):
            return ctx.enter_context(nc.sbuf_tensor(name, shape, dt))

        def pb(name, shape):
            return ctx.enter_context(nc.psum_tensor(name, shape, F32))

        def sem(name):
            return ctx.enter_context(nc.semaphore(name))

        q_st = sb("q_st", [P, 2, S], F32R)
        k_hi = sb("k_hi", [P, 2, S], F32R)
        k_lo = sb("k_lo", [P, 2, S], F32R)
        v_hi = sb("v_hi_sb", [P, TB, P], F32R)
        v_lo = sb("v_lo_sb", [P, TB, P], F32R)
        bias = sb("bias", [P, 2, S])
        sc = sb("sc", [P, 2, 2, S])
        p_hi = sb("pt_hi", [P, SLOTS, 4, BANK], F32R)
        p_lo = sb("pt_lo", [P, SLOTS, 4, BANK], F32R)
        tf = sb("tf", [P, 2, BANK])
        o_sb = sb("o_sb", [P, 2, BANK])
        low = sb("low", [P, 2, 2, 2])
        den = sb("den", [P, 2, TB])
        coef = sb("coef", [P, 2])
        dens = sb("dens", [P, TB, HEADS])
        ps_s = pb("ps_s", [P, 2, UNIT])
        ps_t = [pb(f"ps_u{i}", [P, BANK]) for i in range(3)]
        ps_o = pb("ps_o", [P, BANK])

        q_in = [sem(f"q_in{c}") for c in range(SUPER)]
        k_in = [sem(f"k_in{c}") for c in range(SUPER)]
        v_in = [sem(f"v_in{c}") for c in range(SUPER)]
        b_in = [sem(f"b_in{c}") for c in range(SUPER)]
        s_ok = sem("s_ok")
        a_ok = sem("a_ok")
        e_ok = sem("e_ok")
        rec_ok = sem("rec_ok")
        coef_ok = sem("coef_ok")
        c_ok = sem("c_ok")
        t_ok = sem("tt_ok")
        even_hi = sem("even_hi")
        even_lo = sem("even_lo")
        odd_hi = sem("odd_hi")
        odd_lo = sem("odd_lo")
        pv_ok = sem("pv_ok")
        o_ok = sem("o_ok")
        o_out = [sem(f"o_out{i}") for i in range(2)]
        d_ok = sem("d_ok")
        d_out = sem("d_out")

        def heads_of(eng, body):
            with eng.Fori(0, HEADS - 1) as h:
                body(h, False)
            body(HEADS - 1, True)

        def following(h, i, last):
            if i < STEPS - 1:
                return h, i + 1
            return None if last else (h + 1, 0)

        with nc.Block() as block:
            @block.sync
            def _(sp):
                halves = (slice(0, HD), slice(HD, P))

                def part(src, i, c):
                    return src[bass.ds(i, 1)].rearrange("i (m d) s -> d (i m) s", m=2)[:, :, c * BANK:(c + 1) * BANK]

                def load_q(h, c):
                    cols = slice(c * BANK, (c + 1) * BANK)
                    for half, src in zip(halves, (scr.qk_hi, scr.qk_lo)):
                        sp.dma_start(f32(q_st[half, :, cols]), part(src, h, c)).then_inc(q_in[c], 16)

                def load_k(h, c):
                    cols = slice(c * BANK, (c + 1) * BANK)
                    for to, src in ((k_hi, scr.qk_hi), (k_lo, scr.qk_lo)):
                        for half in halves:
                            sp.dma_start(f32(to[half, :, cols]), part(src, h + HEADS, c)).then_inc(k_in[c], 16)

                def load_v(h, c):
                    at = slice(4 * c, 4 * c + 4)
                    for to, src in ((v_hi, scr.v_hi), (v_lo, scr.v_lo)):
                        sp.dma_start(f32(to[:, at]), src[bass.ds(h, 1)].rearrange("i p t e -> p (i t) e")[:, at]).then_inc(
                            v_in[c], 16)

                def load_bias(h, x):
                    rows = bass.AP(scr.bias_row.tensor, x * BANK, [[1, P], [DIAG, 2 * HEADS], [1, BANK]])
                    sp.dma_start(bias[:, :, x * BANK:(x + 1) * BANK], rows[:, bass.ds(h * 2, 2)]).then_inc(b_in[x], 16)

                def store_o(h, q):
                    cols = slice((SUPER - 1 - q) * BANK, (SUPER - q) * BANK)
                    sp.wait_ge(o_ok, h * SUPER + q + 2)
                    settle(sp, keep.passed)
                    sp.dma_start(scr.o_t[bass.ds(h, 1)].rearrange("i p s -> p (i s)")[:, cols], o_sb[:, q % 2]).then_inc(
                        o_out[q % 2], 16)

                def head(h, last):
                    for q in range(SUPER):
                        c = SUPER - 1 - q
                        if not last:
                            sp.wait_ge(s_ok, h * UNITS + units_before(4 * q + 4))
                            settle(sp, keep.passed)
                            load_q(h + 1, c)
                            load_k(h + 1, c)
                            sp.wait_ge(a_ok, h * UNITS + units_before(4 * q + 4) + 2)
                            settle(sp, keep.passed)
                            load_bias(h + 1, q)
                            if q:
                                sp.wait_ge(pv_ok, h * PV_GROUPS + pv_before(q) + SLOTS)
                                settle(sp, keep.passed)
                                load_v(h + 1, c + 1)
                        if q:
                            store_o(h, q - 1)
                    if not last:
                        sp.wait_ge(pv_ok, h * PV_GROUPS + PV_GROUPS + SLOTS)
                        settle(sp, keep.passed)
                        load_v(h + 1, 0)
                    store_o(h, SUPER - 1)

                sp.sem_inc(a_ok, 2)
                sp.sem_inc(t_ok, 1)
                sp.sem_inc(even_lo, 2)
                sp.sem_inc(odd_hi, 1)
                sp.sem_inc(odd_lo, 2)
                sp.sem_inc(pv_ok, SLOTS)
                sp.sem_inc(o_ok, 1)
                for i in range(2):
                    sp.sem_inc(o_out[i], 16)
                load_q(0, SUPER - 1)
                for c in range(SUPER):
                    load_k(0, c)
                    load_bias(0, c)
                for c in reversed(range(SUPER - 1)):
                    load_q(0, c)
                for c in range(SUPER):
                    load_v(0, c)
                heads_of(sp, head)
                sp.wait_ge(d_ok, 2 * HEADS)
                sp.dma_start(scr.l_sum, dens[:]).then_inc(d_out, 16)
                sp.wait_ge(d_out, 16)
                for i in range(2):
                    sp.wait_ge(o_out[i], 16 * (1 + HEADS * SUPER // 2))

            @block.tensor
            def _(pe):
                def scores(h, i, m, u):
                    n = units_before(i) + m * units(i) + u
                    pe.wait_ge(a_ok, h * UNITS + n + 1)
                    q_cols = slice((STEPS - 1 - i) * P, (STEPS - i) * P)
                    if i % 4 == 0 and m == 0 and u == 0:
                        pe.wait_ge(q_in[SUPER - 1 - i // 4], (h + 1) * 32)
                    for b in range(2 * u, min(2 * u + 2, groups(i))):
                        w = min(BANK, keys(i) - b * BANK)
                        if i == 0 and m == 0:
                            pe.wait_ge(k_in[b], (h + 1) * 64)
                        out = ps_s[:, n % 2, (b % 2) * BANK:(b % 2) * BANK + w]
                        for k in (k_hi, k_lo):
                            mm = nc.tensor.matmul(out, q_st[:, m, q_cols], k[:, m, b * BANK:b * BANK + w],
                                                  start=(k is k_hi), stop=(k is k_lo))
                    mm.then_inc(s_ok, 1)

                def transposes(h, i, g):
                    n = groups_before(i) + g
                    before = units_before(i) // 2
                    pe.wait_ge(c_ok, h * (UNITS // 2) + before + g // 2 + 1)
                    pe.wait_ge(odd_hi if n % 2 else even_lo, h * EACH + n // 2 + 1)
                    w = min(BANK, keys(i) - g * BANK)
                    for k in range(w // P):
                        at = g * BANK + k * P
                        mm = nc.tensor.transpose(ps_t[bank_of(n)][:, k * P:(k + 1) * P], sc[:, i % 2, 0, at:at + P],
                                                 keep.ident[:])
                    mm.then_inc(t_ok, 1)

                def pv(h, q, g):
                    s = SUPER - 1 - q
                    slot = (pv_before(q) + g) % SLOTS
                    n = groups_before(4 * q + 3) + g + 1
                    pe.wait_ge(even_lo, h * EACH + (n + 1) // 2 + 2)
                    pe.wait_ge(odd_lo, h * EACH + n // 2 + 2)
                    pe.wait_ge(v_in[g], (h + 1) * 32)
                    if g == 0:
                        pe.wait_ge(o_ok, h * SUPER + q + 1)
                    for kb in range(4 * g, 4 * g + 4):
                        c0 = max(kb - 4 * s, 0) * P
                        for v, p in ((v_hi, p_lo), (v_lo, p_hi), (v_hi, p_hi)):
                            mm = nc.tensor.matmul(ps_o[:, c0:BANK], v[:, kb], p[:, slot, kb % 4, c0:BANK],
                                                  start=(kb == 0 and p is p_lo),
                                                  stop=(kb == 4 * s + 3 and v is v_hi and p is p_hi))
                    mm.then_inc(pv_ok, 1)

                def head(h, last):
                    for i in range(STEPS):
                        then = following(h, i, last)
                        if then:
                            for u in range(units(then[1])):
                                scores(*then, 1, u)
                        for q, g in PV_AT.get(i, []):
                            pv(h, q, g)
                        for g in range(groups(i)):
                            transposes(h, i, g)
                        then = then and following(*then, last)
                        if then:
                            for u in range(units(then[1])):
                                scores(*then, 0, u)
                    pv(h, SUPER - 1, 0)

                for m in range(2):
                    for u in range(units(0)):
                        scores(0, 0, m, u)
                for u in range(units(1)):
                    scores(0, 1, 0, u)
                heads_of(pe, head)

            @block.scalar
            def _(act):
                def exponentials(h, i, m):
                    u = units_before(i) + (m + 1) * units(i)
                    act.wait_ge(a_ok, h * UNITS + u + 2)
                    s = sc[:, i % 2, m, 0:keys(i)]
                    nc.scalar.activation(s, s, ACT.Exp, bias=low[:, i % 2, m, units(i) - 1:units(i)], scale=-1.0,
                                         accum_out=den[:, m, TB - 1 - i:TB - i]).then_inc(e_ok, 1)

                def out_of_psum(h, i, g):
                    n = groups_before(i) + g
                    w = min(BANK, keys(i) - g * BANK)
                    act.wait_ge(t_ok, h * GROUPS + n + 2)
                    if n % 2:
                        act.wait_ge(odd_lo, h * EACH + n // 2 + 1)
                        nc.scalar.copy(tf[:, (n // 2) % 2, 0:w], ps_t[2][:, 0:w])
                    if i % 4 == 0:
                        act.wait_ge(pv_ok, h * PV_GROUPS + pv_before(i // 4) + g + 1)
                    nc.scalar.copy(slot_view(p_hi, i, g, w), ps_t[bank_of(n)][:, 0:w].rearrange("p (k c) -> p k c", c=P)
                                   ).then_inc(odd_hi if n % 2 else even_hi, 1)

                def out_super(h, q):
                    act.wait_ge(pv_ok, h * PV_GROUPS + pv_before(q + 1) + SLOTS)
                    act.wait_ge(o_out[q % 2], 16 * (h * (SUPER // 2) + q // 2 + 1))
                    nc.scalar.copy(o_sb[:, q % 2], ps_o[:]).then_inc(o_ok, 1)

                def head(h, last):
                    for i in range(STEPS):
                        then = following(h, i, last)
                        if then:
                            exponentials(*then, 0)
                        for g in range(groups(i)):
                            out_of_psum(h, i, g)
                        if then:
                            exponentials(*then, 1)
                        if i in OUT_AT:
                            out_super(h, OUT_AT[i])
                    out_super(h, SUPER - 1)

                for m in range(2):
                    exponentials(0, 0, m)
                heads_of(act, head)

            @block.gpsimd
            def _(pool):
                def head(h, last):
                    for i in range(STEPS):
                        for g in range(groups(i)):
                            n = groups_before(i) + g
                            if n % 2 == 0:
                                continue
                            w = min(BANK, keys(i) - g * BANK)
                            pool.wait_ge(odd_hi, h * EACH + n // 2 + 2)
                            nc.gpsimd.tensor_tensor(slot_view(p_lo, i, g, w),
                                                    tf[:, (n // 2) % 2, 0:w].rearrange("p (k c) -> p k c", c=P),
                                                    f32(slot_view(p_hi, i, g, w)), ALU.subtract).then_inc(odd_lo, 1)

                heads_of(pool, head)

            @block.vector
            def _(dve):
                def add_bias(h, i, m, u, first=False):
                    n = units_before(i) + m * units(i) + u
                    dve.wait_ge(s_ok, h * UNITS + n + 1)
                    w = min(UNIT, keys(i) - u * UNIT)
                    x0 = i * P + u * UNIT
                    if i == 0 and m == 0:
                        for x in (2 * u, 2 * u + 1):
                            dve.wait_ge(b_in[x], (h + 1) * 16)
                    if u:
                        dve.wait_ge(a_ok, h * UNITS + n + 2)
                    read = groups_before(i - 1) if i >= 2 else -groups(STEPS - 1) if i == 0 else 0
                    if not first:
                        dve.wait_ge(t_ok, h * GROUPS + read + 1)
                    settle(dve, keep.passed)
                    nc.vector.tensor_tensor_reduce(sc[:, i % 2, m, u * UNIT:u * UNIT + w], ps_s[:, n % 2, 0:w],
                                                   bias[:, m, x0:x0 + w], 1.0,
                                                   low[:, i % 2, m, 0:1] if u else FAR, ALU.add, ALU.min,
                                                   low[:, i % 2, m, u:u + 1]).then_inc(a_ok, 1)

                def weigh(h, i):
                    n = h * STEPS + i
                    dve.wait_ge(e_ok, n * 2 + 2)
                    nc.vector.reciprocal(coef[:, 0:1], den[:, 1, TB - 1 - i:TB - i]).then_inc(rec_ok, 1)
                    dve.wait_ge(rec_ok, n + 1)
                    nc.vector.scalar_tensor_tensor(out=coef[:, 1:2], in0=den[:, 0, TB - 1 - i:TB - i], scalar=keep.neg_lambda[:],
                                                   in1=coef[:, 0:1], op0=ALU.mult, op1=ALU.mult).then_inc(coef_ok, 1)
                    dve.wait_ge(coef_ok, n + 1)

                def combine(h, i, u):
                    if u == 0:
                        weigh(h, i)
                    at = slice(u * UNIT, min((u + 1) * UNIT, keys(i)))
                    a, b = sc[:, i % 2, 0, at], sc[:, i % 2, 1, at]
                    nc.vector.scalar_tensor_tensor(out=a, in0=b, scalar=coef[:, 1:2], in1=a, op0=ALU.mult,
                                                   op1=ALU.add).then_inc(c_ok, 1)

                def split_lo(h, i, g):
                    n = groups_before(i) + g
                    dve.wait_ge(even_hi, h * EACH + n // 2 + 1)
                    w = min(BANK, keys(i) - g * BANK)
                    nc.vector.tensor_tensor(slot_view(p_lo, i, g, w), ps_t[bank_of(n)][:, 0:w].rearrange("p (k c) -> p k c", c=P),
                                            f32(slot_view(p_hi, i, g, w)), ALU.subtract).then_inc(even_lo, 1)

                def keep_sums(h, i0, i1):
                    nc.vector.tensor_copy(dens[:, i0:i1, bass.ds(h, 1)],
                                          den[:, 0, i0:i1].rearrange("p (t b) -> p t b", b=1)).then_inc(d_ok, 1)

                def head(h, last):
                    for i in range(STEPS):
                        then = following(h, i, last)
                        evens = [g for g in range(groups(i)) if (groups_before(i) + g) % 2 == 0]
                        if i == STEPS - 1:
                            keep_sums(h, 1, TB)
                        if then:
                            for u in range(units(then[1])):
                                add_bias(*then, 0, u)
                        for u in range(units(i)):
                            combine(h, i, u)
                        adds = [(*then, 1, u) for u in range(units(then[1]))] if then else []
                        while adds or evens:
                            if adds:
                                add_bias(*adds.pop(0))
                            if evens:
                                split_lo(h, i, evens.pop(0))
                    keep_sums(h, 0, 1)

                for m in range(2):
                    for u in range(units(0)):
                        add_bias(0, 0, m, u, first=True)
                heads_of(dve, head)


def mix(nc, ins, keep, scr):
    with ExitStack() as ctx:
        def sb(name, shape, dt=F32):
            return ctx.enter_context(nc.sbuf_tensor(name, shape, dt))

        def pb(name, shape):
            return ctx.enter_context(nc.psum_tensor(name, shape, F32))

        def sem(name):
            return ctx.enter_context(nc.semaphore(name))

        wo_raw = sb("wo_raw", [P, 2, D])
        wo_hi = sb("wo_hi", [P, HEADS, D], F32R)
        wo_lo = sb("wo_lo", [P, HEADS, D], F32R)
        gate = sb("gate_m", [P, D])
        diag = sb("diag_m", [P, P])
        ones = sb("ones_m", [P, P])
        ot = sb("ot", [P, 2, HEADS, P])
        xr = sb("xr", [P, 2, D])
        den = sb("den_m", [P, TB, HEADS])
        sq = sb("sq_m", [P, D])
        st = sb("st_m", [P, 2, HEADS])
        on = sb("on", [P, D])
        o_hi = sb("o_hi", [P, 2, D], F32R)
        o_lo = sb("o_lo", [P, 2, D], F32R)
        x1 = sb("x1_m", [P, 2, D])
        sq2 = sb("sq2_m", [P, D])
        st2 = sb("st2_m", [P, 2])
        xn = sb("xn_m", [P, D])
        hf = sb("hf", [P, 2, D])
        h_hi = sb("h_hi_m", [P, 2, D], F32R)
        h_lo = sb("h_lo_m", [P, 2, D], F32R)
        ps_a = pb("ps_a", [P, D])
        ps_b = pb("ps_b", [P, D])
        ps_y = pb("ps_y", [P, D])
        ps_d = pb("ps_d", [P, D])

        wo_in = [sem(f"wo_in{i}") for i in range(2)]
        wo_hi_ok = sem("wo_hi_ok")
        wo_lo_ok = sem("wo_lo_ok")
        gate_d = sem("gate_d")
        gate_m = sem("gate_mm")
        gate_ok = sem("gate_ok")
        den_in = sem("den_in")
        den_ok = sem("den_ok")
        o_in = [sem(f"o_in{i}") for i in range(2)]
        x_in = [sem(f"xm_in{i}") for i in range(2)]
        ta_ok = sem("ta_ok")
        sq_ok = sem("sqm_ok")
        ss_ok = sem("ssm_ok")
        var_ok = sem("var_ok")
        sd_ok = sem("sdm_ok")
        ri_ok = sem("rim_ok")
        on_ok = sem("on_ok")
        tb_ok = sem("tb_ok")
        ohi_ok = sem("ohi_ok")
        olo_ok = sem("olo_ok")
        y_ok = sem("y_ok")
        gy_ok = sem("gy_ok")
        x1_ok = sem("x1_ok")
        sq2_ok = sem("sq2_ok")
        sd2_ok = sem("sd2_ok")
        ri2_ok = sem("ri2_ok")
        xn_ok = sem("xn_ok")
        td_ok = sem("td_ok")
        hf_ok = sem("hf_ok")
        hhi_ok = sem("hhi_ok")
        hlo_ok = sem("hlo_ok")
        x1_out = [sem(f"x1_out{i}") for i in range(2)]
        h_out = [sem(f"h_out{i}") for i in range(2)]

        wo_v = ins["da_w_o"][0].rearrange("(h p) n -> h p n", p=P)
        ot_v = scr.o_t.rearrange("h p s -> p h s")
        blocks = lambda a: a.rearrange("p (b n) -> p b n", n=P)
        wide = lambda a: a.rearrange("p (b n) -> p b n", n=1).to_broadcast([P, HEADS, P])

        class Block:

            def __init__(self, pair, k):
                self.pair, self.k = pair, k
                self.t = pair * 2 + k
                self.turn = pair + k // 2
                self.side = k % 2

            def reaches(self, n):
                return not isinstance(self.t, int) or self.t >= n

            def valid(self):
                return not isinstance(self.t, int) or 0 <= self.t < TB

        def iterations(eng, body):
            def run(pair, k):
                body(lambda d: Block(pair, k + d))

            for pair in (-1, 0, 1):
                for k in range(2):
                    run(pair, k)
            with eng.Fori(2, TB // 2 - 2) as pair:
                for k in range(2):
                    run(pair, k)
            for pair in (TB // 2 - 2, TB // 2 - 1, TB // 2):
                for k in range(2):
                    run(pair, k)

        with nc.Block() as block:
            @block.sync
            def _(sp):
                def load_o(b):
                    if b.reaches(2):
                        sp.wait_ge(ta_ok, b.t - 1)
                        settle(sp, keep.passed)
                    sp.dma_start(ot[:, b.side], ot_v[:, :, bass.ds(b.t * P, P)]).then_inc(o_in[b.side], 16)

                def load_x(b):
                    if b.reaches(2):
                        sp.wait_ge(x1_ok, b.t - 1)
                        settle(sp, keep.passed)
                    sp.dma_start(xr[:, b.side], ins["x"][0][bass.ds(b.t * P, P)]).then_inc(x_in[b.side], 16)

                def store_x1(b):
                    sp.wait_ge(x1_ok, b.t + 1)
                    settle(sp, keep.passed)
                    sp.dma_start(scr.x1[bass.ds(b.t * P, P)], x1[:, b.side]).then_inc(x1_out[b.side], 16)

                def store_h(b):
                    for part_ok, part, to in ((hhi_ok, h_hi, scr.h2_hi), (hlo_ok, h_lo, scr.h2_lo)):
                        sp.wait_ge(part_ok, b.t + 1)
                        settle(sp, keep.passed)
                        sp.dma_start(to[:, :, bass.ds(b.t * P, P)], f32(blocks(part[:, b.side]))).then_inc(h_out[b.side], 16)

                def body(at):
                    if at(3).valid() and at(3).reaches(2):
                        load_o(at(3))
                    if at(1).valid() and at(1).reaches(2):
                        load_x(at(1))
                    if at(-1).valid():
                        store_x1(at(-1))
                    if at(-2).valid():
                        store_h(at(-2))

                sp.dma_start(den[:], scr.l_sum).then_inc(den_in, 16)
                for k in range(2):
                    load_o(Block(0, k))
                for hh in range(HEADS):
                    if hh >= 2:
                        sp.wait_ge(wo_lo_ok, hh - 1)
                    sp.dma_start(wo_raw[:, hh % 2], wo_v[hh]).then_inc(wo_in[hh % 2], 16)
                for k in range(2):
                    load_x(Block(0, k))
                iterations(sp, body)
                for i in range(2):
                    sp.wait_ge(x1_out[i], 16 * TB // 2)
                    sp.wait_ge(h_out[i], 32 * TB // 2)

            @block.gpsimd
            def _(pool):
                def second_lo(b):
                    pool.wait_ge(hhi_ok, b.t + 1)
                    nc.gpsimd.tensor_tensor(h_lo[:, b.side], hf[:, b.side], f32(h_hi[:, b.side]), ALU.subtract
                                            ).then_inc(hlo_ok, 1)

                def body(at):
                    if at(-2).valid():
                        second_lo(at(-2))

                iterations(pool, body)

            @block.scalar
            def _(act):
                def squares(b):
                    act.wait_ge(ta_ok, b.t + 1)
                    if b.reaches(1):
                        act.wait_ge(ss_ok, b.t)
                    nc.scalar.activation(sq[:], ps_a[:], ACT.Square).then_inc(sq_ok, 1)

                def deviations(b):
                    act.wait_ge(var_ok, b.t + 1)
                    nc.scalar.activation(st[:, 1], st[:, 0], ACT.Sqrt).then_inc(sd_ok, 1)

                def first_hi(b):
                    act.wait_ge(tb_ok, b.t + 1)
                    if b.reaches(2):
                        act.wait_ge(y_ok, 2 * b.t - 2)
                    nc.scalar.copy(o_hi[:, b.side], ps_b[:]).then_inc(ohi_ok, 1)

                def second_norm(b):
                    act.wait_ge(x1_ok, b.t + 1)
                    nc.scalar.activation(sq2[:], x1[:, b.side], ACT.Square, accum_out=st2[:, 0:1]).then_inc(sq2_ok, 1)
                    act.wait_ge(sq2_ok, b.t + 1)
                    nc.scalar.activation(st2[:, 1:2], st2[:, 0:1], ACT.Sqrt, bias=keep.eps[:],
                                         scale=1.0 / D).then_inc(sd2_ok, 1)

                def second_affine(b):
                    act.wait_ge(td_ok, b.t + 1)
                    if b.reaches(2):
                        act.wait_ge(hlo_ok, b.t - 1)
                    for d in range(DB):
                        at = slice(d * P, (d + 1) * P)
                        a = nc.scalar.activation(hf[:, b.side, at], ps_d[:, at], ACT.Identity,
                                                 bias=keep.mod[:, 3 * DB + d:3 * DB + d + 1],
                                                 scale=keep.affine[:, 1, d:d + 1])
                    a.then_inc(hf_ok, 1)
                    act.wait_ge(hf_ok, b.t + 1)
                    if b.reaches(2):
                        act.wait_ge(h_out[b.side], 32 * b.turn)
                    nc.scalar.copy(h_hi[:, b.side], hf[:, b.side]).then_inc(hhi_ok, 1)

                def body(at):
                    if at(-1).valid():
                        second_norm(at(-1))
                    if at(-2).valid():
                        second_affine(at(-2))
                    if at(1).valid():
                        first_hi(at(1))
                    if at(2).valid():
                        squares(at(2))
                        deviations(at(2))

                for hh in range(HEADS):
                    act.wait_ge(wo_in[hh % 2], 16 * (hh // 2 + 1))
                    nc.scalar.activation(wo_hi[:, hh], wo_raw[:, hh % 2], ACT.Copy, scale=keep.sub_gain[:]).then_inc(wo_hi_ok, 1)
                iterations(act, body)

            @block.vector
            def _(dve):
                def gate_row(first, j):
                    if j:
                        dve.wait_ge(gate_m, j)
                    nc.vector.tensor_scalar(diag[:], keep.ident[:], keep.mod[:, first + j:first + j + 1], None,
                                            ALU.mult).then_inc(gate_d, 1)

                def head_rows(b):
                    dve.wait_ge(sq_ok, b.t + 1)
                    if b.reaches(1):
                        dve.wait_ge(sd_ok, b.t)
                    nc.vector.tensor_reduce(st[:, 0], blocks(sq[:]), AX_X, ALU.add).then_inc(ss_ok, 1)
                    dve.wait_ge(ss_ok, b.t + 1)
                    settle(dve, keep.passed)
                    nc.vector.scalar_tensor_tensor(out=st[:, 0], in0=st[:, 0], scalar=1.0 / P,
                                                   in1=den[:, bass.ds(b.t, 1)].rearrange("p i h -> p (i h)"),
                                                   op0=ALU.mult, op1=ALU.add).then_inc(var_ok, 1)
                    dve.wait_ge(sd_ok, b.t + 1)
                    nc.vector.reciprocal(st[:, 1], st[:, 1]).then_inc(ri_ok, 1)
                    dve.wait_ge(ri_ok, b.t + 1)
                    if b.reaches(1):
                        dve.wait_ge(tb_ok, b.t)
                    nc.vector.tensor_tensor(blocks(on[:]), blocks(ps_a[:]), wide(st[:, 1]), ALU.mult).then_inc(on_ok, 1)

                def first_lo(b):
                    dve.wait_ge(ohi_ok, b.t + 1)
                    nc.vector.tensor_tensor(o_lo[:, b.side], ps_b[:], f32(o_hi[:, b.side]), ALU.subtract).then_inc(olo_ok, 1)

                def gated(b, n):
                    at = slice(n * BANK, (n + 1) * BANK)
                    dve.wait_ge(y_ok, 2 * b.t + n + 1)
                    if b.reaches(2) and n == 0:
                        dve.wait_ge(x1_out[b.side], 16 * b.turn)
                        dve.wait_ge(sq2_ok, b.t - 1)
                    nc.vector.tensor_tensor(x1[:, b.side, at], ps_y[:, at], gate[:, at], ALU.mult).then_inc(gy_ok, 1)

                def residual(b):
                    dve.wait_ge(gy_ok, 2 * b.t + 2)
                    dve.wait_ge(x_in[b.side], 16 * b.turn + 16)
                    nc.vector.tensor_tensor(x1[:, b.side], x1[:, b.side], xr[:, b.side], ALU.add).then_inc(x1_ok, 1)

                def second_rows(b):
                    dve.wait_ge(sd2_ok, b.t + 1)
                    nc.vector.reciprocal(st2[:, 1:2], st2[:, 1:2]).then_inc(ri2_ok, 1)
                    dve.wait_ge(ri2_ok, b.t + 1)
                    if b.reaches(1):
                        dve.wait_ge(td_ok, b.t)
                    nc.vector.tensor_scalar(xn[:], x1[:, b.side], st2[:, 1:2], None, ALU.mult).then_inc(xn_ok, 1)

                def body(at):
                    if at(-1).valid():
                        gated(at(-1), 1)
                        residual(at(-1))
                        second_rows(at(-1))
                    if at(0).valid():
                        gated(at(0), 0)
                    if at(1).valid():
                        first_lo(at(1))
                    if at(2).valid():
                        head_rows(at(2))

                nc.vector.memset(ones[:], 1.0)
                for j in range(DB):
                    gate_row(2 * DB, j)
                dve.wait_ge(gate_m, DB)
                nc.vector.tensor_copy(gate[:], ps_y[:]).then_inc(gate_ok, 1)
                dve.wait_ge(den_in, 16)
                nc.vector.scalar_tensor_tensor(out=den[:], in0=den[:], scalar=EPS, in1=den[:], op0=ALU.mult,
                                               op1=ALU.mult).then_inc(den_ok, 1)
                dve.wait_ge(den_ok, 1)
                for hh in range(HEADS):
                    dve.wait_ge(wo_hi_ok, hh + 1)
                    nc.vector.scalar_tensor_tensor(out=wo_lo[:, hh], in0=wo_raw[:, hh % 2], scalar=keep.sub_gain[:],
                                                   in1=f32(wo_hi[:, hh]), op0=ALU.mult, op1=ALU.subtract
                                                   ).then_inc(wo_lo_ok, 1)
                iterations(dve, body)

            @block.tensor
            def _(pe):
                def transposes_a(b):
                    pe.wait_ge(o_in[b.side], 16 * b.turn + 16)
                    if b.reaches(1):
                        pe.wait_ge(on_ok, b.t)
                    for hh in range(HEADS):
                        mm = nc.tensor.transpose(ps_a[:, hh * P:(hh + 1) * P], ot[:, b.side, hh], keep.ident[:])
                    mm.then_inc(ta_ok, 1)

                def transposes_b(b):
                    pe.wait_ge(on_ok, b.t + 1)
                    if b.reaches(1):
                        pe.wait_ge(olo_ok, b.t)
                    for hh in range(HEADS):
                        mm = nc.tensor.transpose(ps_b[:, hh * P:(hh + 1) * P], on[:, hh * P:(hh + 1) * P], keep.mirror[:])
                    mm.then_inc(tb_ok, 1)

                def product(b, n):
                    pe.wait_ge(olo_ok, b.t + 1)
                    if b.reaches(1):
                        pe.wait_ge(gy_ok, 2 * b.t - 1 + n)
                    else:
                        pe.wait_ge(gate_ok, 1)
                        pe.wait_ge(wo_lo_ok, HEADS)
                    at = slice(n * BANK, (n + 1) * BANK)
                    for hh in range(HEADS):
                        hs = slice(hh * P, (hh + 1) * P)
                        nc.tensor.matmul(ps_y[:, at], o_hi[:, b.side, hs], wo_hi[:, hh, at], start=(hh == 0), stop=False)
                        nc.tensor.matmul(ps_y[:, at], o_hi[:, b.side, hs], wo_lo[:, hh, at], start=False, stop=False)
                        mm = nc.tensor.matmul(ps_y[:, at], o_lo[:, b.side, hs], wo_hi[:, hh, at], start=False,
                                              stop=(hh == HEADS - 1))
                    mm.then_inc(y_ok, 1)

                def transposes_d(b):
                    pe.wait_ge(xn_ok, b.t + 1)
                    if b.reaches(1):
                        pe.wait_ge(hf_ok, b.t)
                    for d in range(DB):
                        mm = nc.tensor.transpose(ps_d[:, d * P:(d + 1) * P], xn[:, d * P:(d + 1) * P], keep.ident[:])
                    mm.then_inc(td_ok, 1)

                def body(at):
                    if at(0).valid():
                        product(at(0), 0)
                    if at(1).valid():
                        transposes_b(at(1))
                    if at(2).valid():
                        transposes_a(at(2))
                    if at(0).valid():
                        product(at(0), 1)
                    if at(-1).valid():
                        transposes_d(at(-1))

                for j in range(DB):
                    pe.wait_ge(gate_d, j + 1)
                    nc.tensor.matmul(ps_y[:, j * P:(j + 1) * P], ones[:], diag[:], start=True, stop=True).then_inc(gate_m, 1)
                iterations(pe, body)


def mlp(nc, ins, keep, scr, out):
    HALVES = 2
    HT = S // HALVES
    FC = 256
    CHUNKS = F // FC
    FB = FC // P
    TG = HT // BANK
    HB = HT // P
    UB = BANK // P
    NB = D // BANK
    with ExitStack() as ctx:
        def sb(name, shape, dt=F32):
            return ctx.enter_context(nc.sbuf_tensor(name, shape, dt))

        def pb(name, shape):
            return ctx.enter_context(nc.psum_tensor(name, shape, F32))

        def sem(name):
            return ctx.enter_context(nc.semaphore(name))

        h_hi = sb("h_hi_f", [P, DB, HT], F32R)
        h_lo = sb("h_lo_f", [P, DB, HT], F32R)
        acc = sb("acc", [P, HB, D])
        w_raw = sb("wf_raw", [P, 2, DB * FC])
        w1_hi = sb("w1_hi", [P, 2, DB, FC], F32R)
        w1_lo = sb("w1_lo", [P, 2, DB, FC], F32R)
        w2_hi = sb("w2_hi", [P, 2, FB, D], F32R)
        w2_lo = sb("w2_lo", [P, 2, FB, D], F32R)
        r = sb("r", [P, 2, BANK])
        g_hi = sb("g_hi", [P, TG, FB, BANK], F32R)
        g_lo = sb("g_lo", [P, TG, FB, BANK], F32R)
        gate = sb("gate_f", [P, D])
        diag = sb("diag_f", [P, P])
        ones = sb("ones_f", [P, P])
        ps_h = [pb(f"ps_h{i}", [P, BANK]) for i in range(4)]
        ps_y = [pb(f"ps_y{i}", [P, BANK]) for i in range(4)]

        h_in = [sem(f"h_in{g}") for g in range(TG)]
        acc_in = [sem(f"acc_in{g}") for g in range(TG)]
        acc_out = [sem(f"acc_out{g}") for g in range(TG)]
        w_in = [sem(f"wf_in{i}") for i in range(2)]
        w_hi_ok = [sem(f"wfhi_ok{i}") for i in range(2)]
        w_lo_ok = [sem(f"wflo_ok{i}") for i in range(2)]
        w2g_ok = sem("w2g_ok")
        gate_d = sem("gatef_d")
        gate_m = sem("gatef_m")
        gate_ok = sem("gatef_ok")
        mh_ok = sem("mh_ok")
        r_ok = sem("r_ok")
        g_ok = sem("g_ok")
        ghi_ok = sem("ghi_ok")
        glo_ok = sem("glo_ok")
        y_ok = sem("yf_ok")
        add_ok = sem("add_ok")

        YB = UB * NB
        w1_v = ins["mlp_w1"][0].rearrange("(b p) f -> p b f", p=P)
        w2_v = ins["mlp_w2"][0].rearrange("(b p) n -> p b n", p=P)
        x1_v = scr.x1.rearrange("(t p) d -> t p d", p=P)
        out_v = out[0].rearrange("(t p) d -> t p d", p=P)
        raw = [w_raw[:, 0].rearrange("p (b f) -> p b f", b=DB), w_raw[:, 1].rearrange("p (b n) -> p b n", b=FB)]
        hi = [w1_hi, w2_hi]
        lo = [w1_lo, w2_lo]

        def rounds(eng, head, body):
            with eng.Fori(0, HALVES) as half:
                i0 = half * CHUNKS
                head(half, i0)
                with eng.Fori(0, CHUNKS // 2 - 1) as pair:
                    for e in range(2):
                        body(half, i0 + pair * 2 + e, e, False)
                body(half, i0 + (CHUNKS - 2), 0, False)
                body(half, i0 + (CHUNKS - 1), 1, True)

        with nc.Block() as block:
            @block.sync
            def _(sp):
                def load_w(i, f):
                    sp.wait_ge(w_lo_ok[0], i + 1)
                    settle(sp, keep.passed)
                    sp.dma_start(raw[0], w1_v[:, :, bass.ds(f * FC, FC)]).then_inc(w_in[0], 16)
                    sp.wait_ge(w_lo_ok[1], i + 1)
                    settle(sp, keep.passed)
                    sp.dma_start(raw[1], w2_v[:, bass.ds(f * FB, FB)]).then_inc(w_in[1], 16)

                def load_h(half, g):
                    if half:
                        sp.wait_ge(mh_ok, (half * CHUNKS - 1) * TG * FB + (g + 1) * FB)
                    at = half * HT + g * BANK
                    for to, src in ((h_hi, scr.h2_hi), (h_lo, scr.h2_lo)):
                        sp.dma_start(f32(to[:, :, g * BANK:(g + 1) * BANK]), src[:, :, at:at + BANK]).then_inc(h_in[g], 16)

                sp.sem_inc(w_lo_ok[0], 1)
                sp.sem_inc(w_lo_ok[1], 1)
                sp.sem_inc(g_ok, 4)
                sp.sem_inc(glo_ok, 2)
                sp.sem_inc(add_ok, 4)
                sp.sem_inc(y_ok, 2 * YB)
                for half in range(HALVES):
                    load_h(half, 0)
                    load_w(half * CHUNKS, 0)
                    load_h(half, 1)
                    for t in range(HB):
                        if half:
                            sp.wait_ge(acc_out[t // UB], UB * 16)
                        sp.dma_start(acc[:, t], x1_v[half * HB + t]).then_inc(acc_in[t // UB], 16)
                    with sp.Fori(1, CHUNKS) as f:
                        load_w(half * CHUNKS + f, f)
                    for t in range(HB):
                        unit = ((half + 1) * CHUNKS - 1) * TG + t // UB
                        sp.wait_ge(add_ok, unit * YB + (t % UB + 1) * NB + 4)
                        sp.dma_start(out_v[half * HB + t], acc[:, t]).then_inc(acc_out[t // UB], 16)
                for g in range(TG):
                    sp.wait_ge(acc_out[g], UB * 16 * HALVES)

            @block.gpsimd
            def _(pool):
                def w2_gate(i):
                    pool.wait_ge(w_in[1], i * 16 + 16)
                    for b in range(FB):
                        g = nc.gpsimd.tensor_tensor(raw[1][:, b], raw[1][:, b], gate[:], ALU.mult)
                    g.then_inc(w2g_ok, 1)

                def unit_lo(i, g):
                    for fb in range(FB):
                        b = (i * TG + g) * FB + fb
                        pool.wait_ge(ghi_ok, b + 1)
                        nc.gpsimd.tensor_tensor(g_lo[:, g, fb], r[:, fb], f32(g_hi[:, g, fb]), ALU.subtract).then_inc(glo_ok, 1)

                def head(half, i):
                    w2_gate(i)
                    unit_lo(i, 0)

                def body(half, i, parity, last):
                    if not last:
                        w2_gate(i + 1)
                    unit_lo(i, 1)
                    if not last:
                        unit_lo(i + 1, 0)

                pool.wait_ge(gate_ok, NB)
                rounds(pool, head, body)

            @block.scalar
            def _(act):
                def split(i, parity, more=0):
                    act.wait_ge(y_ok, i * (TG * YB) + more)
                    for m in range(2):
                        if m == 0:
                            act.wait_ge(w_in[0], i * 16 + 16)
                        else:
                            act.wait_ge(w2g_ok, i + 1)
                        nc.scalar.copy(hi[m][:, parity], raw[m]).then_inc(w_hi_ok[m], 1)

                def unit(i, g):
                    for fb in range(FB):
                        b = (i * TG + g) * FB + fb
                        act.wait_ge(mh_ok, b + 1)
                        act.wait_ge(glo_ok, b + 1)
                        nc.scalar.activation(r[:, fb], ps_h[g * FB + fb][:], ACT.Relu).then_inc(r_ok, 1)
                        act.wait_ge(g_ok, b + 5)
                        act.wait_ge(y_ok, (i * TG + g + 1) * YB)
                        nc.scalar.copy(g_hi[:, g, fb], r[:, fb]).then_inc(ghi_ok, 1)

                def head(half, i):
                    split(i, 0, more=1)
                    unit(i, 0)

                def body(half, i, parity, last):
                    if not last:
                        split(i + 1, 1 - parity)
                    unit(i, 1)
                    if not last:
                        unit(i + 1, 0)

                rounds(act, head, body)

            @block.vector
            def _(dve):
                def split(i, parity):
                    for m in range(2):
                        dve.wait_ge(w_hi_ok[m], i + 1)
                        nc.vector.tensor_tensor(lo[m][:, parity], raw[m], f32(hi[m][:, parity]), ALU.subtract).then_inc(
                            w_lo_ok[m], 1)

                def squares(i, g):
                    for fb in range(FB):
                        b = (i * TG + g) * FB + fb
                        dve.wait_ge(r_ok, b + 1)
                        nc.vector.scalar_tensor_tensor(out=r[:, fb], in0=ps_h[g * FB + fb][:], scalar=0.0, in1=r[:, fb],
                                                       op0=ALU.max, op1=ALU.mult).then_inc(g_ok, 1)

                def adds(half, i, g):
                    for k in range(YB):
                        n = (i * TG + g) * YB + k
                        t = g * UB + k // NB
                        at = slice((k % NB) * BANK, (k % NB + 1) * BANK)
                        if k == 0:
                            dve.wait_ge(acc_in[g], half * (UB * 16) + UB * 16)
                        dve.wait_ge(y_ok, n + 2 * YB + 1)
                        nc.vector.tensor_tensor(acc[:, t, at], ps_y[k % 4][:], acc[:, t, at], ALU.add).then_inc(add_ok, 1)

                def head(half, i):
                    split(i, 0)
                    squares(i, 0)

                def body(half, i, parity, last):
                    if not last:
                        split(i + 1, 1 - parity)
                    squares(i, 1)
                    adds(half, i, 0)
                    if not last:
                        squares(i + 1, 0)
                    adds(half, i, 1)

                nc.vector.memset(ones[:], 1.0)
                for j in range(DB):
                    if j:
                        dve.wait_ge(gate_m, j)
                    nc.vector.tensor_scalar(diag[:], keep.ident[:], keep.mod[:, 5 * DB + j:5 * DB + j + 1], None,
                                            ALU.mult).then_inc(gate_d, 1)
                dve.wait_ge(gate_m, DB)
                for n in range(NB):
                    nc.vector.tensor_copy(gate[:, n * BANK:(n + 1) * BANK], ps_y[n][:]).then_inc(gate_ok, 1)
                rounds(dve, head, body)

            @block.tensor
            def _(pe):
                def hidden(half, i, g, parity):
                    if g == 0:
                        pe.wait_ge(w_lo_ok[0], i + 2)
                    pe.wait_ge(h_in[g], half * 32 + 32)
                    at = slice(g * BANK, (g + 1) * BANK)
                    for fb in range(FB):
                        b = (i * TG + g) * FB + fb
                        pe.wait_ge(g_ok, b + 1)
                        ps = ps_h[g * FB + fb][:]
                        fs = slice(fb * P, (fb + 1) * P)
                        for d in range(DB):
                            nc.tensor.matmul(ps, w1_hi[:, parity, d, fs], h_hi[:, d, at], start=(d == 0), stop=False)
                            nc.tensor.matmul(ps, w1_hi[:, parity, d, fs], h_lo[:, d, at], start=False, stop=False)
                            mm = nc.tensor.matmul(ps, w1_lo[:, parity, d, fs], h_hi[:, d, at], start=False, stop=(d == DB - 1))
                        mm.then_inc(mh_ok, 1)

                def products(i, g, parity):
                    if g == 0:
                        pe.wait_ge(w_lo_ok[1], i + 2)
                    pe.wait_ge(glo_ok, (i * TG + g) * FB + FB + 2)
                    for k in range(YB):
                        n = (i * TG + g) * YB + k
                        pe.wait_ge(add_ok, n + 1)
                        ts = slice((k // NB) * P, (k // NB + 1) * P)
                        at = slice((k % NB) * BANK, (k % NB + 1) * BANK)
                        for fb in range(FB):
                            nc.tensor.matmul(ps_y[k % 4][:], g_hi[:, g, fb, ts], w2_hi[:, parity, fb, at], start=(fb == 0), stop=False)
                            nc.tensor.matmul(ps_y[k % 4][:], g_hi[:, g, fb, ts], w2_lo[:, parity, fb, at], start=False, stop=False)
                            mm = nc.tensor.matmul(ps_y[k % 4][:], g_lo[:, g, fb, ts], w2_hi[:, parity, fb, at], start=False,
                                                  stop=(fb == FB - 1))
                        mm.then_inc(y_ok, 1)

                def head(half, i):
                    hidden(half, i, 0, 0)

                def body(half, i, parity, last):
                    hidden(half, i, 1, parity)
                    products(i, 0, parity)
                    if not last:
                        hidden(half, i + 1, 0, 1 - parity)
                    products(i, 1, parity)

                for j in range(DB):
                    pe.wait_ge(gate_d, j + 1)
                    nc.tensor.matmul(ps_y[j // 4][:, (j % 4) * P:(j % 4 + 1) * P], ones[:], diag[:], start=True,
                                     stop=True).then_inc(gate_m, 1)
                pe.wait_ge(gate_ok, NB)
                rounds(pe, head, body)


def decoder_layer(nc, ins, out):
    scr = Scratch(nc)
    with ExitStack() as ctx:
        keep = Persist(nc, ctx)
        with ExitStack() as both:
            over = Handover(nc, both)
            modulate(nc, ins, keep, scr, over)
            project(nc, ins, keep, scr, over)
        attend(nc, keep, scr)
        mix(nc, ins, keep, scr)
        mlp(nc, ins, keep, scr, out)


_INS = ["x", "c", "rel_bias", "w_ada", "b_ada", "norm_mix", "norm_mlp", "mlp_w1", "mlp_w2", "da_w_qkv", "da_w_o",
        "da_q_gain", "da_k_gain", "da_lam_q1", "da_lam_k1", "da_lam_q2", "da_lam_k2", "da_sub_gain"]


def kernel(**inputs):
    import concourse.bacc as bacc
    from concourse.bass_utils import run_bass_kernel_spmd

    nc = bacc.Bacc("TRN2", target_bir_lowering=False, num_devices=1)
    arrays, ins = {}, {}
    for name in _INS:
        a = np.ascontiguousarray(inputs[name])
        arrays[f"in_{name}"] = a
        ins[name] = nc.dram_tensor(f"in_{name}", a.shape, mybir.dt.from_np(a.dtype), kind="ExternalInput").ap()
    table = bucket_table()
    arrays["in_buckets"] = table
    ins["buckets"] = nc.dram_tensor("in_buckets", table.shape, F32, kind="ExternalInput").ap()
    out = nc.dram_tensor("out", (1, S, D), F32, kind="ExternalOutput").ap()
    decoder_layer(nc, ins, out)
    r = run_bass_kernel_spmd(nc, [arrays], core_ids=[0])
    return r.results[0]["out"]
```

```python
import math
from contextlib import ExitStack

import concourse.bass as bass
import numpy as np
from concourse import mybir

F32 = mybir.dt.float32
F32R = mybir.dt.float32r
ALU = mybir.AluOpType
ACT = mybir.ActivationFunctionType
AX_X = mybir.AxisListType.X

P = 128
D = 1024
S = 2048
F = 4 * D
DB = D // P
TB = S // P
HD = 64
HEADS = D // (2 * HD)
BANK = 512
SUPER = S // BANK
EPS = 1e-6
LAMBDA_INIT = 0.8 - 0.6 * math.exp(-0.3 * 0)
BUCKETS = 32
REL_MAX = 2048
MASK = 1e30
DIAG = S + P
FAR = 3.0e38


def bucket_table():
    dist = S - 1 - np.arange(DIAG)
    n = np.maximum(dist, 0)
    exact = BUCKETS // 2
    nf = np.maximum(n, exact).astype(np.float32)
    steps = np.log(nf / np.float32(exact)) / np.float32(math.log(REL_MAX / exact)) * np.float32(BUCKETS - exact)
    large = np.minimum(exact + steps.astype(np.int32), BUCKETS - 1)
    bucket = np.where(n < exact, n, large)
    bucket = np.where(dist < 0, BUCKETS, bucket)
    return (np.arange(BUCKETS + 1)[:, None] == bucket[None, :]).astype(np.float32)


class Scratch:

    def __init__(self, nc):
        def dram(name, shape):
            return nc.dram_tensor(name, shape, F32, kind="Internal").ap()

        self.bias_row = dram("bias_row", (2 * HEADS, DIAG))
        self.qk_hi = dram("qk_hi", (2 * HEADS, P, S))
        self.qk_lo = dram("qk_lo", (2 * HEADS, P, S))
        self.v_hi = dram("v_hi", (HEADS, P, TB, P))
        self.v_lo = dram("v_lo", (HEADS, P, TB, P))
        self.o_t = dram("o_t", (HEADS, P, S))
        self.l_sum = dram("l_sum", (P, TB, HEADS))
        self.x1 = dram("x1", (S, D))
        self.h2_hi = dram("h2_hi", (P, DB, S))
        self.h2_lo = dram("h2_lo", (P, DB, S))


def f32(ap):
    return ap.bitcast(F32)


def settle(eng, passed):
    eng.sem_inc(passed, 1)


class Persist:

    def __init__(self, nc, ctx):
        def sb(name, shape, dt=F32):
            return ctx.enter_context(nc.sbuf_tensor(name, shape, dt))

        self.ident = sb("ident", [P, P])
        self.mirror = sb("mirror", [P, P])
        self.mod = sb("mod", [P, 6 * DB])
        self.affine = sb("affine", [P, 2, DB])
        self.c_silu = sb("c_silu", [P, DB])
        self.one = sb("one", [P, 1])
        self.b_ada = sb("b_ada", [P, 6 * DB])
        self.norm_gain = sb("norm_gain", [P, 2, DB])
        self.neg_lambda = sb("neg_lambda", [P, 1])
        self.qk_gain = sb("qk_gain", [P, 4])
        self.sub_gain = sb("sub_gain", [P, 1])
        self.eps = sb("eps", [P, 1])
        self.passed = ctx.enter_context(nc.semaphore("passed"))


class Handover:

    def __init__(self, nc, ctx):
        self.ht_hi = ctx.enter_context(nc.sbuf_tensor("ht_hi", [P, DB, S], F32R))
        self.ht_lo = ctx.enter_context(nc.sbuf_tensor("ht_lo", [P, DB, S], F32R))
        self.w_raw = ctx.enter_context(nc.sbuf_tensor("w_raw", [P, DB, BANK], F32))
        self.w_in = [ctx.enter_context(nc.semaphore(f"w_in{b}")) for b in range(DB)]


def weighted_rows(nc, dve, keep, acc, w, acc_ok, n, blocks=DB):
    for b in range(blocks):
        c = keep.c_silu[:, b:b + 1]
        if b == 0:
            a = nc.vector.tensor_scalar(acc, w[:, b], c, None, ALU.mult)
        else:
            dve.wait_ge(acc_ok, n * blocks + b)
            a = nc.vector.scalar_tensor_tensor(out=acc, in0=w[:, b], scalar=c, in1=acc, op0=ALU.mult, op1=ALU.add)
        a.then_inc(acc_ok, 1)


def load_qkv_weights(sp, ins, over, cols):
    w_v = ins["da_w_qkv"][0].rearrange("(b p) n -> p b n", p=P)
    for b in range(DB):
        sp.dma_start(over.w_raw[:, b], w_v[:, b, cols]).then_inc(over.w_in[b], 16)


def modulate(nc, ins, keep, scr, over):
    ADA_N = 256
    CHUNKS = 2 * D // ADA_N
    CJ = ADA_N // P
    SUMMED = 5
    HI_BY_DVE = (1, 2, 3, 5, 6, 7)
    ROWS_AT = ((0, 1), (2, 3), (4,), ())
    assert SUPER == len(ROWS_AT) and sum(map(len, ROWS_AT)) == -(-DIAG // BANK)
    ht_hi, ht_lo = over.ht_hi, over.ht_lo
    with ExitStack() as ctx:
        def sb(name, shape, dt=F32):
            return ctx.enter_context(nc.sbuf_tensor(name, shape, dt))

        def pb(name, shape):
            return ctx.enter_context(nc.psum_tensor(name, shape, F32))

        def sem(name):
            return ctx.enter_context(nc.semaphore(name))

        ada = sb("ada", [P, 2, DB, ADA_N])
        acc = sb("acc_a", [P, 2, ADA_N])
        xg = sb("xg", [P, 4, D])
        sq = sb("sq_a", [P, D])
        tmp = sb("tmp_a", [P, 2, BANK])
        ccol = sb("ccol", [P, 2, DB])
        lam = sb("lam", [P, 4, HD])
        lam_s = sb("lam_s", [P, 4])
        stat = sb("stat_a", [P, 2, TB])
        rel = sb("rel", [BUCKETS + 1, 2 * HEADS])
        hot = sb("hot", [BUCKETS + 1, DIAG])
        row = sb("row", [2 * HEADS, DIAG])
        ps_mod = pb("ps_mod", [P, 2 * DB])
        ps_row = [pb(f"ps_row{i}", [2 * HEADS, BANK]) for i in range(2)]
        ps_t = [pb(f"ps_t{i}", [P, BANK]) for i in range(4)]

        small_in = sem("small_in")
        ada_in = [sem(f"ada_in{i}") for i in range(2)]
        x_in = [sem(f"x_in{i}") for i in range(2)]
        ident_ok = sem("ident_ok")
        pool_ok = sem("pool_ok")
        silu_a = sem("silu_a")
        silu_d = sem("silu_d")
        acc_ok = sem("acc_a_ok")
        mod_part = sem("mod_part")
        mod_ok_d = sem("mod_ok_d")
        mod_ok = sem("mod_ok")
        lam_d = sem("lam_d")
        lam_a = sem("lam_a")
        rel_ok = sem("rel_ok")
        row_mm = sem("row_mm")
        row_ok = sem("row_ok")
        row_out = sem("row_out")
        x_sq = sem("x_sq")
        x_sd = sem("x_sd")
        x_ri = sem("x_ri")
        x_n = sem("x_n")
        x_t = sem("x_t")
        h_f = sem("h_f")
        h_hi = sem("h_hi")
        h_lo = sem("h_lo")
        SMALL = 17

        ada_v = ins["w_ada"][0].rearrange("(b p) n -> p b n", p=P)
        x_v = ins["x"][0].rearrange("(t p) d -> p t d", p=P)
        x_of = [xg[:], ada[:].rearrange("p i (k b) n -> p (i k) (b n)", k=2)]

        with nc.Block() as block:
            @block.sync
            def _(sp):
                with nc.allow_non_contiguous_dma(reason="columns of small vectors"):
                    col = lambda a: a.rearrange("(b p) -> p b", p=P)
                    loads = [(ccol[:, 0, :], col(ins["c"][0])), (keep.b_ada[:], col(ins["b_ada"][0])),
                             (keep.norm_gain[:, 0, :], col(ins["norm_mix"][0])), (keep.norm_gain[:, 1, :], col(ins["norm_mlp"][0])),
                             (keep.sub_gain[:], col(ins["da_sub_gain"][0]))]
                    for half in range(2):
                        at = slice(half * HD, half * HD + HD)
                        for g, name in ((0, "da_q_gain"), (1, "da_q_gain"), (2, "da_k_gain"), (3, "da_k_gain")):
                            loads.append((keep.qk_gain[at, g:g + 1], ins[name][0].rearrange("(p b) -> p b", b=1)))
                    for n, name in enumerate(("da_lam_q1", "da_lam_k1", "da_lam_q2", "da_lam_k2")):
                        loads.append((lam[:, n, :], ins[name].to_broadcast([P, HD])))
                    assert len(loads) == SMALL
                    for to, src in loads:
                        sp.dma_start(to, src).then_inc(small_in, 16)
                sp.dma_start(rel[0:BUCKETS, :], ins["rel_bias"]).then_inc(small_in, 16)
                sp.dma_start(hot[:], ins["buckets"]).then_inc(small_in, 16)
                for n in range(CHUNKS):
                    if n >= 2:
                        sp.wait_ge(mod_part, n - 1)
                    sp.dma_start(ada[:, n % 2], ada_v[:, :, n * ADA_N:(n + 1) * ADA_N]).then_inc(ada_in[n % 2], 16)
                load_qkv_weights(sp, ins, over, slice(0, BANK))
                sp.wait_ge(row_ok, -(-DIAG // BANK))
                sp.dma_start(scr.bias_row, row[:]).then_inc(row_out, 16)
                sp.wait_ge(row_out, 16)

            @block.gpsimd
            def _(pool):
                nc.gpsimd.memset(keep.ident[:], 0.0).then_inc(pool_ok, 1)
                pool.wait_ge(pool_ok, 1)
                nc.gpsimd.affine_select(out=keep.ident[:], in_=keep.ident[:], compare_op=ALU.not_equal, fill=1.0,
                                        base=0, pattern=[[-1, P]], channel_multiplier=1).then_inc(ident_ok, 1)
                nc.gpsimd.memset(keep.mirror[:], 0.0).then_inc(pool_ok, 1)
                pool.wait_ge(pool_ok, 2)
                nc.gpsimd.affine_select(out=keep.mirror[:], in_=keep.mirror[:], compare_op=ALU.not_equal, fill=1.0,
                                        base=1 - P, pattern=[[1, P]], channel_multiplier=1)

            @block.scalar
            def _(act):
                def load_x(g):
                    for t in range(4):
                        act.dma_start(x_of[g % 2][:, t], x_v[:, 4 * g + t]).then_inc(x_in[g % 2], 16)

                def stats(g):
                    act.wait_ge(x_in[g % 2], 64 * (g // 2 + 1))
                    for t in range(4 * g, 4 * g + 4):
                        if t:
                            act.wait_ge(x_sq, t)
                        nc.scalar.activation(sq[:], x_of[g % 2][:, t % 4], ACT.Square,
                                             accum_out=stat[:, 0, t:t + 1]).then_inc(x_sq, 1)
                    act.wait_ge(x_sq, 4 * g + 4)
                    nc.scalar.activation(stat[:, 1, 4 * g:4 * g + 4], stat[:, 0, 4 * g:4 * g + 4], ACT.Sqrt,
                                         bias=keep.eps[:], scale=1.0 / D).then_inc(x_sd, 1)

                load_x(0)
                act.wait_ge(small_in, 16 * (SMALL + 2))
                nc.scalar.activation(ccol[:, 1, :], ccol[:, 0, :], ACT.Exp, scale=-1.0).then_inc(silu_a, 1)
                act.wait_ge(lam_d, 2)
                nc.scalar.activation(lam_s[:, 2:4], lam_s[:, 0:2], ACT.Exp).then_inc(lam_a, 1)
                act.wait_ge(silu_d, 1)
                stats(0)
                act.wait_ge(mod_part, CHUNKS)
                load_x(1)
                act.wait_ge(mod_ok, 1)
                for g in range(SUPER):
                    for d in range(DB):
                        if d == DB // 2 and g + 1 < SUPER:
                            stats(g + 1)
                        n = DB * g + d
                        act.wait_ge(x_t, n + 1)
                        if d not in HI_BY_DVE:
                            nc.scalar.activation(ht_hi[:, d, g * BANK:(g + 1) * BANK], ps_t[n % 4][:], ACT.Identity,
                                                 bias=keep.mod[:, d:d + 1], scale=keep.affine[:, 0, d:d + 1])
                        if n >= 2:
                            act.wait_ge(h_lo, n - 1)
                        nc.scalar.activation(tmp[:, n % 2], ps_t[n % 4][:], ACT.Identity,
                                             bias=keep.mod[:, d:d + 1],
                                             scale=keep.affine[:, 0, d:d + 1]).then_inc(h_f, 1)
                    for n in ROWS_AT[g]:
                        w = min(BANK, DIAG - n * BANK)
                        act.wait_ge(row_mm, n + 1)
                        nc.scalar.copy(row[:, n * BANK:n * BANK + w], ps_row[n % 2][:, 0:w]).then_inc(row_ok, 1)
                    if g + 2 < SUPER:
                        load_x(g + 2)

            @block.vector
            def _(dve):
                nc.vector.memset(keep.eps[:], EPS)
                nc.vector.memset(keep.one[:], 1.0)
                nc.vector.memset(rel[BUCKETS:BUCKETS + 1, :], MASK).then_inc(silu_d, 1)
                dve.wait_ge(small_in, 16 * (SMALL + 2))
                nc.vector.tensor_scalar(rel[0:BUCKETS, :], rel[0:BUCKETS, :], -1.0, None, ALU.mult).then_inc(rel_ok, 1)
                for n in range(2):
                    nc.vector.tensor_tensor_reduce(lam[:, 2 * n], lam[:, 2 * n], lam[:, 2 * n + 1], 1.0, 0.0,
                                                   ALU.mult, ALU.add, lam_s[:, n:n + 1]).then_inc(lam_d, 1)
                nc.vector.tensor_scalar(keep.qk_gain[:, 0:2], keep.qk_gain[:, 0:2], -(HD ** -0.5), None, ALU.mult)
                nc.vector.tensor_scalar(keep.sub_gain[:], keep.sub_gain[:], 1.0 - LAMBDA_INIT, None, ALU.mult)
                dve.wait_ge(silu_a, 1)
                nc.vector.tensor_scalar(ccol[:, 1, :], ccol[:, 1, :], 1.0, None, ALU.add).then_inc(silu_d, 1)
                dve.wait_ge(silu_d, 2)
                nc.vector.reciprocal(ccol[:, 1, :], ccol[:, 1, :]).then_inc(silu_d, 1)
                dve.wait_ge(silu_d, 3)
                nc.vector.tensor_tensor(keep.c_silu[:], ccol[:, 0, :], ccol[:, 1, :], ALU.mult).then_inc(silu_d, 1)
                dve.wait_ge(lam_a, 1)
                nc.vector.scalar_tensor_tensor(out=keep.neg_lambda[:], in0=lam_s[:, 3:4], scalar=-LAMBDA_INIT,
                                               in1=lam_s[:, 2:3], op0=ALU.add, op1=ALU.subtract)
                def scale_rows(g):
                    dve.wait_ge(x_sd, g + 1)
                    nc.vector.reciprocal(stat[:, 1, 4 * g:4 * g + 4], stat[:, 1, 4 * g:4 * g + 4]).then_inc(x_ri, 1)
                    dve.wait_ge(x_ri, g + 1)
                    for t in range(4):
                        x = x_of[g % 2][:, t]
                        nc.vector.tensor_scalar(x, x, stat[:, 1, 4 * g + t:4 * g + t + 1], None, ALU.mult).then_inc(x_n, 1)

                dve.wait_ge(silu_d, 4)
                for n in range(CHUNKS):
                    if n == CHUNKS // 2:
                        scale_rows(0)
                    dve.wait_ge(ada_in[n % 2], 16 * (n // 2 + 1))
                    if n >= 2:
                        dve.wait_ge(mod_part, n - 1)
                    weighted_rows(nc, dve, keep, acc[:, n % 2], ada[:, n % 2], acc_ok, n, SUMMED)
                dve.wait_ge(mod_part, CHUNKS)
                nc.vector.tensor_tensor(keep.mod[:, 0:2 * DB], ps_mod[:], keep.b_ada[:, 0:2 * DB], ALU.add).then_inc(mod_ok_d, 1)
                dve.wait_ge(mod_ok_d, 1)
                nc.vector.scalar_tensor_tensor(out=keep.affine[:, 0, :], in0=keep.mod[:, DB:2 * DB], scalar=1.0,
                                               in1=keep.norm_gain[:, 0, :], op0=ALU.add, op1=ALU.mult).then_inc(mod_ok, 1)
                for g in range(SUPER):
                    for d in range(DB):
                        if d == DB // 2 and g + 1 < SUPER:
                            scale_rows(g + 1)
                        n = DB * g + d
                        at = slice(g * BANK, (g + 1) * BANK)
                        dve.wait_ge(h_f, n + 1)
                        if d in HI_BY_DVE:
                            nc.vector.tensor_copy(ht_hi[:, d, at], tmp[:, n % 2]).then_inc(h_hi, 1)
                            dve.wait_ge(h_hi, g * len(HI_BY_DVE) + HI_BY_DVE.index(d) + 1)
                        nc.vector.tensor_tensor(ht_lo[:, d, at], tmp[:, n % 2], f32(ht_hi[:, d, at]),
                                                ALU.subtract).then_inc(h_lo, 1)

            @block.tensor
            def _(pe):
                def ada_chunk(n):
                    pe.wait_ge(ada_in[n % 2], 16 * (n // 2 + 1))
                    for j in range(CJ):
                        out, cols = ps_mod[:, n * CJ + j:n * CJ + j + 1], slice(j * P, (j + 1) * P)
                        for b in range(SUMMED, DB):
                            nc.tensor.matmul(out, ada[:, n % 2, b, cols], keep.c_silu[:, b:b + 1], start=(b == SUMMED), stop=False)
                        if j == 0:
                            pe.wait_ge(acc_ok, (n + 1) * SUMMED)
                        mm = nc.tensor.matmul(out, acc[:, n % 2, cols], keep.one[:], start=False, stop=True)
                    mm.then_inc(mod_part, 1)

                def transposes(g):
                    pe.wait_ge(x_n, 4 * g + 4)
                    for d in range(DB):
                        n = DB * g + d
                        if n >= 4:
                            pe.wait_ge(h_f, n - 3)
                        for t in range(4):
                            mm = nc.tensor.transpose(ps_t[n % 4][:, t * P:(t + 1) * P], x_of[g % 2][:, t, d * P:(d + 1) * P],
                                                     keep.ident[:])
                        mm.then_inc(x_t, 1)

                pe.wait_ge(silu_d, 4)
                for n in range(CHUNKS):
                    ada_chunk(n)
                pe.wait_ge(ident_ok, 1)
                for g in range(SUPER):
                    transposes(g)
                    for n in ROWS_AT[g]:
                        w = min(BANK, DIAG - n * BANK)
                        if n == 0:
                            pe.wait_ge(rel_ok, 1)
                        if n >= 2:
                            pe.wait_ge(row_ok, n - 1)
                        nc.tensor.matmul(ps_row[n % 2][:, 0:w], rel[:], hot[:, n * BANK:n * BANK + w], start=True,
                                         stop=True).then_inc(row_mm, 1)


def project(nc, ins, keep, scr, over):
    ht_hi, ht_lo, w_raw, w_in = over.ht_hi, over.ht_lo, over.w_raw, over.w_in
    ADA0 = 2 * DB
    with ExitStack() as ctx:
        def sb(name, shape, dt=F32):
            return ctx.enter_context(nc.sbuf_tensor(name, shape, dt))

        def pb(name, shape):
            return ctx.enter_context(nc.psum_tensor(name, shape, F32))

        def sem(name):
            return ctx.enter_context(nc.semaphore(name))

        ada = sb("ada_b", [P, 2, DB, P])
        w_hi = sb("w_hi", [P, DB, BANK], F32R)
        w_lo = sb("w_lo", [P, DB, BANK], F32R)
        sq = sb("sq_b", [P, 2, BANK])
        st = sb("st_b", [P, 2, 2, 8])
        qn = sb("qn", [P, 2, BANK])
        qt = sb("qt", [P, 2, BANK])
        p_hi = sb("p_hi", [P, 2, BANK], F32R)
        p_lo = sb("p_lo", [P, 2, BANK], F32R)
        ps = [pb(f"ps_p{i}", [P, BANK]) for i in range(4)]
        pst = [pb(f"ps_q{i}", [P, BANK]) for i in range(2)]
        ps_mod = pb("ps_mod_b", [P, 4 * DB])
        acc = sb("acc_b", [P, 2, P])

        ada_in = [sem(f"adab_in{i}") for i in range(2)]
        acc_ok = sem("acc_b_ok")
        ada_part = sem("ada_part")
        mod_ok = sem("modb_ok")
        w_hi_ok = sem("w_hi_ok")
        w_lo_ok = sem("w_lo_ok")
        w_free = sem("w_free")
        mm_ok = sem("mm_ok")
        sq_ok = sem("sq_ok")
        ss_ok = sem("ss_ok")
        sd_ok = sem("sd_ok")
        ri_ok = sem("ri_ok")
        ps_free = sem("ps_free")
        t_ok = sem("t_ok")
        qt_ok = sem("qt_ok")
        hi_ok = sem("hi_ok")
        lo_ok = sem("lo_ok")
        v_hi_ok = sem("v_hi_ok")
        stored = [sem(f"stored{i}") for i in range(2)]

        QK, V = 4, 2
        ada_v = ins["w_ada"][0].rearrange("(b p) n -> p b n", p=P)
        assert V * TB == 4 * DB
        qkh = scr.qk_hi.rearrange("i p s -> p i s")
        qkl = scr.qk_lo.rearrange("i p s -> p i s")
        vh = scr.v_hi.rearrange("h p t e -> p h t e")
        vl = scr.v_lo.rearrange("h p t e -> p h t e")

        with nc.Block() as block:
            def split_hi(act, c, first=False):
                for b in range(DB):
                    act.wait_ge(w_in[b], c * 16 + 16)
                    if not first and b < DB - 1:
                        act.wait_ge(w_free, (c - 1) * (DB - 1) + b + 1)
                    elif not first:
                        act.wait_ge(mm_ok, c * TB)
                    nc.scalar.copy(w_hi[:, b], w_raw[:, b]).then_inc(w_hi_ok, 1)

            def split_lo(dve, c):
                for b in range(DB):
                    dve.wait_ge(w_hi_ok, c * DB + b + 1)
                    nc.vector.tensor_tensor(w_lo[:, b], w_raw[:, b], f32(w_hi[:, b]),
                                            ALU.subtract).then_inc(w_lo_ok, 1)

            heads = lambda a: f32(a).rearrange("p (h n) -> p h n", h=4)

            @block.sync
            def _(sp):
                def load_ada(j):
                    if j >= 2:
                        sp.wait_ge(acc_ok, (j - 1) * DB)
                    sp.dma_start(ada[:, j % 2], ada_v[:, :, (ADA0 + j) * P:(ADA0 + j + 1) * P]).then_inc(ada_in[j % 2], 16)

                def load_next(c):
                    sp.wait_ge(w_hi_ok, c * DB + DB)
                    sp.wait_ge(w_lo_ok, c * DB + DB)
                    settle(sp, keep.passed)
                    load_qkv_weights(sp, ins, over, bass.ds((c + 1) * BANK, BANK))

                sp.sem_inc(ps_free, 4)
                sp.sem_inc(t_ok, 2)
                sp.sem_inc(qt_ok, 2)
                sp.sem_inc(lo_ok, 2)
                for parity in range(2):
                    sp.sem_inc(stored[parity], 32)
                for j in range(2):
                    load_ada(j)
                with sp.Fori(0, QK) as c:
                    load_next(c)
                    for t in range(TB):
                        sp.wait_ge(hi_ok, c * TB + t + 1)
                        settle(sp, keep.passed)
                        sp.dma_start(qkh[:, bass.ds(c * 4, 4), t * P:(t + 1) * P], heads(p_hi[:, t % 2])).then_inc(
                            stored[t % 2], 16)
                        sp.wait_ge(lo_ok, c * TB + t + 3)
                        settle(sp, keep.passed)
                        sp.dma_start(qkl[:, bass.ds(c * 4, 4), t * P:(t + 1) * P], heads(p_lo[:, t % 2])).then_inc(
                            stored[t % 2], 16)
                for v in range(V):
                    if v < V - 1:
                        load_next(QK + v)
                    for t in range(TB):
                        sp.wait_ge(v_hi_ok, v * TB + t + 1)
                        sp.dma_start(vh[:, 4 * v:4 * v + 4, t], heads(p_hi[:, t % 2])).then_inc(stored[t % 2], 16)
                        sp.wait_ge(ps_free, (QK + v) * TB + t + 5)
                        sp.dma_start(vl[:, 4 * v:4 * v + 4, t], heads(p_lo[:, t % 2])).then_inc(stored[t % 2], 16)
                        if v * TB + t + 2 < V * TB:
                            load_ada(v * TB + t + 2)
                for parity in range(2):
                    sp.wait_ge(stored[parity], 32 * (1 + (QK + V) * TB // 2))

            @block.gpsimd
            def _(pool):
                with pool.Fori(0, QK) as c:
                    for t in range(TB):
                        n = c * TB + t
                        pool.wait_ge(qt_ok, n + 3)
                        pool.wait_ge(stored[t % 2], (c * (TB // 2) + t // 2 + 1) * 32)
                        settle(pool, keep.passed)
                        nc.gpsimd.tensor_copy(p_hi[:, t % 2], qt[:, t % 2]).then_inc(hi_ok, 1)
                        pool.wait_ge(hi_ok, n + 1)
                        nc.gpsimd.tensor_tensor(p_lo[:, t % 2], qt[:, t % 2], f32(p_hi[:, t % 2]),
                                                ALU.subtract).then_inc(lo_ok, 1)

            @block.scalar
            def _(act):
                split_hi(act, 0, first=True)
                with act.Fori(0, QK) as c:
                    for t in range(TB):
                        n = c * TB + t
                        act.wait_ge(mm_ok, n + 1)
                        nc.scalar.activation(sq[:, t % 2], ps[t % 4][:], ACT.Square).then_inc(sq_ok, 1)
                        act.wait_ge(ss_ok, n + 1)
                        nc.scalar.activation(st[:, t % 2, 1], st[:, t % 2, 0], ACT.Sqrt, bias=keep.eps[:],
                                             scale=1.0 / HD).then_inc(sd_ok, 1)
                        if t == TB - 2:
                            split_hi(act, c + 1)
                        act.wait_ge(t_ok, n + 3)
                        act.wait_ge(lo_ok, n + 1)
                        settle(act, keep.passed)
                        nc.scalar.activation(qt[:, t % 2], pst[t % 2][:], ACT.Copy,
                                             scale=keep.qk_gain[:, bass.ds(c, 1)]).then_inc(qt_ok, 1)
                for v in range(V):
                    for t in range(TB):
                        if v < V - 1 and t == TB - 1:
                            split_hi(act, QK + v + 1)
                        act.wait_ge(mm_ok, (QK + v) * TB + t + 1)
                        act.wait_ge(stored[t % 2], 32 * (QK * TB // 2 + (v * TB + t) // 2 + 1))
                        nc.scalar.copy(p_hi[:, t % 2], ps[t % 4][:]).then_inc(v_hi_ok, 1)

            @block.vector
            def _(dve):
                split_lo(dve, 0)
                with dve.Fori(0, QK) as c:
                    for t in range(TB):
                        n = c * TB + t
                        if t == TB - 1:
                            split_lo(dve, c + 1)
                        dve.wait_ge(sq_ok, n + 1)
                        nc.vector.tensor_reduce(st[:, t % 2, 0], sq[:, t % 2].rearrange("p (g d) -> p g d", d=HD), AX_X,
                                                ALU.add).then_inc(ss_ok, 1)
                        dve.wait_ge(sd_ok, n + 1)
                        nc.vector.reciprocal(st[:, t % 2, 1], st[:, t % 2, 1]).then_inc(ri_ok, 1)
                        dve.wait_ge(ri_ok, n + 1)
                        dve.wait_ge(t_ok, n + 1)
                        nc.vector.tensor_tensor(qn[:, t % 2].rearrange("p (g d) -> p g d", d=HD),
                                                ps[t % 4][:].rearrange("p (g d) -> p g d", d=HD),
                                                st[:, t % 2, 1].rearrange("p (g b) -> p g b", b=1).to_broadcast([P, 8, HD]),
                                                ALU.mult).then_inc(ps_free, 1)
                for v in range(V):
                    for t in range(TB):
                        if v < V - 1 and t == TB - 1:
                            split_lo(dve, QK + v + 1)
                        j = v * TB + t
                        dve.wait_ge(ada_in[j % 2], 16 * (j // 2 + 1))
                        if j >= 2:
                            dve.wait_ge(ada_part, j - 1)
                        weighted_rows(nc, dve, keep, acc[:, j % 2], ada[:, j % 2], acc_ok, j)
                        dve.wait_ge(v_hi_ok, v * TB + t + 1)
                        nc.vector.tensor_tensor(p_lo[:, t % 2], ps[t % 4][:], f32(p_hi[:, t % 2]),
                                                ALU.subtract).then_inc(ps_free, 1)
                dve.wait_ge(ada_part, V * TB)
                nc.vector.tensor_tensor(keep.mod[:, ADA0:6 * DB], ps_mod[:], keep.b_ada[:, ADA0:6 * DB], ALU.add
                                        ).then_inc(mod_ok, 1)
                dve.wait_ge(mod_ok, 1)
                nc.vector.scalar_tensor_tensor(out=keep.affine[:, 1, :], in0=keep.mod[:, 4 * DB:5 * DB], scalar=1.0,
                                               in1=keep.norm_gain[:, 1, :], op0=ALU.add, op1=ALU.mult)

            @block.tensor
            def _(pe):
                def product(c, t):
                    n = c * TB + t
                    pe.wait_ge(ps_free, n + 1)
                    tok = slice(t * P, (t + 1) * P)
                    for b in range(DB):
                        if t == 0:
                            pe.wait_ge(w_lo_ok, c * DB + b + 1)
                        nc.tensor.matmul(ps[t % 4][:], ht_hi[:, b, tok], w_hi[:, b], start=(b == 0), stop=False)
                        nc.tensor.matmul(ps[t % 4][:], ht_hi[:, b, tok], w_lo[:, b], start=False, stop=False)
                        mm = nc.tensor.matmul(ps[t % 4][:], ht_lo[:, b, tok], w_hi[:, b], start=False, stop=(b == DB - 1))
                        if t == TB - 1 and b < DB - 1:
                            mm.then_inc(w_free, 1)
                    mm.then_inc(mm_ok, 1)

                def transposes(c, t, order):
                    n = c * TB + t
                    pe.wait_ge(ps_free, n + 5)
                    pe.wait_ge(qt_ok, n + 1)
                    for k in range(4):
                        mm = nc.tensor.transpose(pst[t % 2][:, k * P:(k + 1) * P], qn[:, t % 2, k * P:(k + 1) * P],
                                                 order[:])
                    mm.then_inc(t_ok, 1)

                product(0, 0)
                for first, order in ((0, keep.mirror), (QK // 2, keep.ident)):
                    with pe.Fori(first, first + QK // 2) as c:
                        for t in range(1, TB):
                            product(c, t)
                            transposes(c, t - 1, order)
                        product(c + 1, 0)
                        transposes(c, TB - 1, order)
                for n in range(V * TB):
                    if n:
                        product(QK + n // TB, n % TB)
                    pe.wait_ge(acc_ok, (n + 1) * DB)
                    nc.tensor.matmul(ps_mod[:, n:n + 1], acc[:, n % 2], keep.one[:], start=True, stop=True).then_inc(ada_part, 1)


def attend(nc, keep, scr):
    UNIT = 2 * BANK
    STEPS = TB
    SLOTS = 5
    WAYS = 2

    def keys(i):
        return (i + 1) * P

    def units(i):
        return -(-keys(i) // UNIT)

    def groups(i):
        return -(-keys(i) // BANK)

    def unit(i, u):
        n = units(i)
        return slice(-(-(i + 1) * u // n) * P, -(-(i + 1) * (u + 1) // n) * P)

    def units_before(i):
        return sum(2 * units(k) for k in range(i))

    def groups_before(i):
        return sum(groups(k) for k in range(i))

    def pv_before(s):
        return sum(k + 1 for k in range(s))

    UNITS, GROUPS, PV_GROUPS = units_before(STEPS), groups_before(STEPS), pv_before(SUPER)
    EACH = GROUPS // WAYS
    assert GROUPS % (2 * WAYS) == 0 and PV_GROUPS % SLOTS == 0 and UNITS % 2 == 0
    PV_AT = {(1, 0): [(3, 0)], (2, 0): [(3, 1)], (3, 0): [(3, 2)], (4, 0): [(3, 3)], (6, 0): [(0, 0)], (10, 3): [(1, 0)],
             (11, 0): [(1, 1)], (13, 0): [(2, 0)], (13, 4): [(2, 1)], (15, 4): [(2, 2)]}
    OUT_AT = {4: [(3, 3)], 6: [(0, 0)], 11: [(1, 1)], 15: [(2, 2)]}
    TURN = 6

    def bank_of(n):
        return 2 if n % 2 else n // 2 % 2

    def slot_view(t, i, g, w):
        c = i % 4
        slot = (pv_before(i // 4) + g) % SLOTS
        return t[:, slot, 0:w // P, c * P:(c + 1) * P]

    with ExitStack() as ctx:
        def sb(name, shape, dt=F32):
            return ctx.enter_context(nc.sbuf_tensor(name, shape, dt))

        def pb(name, shape):
            return ctx.enter_context(nc.psum_tensor(name, shape, F32))

        def sem(name):
            return ctx.enter_context(nc.semaphore(name))

        q_st = sb("q_st", [P, 2, S], F32R)
        k_hi = sb("k_hi", [P, 2, S], F32R)
        k_lo = sb("k_lo", [P, 2, S], F32R)
        v_hi = sb("v_hi_sb", [P, TB, P], F32R)
        v_lo = sb("v_lo_sb", [P, TB, P], F32R)
        bias = sb("bias", [P, 2, S])
        sc = sb("sc", [P, 2, 2, S])
        p_hi = sb("pt_hi", [P, SLOTS, 4, BANK], F32R)
        p_lo = sb("pt_lo", [P, SLOTS, 4, BANK], F32R)
        tf = sb("tf", [P, 2, BANK])
        o_sb = sb("o_sb", [P, 2, BANK])
        low = sb("low", [P, 2, 2, 2])
        den = sb("den", [P, 2, TB])
        coef = sb("coef", [P, 2])
        dens = sb("dens", [P, TB, HEADS])
        ps_s = pb("ps_s", [P, 2, UNIT])
        ps_t = [pb(f"ps_u{i}", [P, BANK]) for i in range(3)]
        ps_o = pb("ps_o", [P, BANK])

        q_in = [sem(f"q_in{c}") for c in range(SUPER)]
        k_in = [sem(f"k_in{c}") for c in range(SUPER)]
        v_in = [sem(f"v_in{c}") for c in range(SUPER)]
        b_in = [sem(f"b_in{c}") for c in range(SUPER)]
        s_ok = sem("s_ok")
        a_ok = sem("a_ok")
        e_ok = sem("e_ok")
        rec_ok = sem("rec_ok")
        coef_ok = sem("coef_ok")
        c_ok = sem("c_ok")
        t_ok = sem("tt_ok")
        even_hi = sem("even_hi")
        even_lo = sem("even_lo")
        odd_hi = sem("odd_hi")
        odd_lo = sem("odd_lo")
        pv_ok = sem("pv_ok")
        o_ok = sem("o_ok")
        o_out = [sem(f"o_out{i}") for i in range(2)]
        d_ok = sem("d_ok")
        d_out = sem("d_out")

        def steps_of(eng, step):
            for i in range(TURN):
                step(0, i, False)
            with eng.Fori(0, HEADS - 1) as h:
                for i in range(TURN, STEPS):
                    step(h, i, False)
                for i in range(TURN):
                    step(h + 1, i, False)
            for i in range(TURN, STEPS):
                step(HEADS - 1, i, True)

        def at_start(h):
            return isinstance(h, int) and h == 0

        def preceding(h, i):
            if i:
                return h, i - 1
            return None if at_start(h) else (h - 1, STEPS - 1)

        def place(i, m, u):
            return units_before(i) + (1 - m) * units(i) + u

        def carried(h, table, i):
            return [(h - (s == SUPER - 1), s, g) for s, g in table.get(i, [])
                    if not (s == SUPER - 1 and at_start(h))]

        def following(h, i, last):
            if i < STEPS - 1:
                return h, i + 1
            return None if last else (h + 1, 0)

        with nc.Block() as block:
            @block.sync
            def _(sp):
                halves = (slice(0, HD), slice(HD, P))

                def part(src, i, c):
                    return src[bass.ds(i, 1)].rearrange("i (m d) s -> d (i m) s", m=2)[:, :, c * BANK:(c + 1) * BANK]

                def load_q(h, c):
                    cols = slice(c * BANK, (c + 1) * BANK)
                    for half, src in zip(halves, (scr.qk_hi, scr.qk_lo)):
                        sp.dma_start(f32(q_st[half, :, cols]), part(src, h, c)).then_inc(q_in[c], 16)

                def load_k(h, c):
                    cols = slice(c * BANK, (c + 1) * BANK)
                    for to, src in ((k_hi, scr.qk_hi), (k_lo, scr.qk_lo)):
                        for half in halves:
                            sp.dma_start(f32(to[half, :, cols]), part(src, h + HEADS, c)).then_inc(k_in[c], 16)

                def load_v(h, c):
                    at = slice(4 * c, 4 * c + 4)
                    for to, src in ((v_hi, scr.v_hi), (v_lo, scr.v_lo)):
                        sp.dma_start(f32(to[:, at]), src[bass.ds(h, 1)].rearrange("i p t e -> p (i t) e")[:, at]).then_inc(
                            v_in[c], 16)

                def load_bias(h, x):
                    rows = bass.AP(scr.bias_row.tensor, x * BANK, [[1, P], [DIAG, 2 * HEADS], [1, BANK]])
                    sp.dma_start(bias[:, :, x * BANK:(x + 1) * BANK], rows[:, bass.ds(h * 2, 2)]).then_inc(b_in[x], 16)

                def store_o(h, s):
                    cols = slice(s * BANK, (s + 1) * BANK)
                    sp.wait_ge(o_ok, h * SUPER + s + 2)
                    settle(sp, keep.passed)
                    sp.dma_start(scr.o_t[bass.ds(h, 1)].rearrange("i p s -> p (i s)")[:, cols], o_sb[:, s % 2]).then_inc(
                        o_out[s % 2], 16)

                def head(h, last):
                    for s in range(2):
                        store_o(h, s)
                        if not last:
                            sp.wait_ge(s_ok, h * UNITS + units_before(4 * s + 4))
                            settle(sp, keep.passed)
                            load_q(h + 1, s)
                    if not last:
                        sp.wait_ge(s_ok, h * UNITS + UNITS)
                        settle(sp, keep.passed)
                        load_k(h + 1, 0)
                        sp.wait_ge(a_ok, h * UNITS + UNITS + 2)
                        settle(sp, keep.passed)
                        load_bias(h + 1, SUPER - 1)
                        for c in range(1, SUPER):
                            load_k(h + 1, c)
                            load_bias(h + 1, SUPER - 1 - c)
                            if c >= 2:
                                load_q(h + 1, c)
                    store_o(h, 2)
                    if not last:
                        for g in range(SUPER):
                            sp.wait_ge(pv_ok, h * PV_GROUPS + pv_before(SUPER - 1) + g + 1 + SLOTS)
                            settle(sp, keep.passed)
                            load_v(h + 1, g)
                    store_o(h, 3)

                sp.sem_inc(a_ok, 2)
                sp.sem_inc(t_ok, 1)
                sp.sem_inc(even_lo, 2)
                sp.sem_inc(odd_hi, 1)
                sp.sem_inc(odd_lo, 2)
                sp.sem_inc(pv_ok, SLOTS)
                sp.sem_inc(o_ok, 1)
                for i in range(2):
                    sp.sem_inc(o_out[i], 16)
                for c in range(SUPER):
                    load_q(0, c)
                    load_k(0, c)
                    load_bias(0, SUPER - 1 - c)
                for c in range(SUPER):
                    load_v(0, c)
                with sp.Fori(0, HEADS - 1) as h:
                    head(h, False)
                head(HEADS - 1, True)
                sp.wait_ge(d_ok, 2 * HEADS)
                sp.dma_start(scr.l_sum, dens[:]).then_inc(d_out, 16)
                sp.wait_ge(d_out, 16)
                for i in range(2):
                    sp.wait_ge(o_out[i], 16 * (1 + HEADS * SUPER // 2))

            @block.tensor
            def _(pe):
                def scores(h, i, m, u):
                    n = place(i, m, u)
                    pe.wait_ge(a_ok, h * UNITS + n + 1)
                    q_cols = slice(i * P, (i + 1) * P)
                    if i % 4 == 0 and m == 1 and u == 0:
                        pe.wait_ge(q_in[i // 4], (h + 1) * 32)
                        pe.wait_ge(k_in[i // 4], (h + 1) * 64)
                    keys_of = unit(i, u)
                    for at in range(keys_of.start, keys_of.stop, BANK):
                        w = min(BANK, keys_of.stop - at)
                        out = ps_s[:, n % 2, at - keys_of.start:at - keys_of.start + w]
                        for k in (k_hi, k_lo):
                            mm = nc.tensor.matmul(out, q_st[:, m, q_cols], k[:, m, at:at + w],
                                                  start=(k is k_hi), stop=(k is k_lo))
                    mm.then_inc(s_ok, 1)

                def transposes(h, i, g):
                    n = groups_before(i) + g
                    w = min(BANK, keys(i) - g * BANK)
                    done = min(u + 1 for u in range(units(i)) if unit(i, u).stop >= g * BANK + w)
                    pe.wait_ge(c_ok, h * (UNITS // 2) + units_before(i) // 2 + done)
                    pe.wait_ge(odd_hi if n % 2 else even_lo, h * EACH + n // 2 + 1)
                    for k in range(w // P):
                        at = g * BANK + k * P
                        mm = nc.tensor.transpose(ps_t[bank_of(n)][:, k * P:(k + 1) * P], sc[:, i % 2, 0, at:at + P],
                                                 keep.ident[:])
                    mm.then_inc(t_ok, 1)

                def pv(h, s, g):
                    slot = (pv_before(s) + g) % SLOTS
                    n = groups_before(4 * s + 3) + g + 1
                    pe.wait_ge(even_lo, h * EACH + (n + 1) // 2 + 2)
                    pe.wait_ge(odd_lo, h * EACH + n // 2 + 2)
                    pe.wait_ge(v_in[g], (h + 1) * 32)
                    if g == 0:
                        pe.wait_ge(o_ok, h * SUPER + s + 1)
                    for kb in range(4 * g, 4 * g + 4):
                        c0 = max(kb - 4 * s, 0) * P
                        for v, p in ((v_hi, p_lo), (v_lo, p_hi), (v_hi, p_hi)):
                            mm = nc.tensor.matmul(ps_o[:, c0:BANK], v[:, kb], p[:, slot, kb % 4, c0:BANK],
                                                  start=(kb == 0 and p is p_lo),
                                                  stop=(kb == 4 * s + 3 and v is v_hi and p is p_hi))
                    mm.then_inc(pv_ok, 1)

                def step(h, i, last):
                    then, past = following(h, i, last), preceding(h, i)
                    rest = [(*then, 0, u) for u in range(units(then[1]))] if then else []
                    for g in range(groups(past[1]) + 1 if past else 0):
                        for at in carried(h, PV_AT, (i, g)):
                            pv(*at)
                        if g < groups(past[1]):
                            transposes(*past, g)
                            if g % 2 and rest:
                                scores(*rest.pop(0))
                    for unit in rest:
                        scores(*unit)
                    then = then and following(*then, last)
                    if then:
                        for u in range(units(then[1])):
                            scores(*then, 1, u)

                for m in (1, 0):
                    for u in range(units(0)):
                        scores(0, 0, m, u)
                for u in range(units(1)):
                    scores(0, 1, 1, u)
                steps_of(pe, step)
                for g in range(groups(STEPS - 1)):
                    transposes(HEADS - 1, STEPS - 1, g)
                for g in range(SUPER):
                    pv(HEADS - 1, SUPER - 1, g)

            @block.scalar
            def _(act):
                def exponentials(h, i, m):
                    n = place(i, m, units(i) - 1)
                    act.wait_ge(a_ok, h * UNITS + n + 3)
                    s = sc[:, i % 2, m, 0:keys(i)]
                    nc.scalar.activation(s, s, ACT.Exp, bias=low[:, i % 2, m, units(i) - 1:units(i)], scale=-1.0,
                                         accum_out=den[:, m, i:i + 1]).then_inc(e_ok, 1)

                def out_of_psum(h, i, g):
                    n = groups_before(i) + g
                    w = min(BANK, keys(i) - g * BANK)
                    act.wait_ge(t_ok, h * GROUPS + n + 2)
                    if n % 2:
                        act.wait_ge(odd_lo, h * EACH + n // 2 + 1)
                        nc.scalar.copy(tf[:, (n // 2) % 2, 0:w], ps_t[2][:, 0:w])
                    if i % 4 == 0:
                        act.wait_ge(pv_ok, h * PV_GROUPS + pv_before(i // 4) + g + 1)
                    nc.scalar.copy(slot_view(p_hi, i, g, w), ps_t[bank_of(n)][:, 0:w].rearrange("p (k c) -> p k c", c=P)
                                   ).then_inc(odd_hi if n % 2 else even_hi, 1)

                def out_super(h, s):
                    act.wait_ge(pv_ok, h * PV_GROUPS + pv_before(s + 1) + SLOTS)
                    act.wait_ge(o_out[s % 2], 16 * (h * (SUPER // 2) + s // 2 + 1))
                    nc.scalar.copy(o_sb[:, s % 2], ps_o[:]).then_inc(o_ok, 1)

                def step(h, i, last):
                    then, past = following(h, i, last), preceding(h, i)
                    for g in range(groups(past[1]) if past else 0):
                        out_of_psum(*past, g)
                    if then:
                        exponentials(*then, 1)
                        exponentials(*then, 0)
                    for h_out, s, _ in carried(h, OUT_AT, i):
                        out_super(h_out, s)

                exponentials(0, 0, 1)
                exponentials(0, 0, 0)
                steps_of(act, step)
                for g in range(groups(STEPS - 1)):
                    out_of_psum(HEADS - 1, STEPS - 1, g)
                out_super(HEADS - 1, SUPER - 1)

            @block.gpsimd
            def _(pool):
                def split_lo(h, i):
                    for g in range(groups(i)):
                        n = groups_before(i) + g
                        if n % 2 == 0:
                            continue
                        w = min(BANK, keys(i) - g * BANK)
                        pool.wait_ge(odd_hi, h * EACH + n // 2 + 2)
                        nc.gpsimd.tensor_tensor(slot_view(p_lo, i, g, w),
                                                tf[:, (n // 2) % 2, 0:w].rearrange("p (k c) -> p k c", c=P),
                                                f32(slot_view(p_hi, i, g, w)), ALU.subtract).then_inc(odd_lo, 1)

                def step(h, i, last):
                    if preceding(h, i):
                        split_lo(*preceding(h, i))

                steps_of(pool, step)
                split_lo(HEADS - 1, STEPS - 1)

            @block.vector
            def _(dve):
                def add_bias(h, i, m, u):
                    n = place(i, m, u)
                    dve.wait_ge(s_ok, h * UNITS + n + 1)
                    at = unit(i, u)
                    w = at.stop - at.start
                    x0 = (STEPS - 1 - i) * P + at.start
                    if i % 4 == 0 and m == 1 and u == 0:
                        dve.wait_ge(b_in[SUPER - 1 - i // 4], (h + 1) * 16)
                    if u:
                        dve.wait_ge(a_ok, h * UNITS + n + 2)
                    if m == 1 and not (at_start(h) and i < 2):
                        dve.wait_ge(c_ok, h * (UNITS // 2) + units_before(i) // 2 - units((i - 1) % STEPS))
                    if m == 0 and not (at_start(h) and i < 2):
                        before = sum(groups((i - k) % STEPS) for k in (1, 2))
                        read = groups_before(i) - before + min(-(-at.stop // BANK), groups((i - 2) % STEPS))
                        dve.wait_ge(t_ok, h * GROUPS + read + 1)
                    settle(dve, keep.passed)
                    nc.vector.tensor_tensor_reduce(sc[:, i % 2, m, at], ps_s[:, n % 2, 0:w],
                                                   bias[:, m, x0:x0 + w], 1.0,
                                                   low[:, i % 2, m, 0:1] if u else FAR, ALU.add, ALU.min,
                                                   low[:, i % 2, m, u:u + 1]).then_inc(a_ok, 1)

                def weigh(h, i):
                    n = h * STEPS + i
                    dve.wait_ge(e_ok, n * 2 + 2)
                    nc.vector.reciprocal(coef[:, 0:1], den[:, 1, i:i + 1]).then_inc(rec_ok, 1)
                    dve.wait_ge(rec_ok, n + 1)
                    nc.vector.scalar_tensor_tensor(out=coef[:, 1:2], in0=den[:, 0, i:i + 1], scalar=keep.neg_lambda[:],
                                                   in1=coef[:, 0:1], op0=ALU.mult, op1=ALU.mult).then_inc(coef_ok, 1)
                    dve.wait_ge(coef_ok, n + 1)

                def combine(h, i, u):
                    if u == 0:
                        weigh(h, i)
                    at = unit(i, u)
                    a, b = sc[:, i % 2, 0, at], sc[:, i % 2, 1, at]
                    nc.vector.scalar_tensor_tensor(out=a, in0=b, scalar=coef[:, 1:2], in1=a, op0=ALU.mult,
                                                   op1=ALU.add).then_inc(c_ok, 1)

                def split_lo(h, i, g):
                    n = groups_before(i) + g
                    dve.wait_ge(even_hi, h * EACH + n // 2 + 1)
                    w = min(BANK, keys(i) - g * BANK)
                    nc.vector.tensor_tensor(slot_view(p_lo, i, g, w), ps_t[bank_of(n)][:, 0:w].rearrange("p (k c) -> p k c", c=P),
                                            f32(slot_view(p_hi, i, g, w)), ALU.subtract).then_inc(even_lo, 1)

                def even_groups(i):
                    return [g for g in range(groups(i)) if (groups_before(i) + g) % 2 == 0]

                def keep_sums(h, i0, i1):
                    nc.vector.tensor_copy(dens[:, i0:i1, bass.ds(h, 1)],
                                          den[:, 0, i0:i1].rearrange("p (t b) -> p t b", b=1)).then_inc(d_ok, 1)

                def step(h, i, last):
                    then, past = following(h, i, last), preceding(h, i)
                    if i == STEPS - 1:
                        keep_sums(h, 0, TB - 1)
                    if then:
                        for u in range(units(then[1])):
                            add_bias(*then, 1, u)
                    adds = [(*then, 0, u) for u in range(units(then[1]))] if then else []
                    evens = even_groups(past[1]) if past else []
                    while adds or evens:
                        if evens:
                            split_lo(*past, evens.pop(0))
                        if adds:
                            add_bias(*adds.pop(0))
                    for u in range(units(i)):
                        combine(h, i, u)
                    if i == STEPS - 1:
                        keep_sums(h, TB - 1, TB)

                for m in (1, 0):
                    add_bias(0, 0, m, 0)
                steps_of(dve, step)
                for g in even_groups(STEPS - 1):
                    split_lo(HEADS - 1, STEPS - 1, g)


def diagonals(nc, keep, diag, first):
    ident = keep.ident[:].rearrange("p (b n) -> p b n", b=1).to_broadcast([P, DB, P])
    cols = keep.mod[:, first:first + DB].rearrange("p (b n) -> p b n", n=1).to_broadcast([P, DB, P])
    return nc.vector.tensor_tensor(diag[:], ident, cols, ALU.mult)


class Ahead:
    FC = 256
    FB = FC // P

    def __init__(self, nc, ctx, ins):
        self.w_raw = ctx.enter_context(nc.sbuf_tensor("wf_raw", [P, 2, DB * self.FC], F32))
        self.h_hi = ctx.enter_context(nc.sbuf_tensor("h_hi_f0", [P, DB, BANK], F32R))
        self.h_lo = ctx.enter_context(nc.sbuf_tensor("h_lo_f0", [P, DB, BANK], F32R))
        self.w_in = [ctx.enter_context(nc.semaphore(f"wf_in{i}")) for i in range(2)]
        self.h_in = [ctx.enter_context(nc.semaphore(f"h_in{g}")) for g in range(2)]
        self.raw = [self.w_raw[:, 0].rearrange("p (b f) -> p b f", b=DB),
                    self.w_raw[:, 1].rearrange("p (b n) -> p b n", b=self.FB)]
        self.w1_v = ins["mlp_w1"][0].rearrange("(b p) f -> p b f", p=P)
        self.w2_v = ins["mlp_w2"][0].rearrange("(b p) n -> p b n", p=P)

    def load_w1(self, sp, f):
        sp.dma_start(self.raw[0], self.w1_v[:, :, bass.ds(f * self.FC, self.FC)]).then_inc(self.w_in[0], 16)

    def load_w2(self, sp, f):
        sp.dma_start(self.raw[1], self.w2_v[:, bass.ds(f * self.FB, self.FB)]).then_inc(self.w_in[1], 16)


def load_h2(sp, scr, ahead, g, h_hi, h_lo, at):
    for to, src in ((h_hi, scr.h2_hi), (h_lo, scr.h2_lo)):
        sp.dma_start(f32(to[:]), src[:, :, at:at + BANK]).then_inc(ahead.h_in[g], 16)


def mix(nc, ins, keep, scr, ahead):
    with ExitStack() as ctx:
        def sb(name, shape, dt=F32):
            return ctx.enter_context(nc.sbuf_tensor(name, shape, dt))

        def pb(name, shape):
            return ctx.enter_context(nc.psum_tensor(name, shape, F32))

        def sem(name):
            return ctx.enter_context(nc.semaphore(name))

        wo_raw = ahead.w_raw[:].rearrange("p a (i n) -> p (a i) n", i=2)
        RAWS = 4
        wo_hi = sb("wo_hi", [P, HEADS, D], F32R)
        wo_lo = sb("wo_lo", [P, HEADS, D], F32R)
        gate = sb("gate_m", [P, D])
        diag = sb("diag_m", [P, DB, P])
        ones = sb("ones_m", [P, P])
        ot = sb("ot", [P, 2, HEADS, P])
        xr = sb("xr", [P, 2, D])
        den = sb("den_m", [P, TB, HEADS])
        sq = sb("sq_m", [P, D])
        st = sb("st_m", [P, 2, HEADS])
        on = sb("on", [P, D])
        o_hi = sb("o_hi", [P, 2, D], F32R)
        o_lo = sb("o_lo", [P, 2, D], F32R)
        x1 = sb("x1_m", [P, 2, D])
        sq2 = sb("sq2_m", [P, D])
        st2 = sb("st2_m", [P, 2])
        xn = sb("xn_m", [P, D])
        hf = sb("hf", [P, 2, D])
        h_hi = sb("h_hi_m", [P, 2, D], F32R)
        h_lo = sb("h_lo_m", [P, 2, D], F32R)
        ps_a = pb("ps_a", [P, D])
        ps_b = pb("ps_b", [P, D])
        ps_y = pb("ps_y", [P, D])
        ps_d = pb("ps_d", [P, D])

        wo_in = [sem(f"wo_in{i}") for i in range(RAWS)]
        wo_hi_ok = sem("wo_hi_ok")
        wo_lo_ok = sem("wo_lo_ok")
        gate_d = sem("gate_d")
        gate_m = sem("gate_mm")
        gate_ok = sem("gate_ok")
        den_in = sem("den_in")
        den_ok = sem("den_ok")
        o_in = [sem(f"o_in{i}") for i in range(2)]
        x_in = [sem(f"xm_in{i}") for i in range(2)]
        ta_ok = sem("ta_ok")
        sq_ok = sem("sqm_ok")
        ss_ok = sem("ssm_ok")
        var_ok = sem("var_ok")
        sd_ok = sem("sdm_ok")
        ri_ok = sem("rim_ok")
        on_ok = sem("on_ok")
        tb_ok = sem("tb_ok")
        ohi_ok = sem("ohi_ok")
        olo_ok = sem("olo_ok")
        y_ok = sem("y_ok")
        gy_ok = sem("gy_ok")
        x1_ok = sem("x1_ok")
        sq2_ok = sem("sq2_ok")
        sd2_ok = sem("sd2_ok")
        ri2_ok = sem("ri2_ok")
        xn_ok = sem("xn_ok")
        td_ok = sem("td_ok")
        hf_ok = sem("hf_ok")
        hhi_ok = sem("hhi_ok")
        hlo_ok = sem("hlo_ok")
        x1_out = [sem(f"x1_out{i}") for i in range(2)]
        h_out = [sem(f"h_out{i}") for i in range(2)]

        wo_v = ins["da_w_o"][0].rearrange("(h p) n -> h p n", p=P)
        ot_v = scr.o_t.rearrange("h p s -> p h s")
        blocks = lambda a: a.rearrange("p (b n) -> p b n", n=P)
        wide = lambda a: a.rearrange("p (b n) -> p b n", n=1).to_broadcast([P, HEADS, P])

        class Block:

            def __init__(self, pair, k):
                self.pair, self.k = pair, k
                self.t = pair * 2 + k
                self.turn = pair + k // 2
                self.side = k % 2

            def reaches(self, n):
                return not isinstance(self.t, int) or self.t >= n

            def valid(self):
                return not isinstance(self.t, int) or 0 <= self.t < TB

        def weights_of(t):
            return range((t + 1) * HEADS // 2, (t + 2) * HEADS // 2) if isinstance(t, int) and t in (-1, 0) else ()

        def iterations(eng, body):
            def run(pair, k):
                body(lambda d: Block(pair, k + d))

            for pair in (-1, 0, 1):
                for k in range(2):
                    run(pair, k)
            with eng.Fori(2, TB // 2 - 2) as pair:
                for k in range(2):
                    run(pair, k)
            for pair in (TB // 2 - 2, TB // 2 - 1, TB // 2):
                for k in range(2):
                    run(pair, k)

        with nc.Block() as block:
            @block.sync
            def _(sp):
                def load_o(b):
                    if b.reaches(2):
                        sp.wait_ge(ta_ok, b.t - 1)
                        settle(sp, keep.passed)
                    sp.dma_start(ot[:, b.side], ot_v[:, :, bass.ds(b.t * P, P)]).then_inc(o_in[b.side], 16)

                def load_x(b):
                    if b.reaches(2):
                        sp.wait_ge(x1_ok, b.t - 1)
                        settle(sp, keep.passed)
                    sp.dma_start(xr[:, b.side], ins["x"][0][bass.ds(b.t * P, P)]).then_inc(x_in[b.side], 16)

                def store_x1(b):
                    sp.wait_ge(x1_ok, b.t + 1)
                    settle(sp, keep.passed)
                    sp.dma_start(scr.x1[bass.ds(b.t * P, P)], x1[:, b.side]).then_inc(x1_out[b.side], 16)

                def store_h(b):
                    for part_ok, part, to in ((hhi_ok, h_hi, scr.h2_hi), (hlo_ok, h_lo, scr.h2_lo)):
                        sp.wait_ge(part_ok, b.t + 1)
                        settle(sp, keep.passed)
                        sp.dma_start(to[:, :, bass.ds(b.t * P, P)], f32(blocks(part[:, b.side]))).then_inc(h_out[b.side], 16)

                def body(at):
                    if isinstance(at(0).t, int) and at(0).t == TB - 4:
                        for i in range(2):
                            sp.wait_ge(h_out[i], 32 * (TB - 6) // 2)
                        load_h2(sp, scr, ahead, 0, ahead.h_hi, ahead.h_lo, 0)
                        sp.wait_ge(wo_lo_ok, HEADS)
                        ahead.load_w1(sp, 0)
                        ahead.load_w2(sp, 0)
                    if at(3).valid() and at(3).reaches(2):
                        load_o(at(3))
                    if at(1).valid() and at(1).reaches(2):
                        load_x(at(1))
                    if at(-1).valid():
                        store_x1(at(-1))
                    if at(-2).valid():
                        store_h(at(-2))

                sp.dma_start(den[:], scr.l_sum).then_inc(den_in, 16)
                for k in range(2):
                    load_o(Block(0, k))
                for hh in range(HEADS):
                    if hh >= RAWS:
                        sp.wait_ge(wo_lo_ok, hh - RAWS + 1)
                    sp.dma_start(wo_raw[:, hh % RAWS], wo_v[hh]).then_inc(wo_in[hh % RAWS], 16)
                for k in range(2):
                    load_x(Block(0, k))
                iterations(sp, body)
                for i in range(2):
                    sp.wait_ge(x1_out[i], 16 * TB // 2)
                    sp.wait_ge(h_out[i], 32 * TB // 2)

            @block.gpsimd
            def _(pool):
                def second_lo(b):
                    pool.wait_ge(hhi_ok, b.t + 1)
                    nc.gpsimd.tensor_tensor(h_lo[:, b.side], hf[:, b.side], f32(h_hi[:, b.side]), ALU.subtract
                                            ).then_inc(hlo_ok, 1)

                def body(at):
                    if at(-2).valid():
                        second_lo(at(-2))

                iterations(pool, body)

            @block.scalar
            def _(act):
                def squares(b):
                    act.wait_ge(ta_ok, b.t + 1)
                    if b.reaches(1):
                        act.wait_ge(ss_ok, b.t)
                    nc.scalar.activation(sq[:], ps_a[:], ACT.Square).then_inc(sq_ok, 1)

                def deviations(b):
                    act.wait_ge(var_ok, b.t + 1)
                    nc.scalar.activation(st[:, 1], st[:, 0], ACT.Sqrt).then_inc(sd_ok, 1)

                def first_hi(b):
                    act.wait_ge(tb_ok, b.t + 1)
                    if b.reaches(2):
                        act.wait_ge(y_ok, 2 * b.t - 2)
                    nc.scalar.copy(o_hi[:, b.side], ps_b[:]).then_inc(ohi_ok, 1)

                def second_norm(b):
                    act.wait_ge(x1_ok, b.t + 1)
                    nc.scalar.activation(sq2[:], x1[:, b.side], ACT.Square, accum_out=st2[:, 0:1]).then_inc(sq2_ok, 1)
                    act.wait_ge(sq2_ok, b.t + 1)
                    nc.scalar.activation(st2[:, 1:2], st2[:, 0:1], ACT.Sqrt, bias=keep.eps[:],
                                         scale=1.0 / D).then_inc(sd2_ok, 1)

                def second_affine(b):
                    act.wait_ge(td_ok, b.t + 1)
                    if b.reaches(2):
                        act.wait_ge(hlo_ok, b.t - 1)
                    for d in range(DB):
                        at = slice(d * P, (d + 1) * P)
                        a = nc.scalar.activation(hf[:, b.side, at], ps_d[:, at], ACT.Identity,
                                                 bias=keep.mod[:, 3 * DB + d:3 * DB + d + 1],
                                                 scale=keep.affine[:, 1, d:d + 1])
                    a.then_inc(hf_ok, 1)
                    act.wait_ge(hf_ok, b.t + 1)
                    if b.reaches(2):
                        act.wait_ge(h_out[b.side], 32 * b.turn)
                    nc.scalar.copy(h_hi[:, b.side], hf[:, b.side]).then_inc(hhi_ok, 1)

                def output_weights(hh):
                    act.wait_ge(wo_in[hh % RAWS], 16 * (hh // RAWS + 1))
                    nc.scalar.activation(wo_hi[:, hh], wo_raw[:, hh % RAWS], ACT.Copy, scale=keep.sub_gain[:]).then_inc(wo_hi_ok, 1)

                def body(at):
                    for hh in weights_of(at(0).t):
                        output_weights(hh)
                    if at(-1).valid():
                        second_norm(at(-1))
                    if at(-2).valid():
                        second_affine(at(-2))
                    if at(1).valid():
                        first_hi(at(1))
                    if at(2).valid():
                        squares(at(2))
                        deviations(at(2))

                iterations(act, body)

            @block.vector
            def _(dve):
                def head_rows(b):
                    dve.wait_ge(sq_ok, b.t + 1)
                    if b.reaches(1):
                        dve.wait_ge(sd_ok, b.t)
                    nc.vector.tensor_reduce(st[:, 0], blocks(sq[:]), AX_X, ALU.add).then_inc(ss_ok, 1)
                    dve.wait_ge(ss_ok, b.t + 1)
                    settle(dve, keep.passed)
                    nc.vector.scalar_tensor_tensor(out=st[:, 0], in0=st[:, 0], scalar=1.0 / P,
                                                   in1=den[:, bass.ds(b.t, 1)].rearrange("p i h -> p (i h)"),
                                                   op0=ALU.mult, op1=ALU.add).then_inc(var_ok, 1)
                    dve.wait_ge(sd_ok, b.t + 1)
                    nc.vector.reciprocal(st[:, 1], st[:, 1]).then_inc(ri_ok, 1)
                    dve.wait_ge(ri_ok, b.t + 1)
                    if b.reaches(1):
                        dve.wait_ge(tb_ok, b.t)
                    nc.vector.tensor_tensor(blocks(on[:]), blocks(ps_a[:]), wide(st[:, 1]), ALU.mult).then_inc(on_ok, 1)

                def first_lo(b):
                    dve.wait_ge(ohi_ok, b.t + 1)
                    nc.vector.tensor_tensor(o_lo[:, b.side], ps_b[:], f32(o_hi[:, b.side]), ALU.subtract).then_inc(olo_ok, 1)

                def gated(b, n):
                    at = slice(n * BANK, (n + 1) * BANK)
                    dve.wait_ge(y_ok, 2 * b.t + n + 1)
                    if b.reaches(2) and n == 0:
                        dve.wait_ge(x1_out[b.side], 16 * b.turn)
                        dve.wait_ge(sq2_ok, b.t - 1)
                    nc.vector.tensor_tensor(x1[:, b.side, at], ps_y[:, at], gate[:, at], ALU.mult).then_inc(gy_ok, 1)

                def residual(b):
                    dve.wait_ge(gy_ok, 2 * b.t + 2)
                    dve.wait_ge(x_in[b.side], 16 * b.turn + 16)
                    nc.vector.tensor_tensor(x1[:, b.side], x1[:, b.side], xr[:, b.side], ALU.add).then_inc(x1_ok, 1)

                def second_rows(b):
                    dve.wait_ge(sd2_ok, b.t + 1)
                    nc.vector.reciprocal(st2[:, 1:2], st2[:, 1:2]).then_inc(ri2_ok, 1)
                    dve.wait_ge(ri2_ok, b.t + 1)
                    if b.reaches(1):
                        dve.wait_ge(td_ok, b.t)
                    nc.vector.tensor_scalar(xn[:], x1[:, b.side], st2[:, 1:2], None, ALU.mult).then_inc(xn_ok, 1)

                def output_weights(hh):
                    dve.wait_ge(wo_hi_ok, hh + 1)
                    nc.vector.scalar_tensor_tensor(out=wo_lo[:, hh], in0=wo_raw[:, hh % RAWS], scalar=keep.sub_gain[:],
                                                   in1=f32(wo_hi[:, hh]), op0=ALU.mult, op1=ALU.subtract
                                                   ).then_inc(wo_lo_ok, 1)

                def body(at):
                    for hh in weights_of(at(0).t):
                        output_weights(hh)
                    if at(-1).valid():
                        gated(at(-1), 1)
                        residual(at(-1))
                        second_rows(at(-1))
                    if at(0).valid():
                        gated(at(0), 0)
                    if at(1).valid():
                        first_lo(at(1))
                    if at(2).valid():
                        head_rows(at(2))

                nc.vector.memset(ones[:], 1.0)
                diagonals(nc, keep, diag, 2 * DB).then_inc(gate_d, 1)
                dve.wait_ge(gate_m, 2)
                nc.vector.tensor_copy(gate[:], ps_y[:]).then_inc(gate_ok, 1)
                dve.wait_ge(den_in, 16)
                nc.vector.scalar_tensor_tensor(out=den[:], in0=den[:], scalar=EPS, in1=den[:], op0=ALU.mult,
                                               op1=ALU.mult).then_inc(den_ok, 1)
                dve.wait_ge(den_ok, 1)
                iterations(dve, body)

            @block.tensor
            def _(pe):
                def transposes_a(b):
                    pe.wait_ge(o_in[b.side], 16 * b.turn + 16)
                    if b.reaches(1):
                        pe.wait_ge(on_ok, b.t)
                    for hh in range(HEADS):
                        mm = nc.tensor.transpose(ps_a[:, hh * P:(hh + 1) * P], ot[:, b.side, hh], keep.ident[:])
                    mm.then_inc(ta_ok, 1)

                def transposes_b(b):
                    pe.wait_ge(on_ok, b.t + 1)
                    if b.reaches(1):
                        pe.wait_ge(olo_ok, b.t)
                    for hh in range(HEADS):
                        mm = nc.tensor.transpose(ps_b[:, hh * P:(hh + 1) * P], on[:, hh * P:(hh + 1) * P], keep.mirror[:])
                    mm.then_inc(tb_ok, 1)

                def product(b, n):
                    pe.wait_ge(olo_ok, b.t + 1)
                    if b.reaches(1):
                        pe.wait_ge(gy_ok, 2 * b.t - 1 + n)
                    else:
                        pe.wait_ge(gate_ok, 1)
                    at = slice(n * BANK, (n + 1) * BANK)
                    for hh in range(HEADS):
                        if not b.reaches(1):
                            pe.wait_ge(wo_lo_ok, hh + 1)
                        hs = slice(hh * P, (hh + 1) * P)
                        nc.tensor.matmul(ps_y[:, at], o_hi[:, b.side, hs], wo_hi[:, hh, at], start=(hh == 0), stop=False)
                        nc.tensor.matmul(ps_y[:, at], o_hi[:, b.side, hs], wo_lo[:, hh, at], start=False, stop=False)
                        mm = nc.tensor.matmul(ps_y[:, at], o_lo[:, b.side, hs], wo_hi[:, hh, at], start=False,
                                              stop=(hh == HEADS - 1))
                    mm.then_inc(y_ok, 1)

                def transposes_d(b):
                    pe.wait_ge(xn_ok, b.t + 1)
                    if b.reaches(1):
                        pe.wait_ge(hf_ok, b.t)
                    for d in range(DB):
                        mm = nc.tensor.transpose(ps_d[:, d * P:(d + 1) * P], xn[:, d * P:(d + 1) * P], keep.ident[:])
                    mm.then_inc(td_ok, 1)

                def body(at):
                    if at(0).valid():
                        product(at(0), 0)
                    if at(1).valid():
                        transposes_b(at(1))
                    if at(2).valid():
                        transposes_a(at(2))
                    if at(0).valid():
                        product(at(0), 1)
                    if at(-1).valid():
                        transposes_d(at(-1))

                pe.wait_ge(gate_d, 1)
                for n in range(2):
                    nc.tensor.matmul(ps_y[:, n * BANK:(n + 1) * BANK], ones[:], diag[:, 4 * n:4 * n + 4].rearrange("p b n -> p (b n)"),
                                     start=True, stop=True).then_inc(gate_m, 1)
                iterations(pe, body)


def mlp(nc, keep, scr, ahead, out):
    HALVES = 2
    HT = S // HALVES
    FC, FB = ahead.FC, ahead.FB
    CHUNKS = F // FC
    TG = HT // BANK
    HB = HT // P
    UB = BANK // P
    NB = D // BANK
    with ExitStack() as ctx:
        def sb(name, shape, dt=F32):
            return ctx.enter_context(nc.sbuf_tensor(name, shape, dt))

        def pb(name, shape):
            return ctx.enter_context(nc.psum_tensor(name, shape, F32))

        def sem(name):
            return ctx.enter_context(nc.semaphore(name))

        h_hi = [ahead.h_hi, sb("h_hi_f1", [P, DB, BANK], F32R)]
        h_lo = [ahead.h_lo, sb("h_lo_f1", [P, DB, BANK], F32R)]
        acc = sb("acc", [P, HB, D])
        w1_hi = sb("w1_hi", [P, 2, DB, FC], F32R)
        w1_lo = sb("w1_lo", [P, 2, DB, FC], F32R)
        w2_hi = sb("w2_hi", [P, 2, FB, D], F32R)
        w2_lo = sb("w2_lo", [P, 2, FB, D], F32R)
        r = sb("r", [P, 2, BANK])
        g_hi = sb("g_hi", [P, TG, FB, BANK], F32R)
        g_lo = sb("g_lo", [P, TG, FB, BANK], F32R)
        gate = sb("gate_f", [P, D])
        diag = sb("diag_f", [P, DB, P])
        ones = sb("ones_f", [P, P])
        ps_h = [pb(f"ps_h{i}", [P, BANK]) for i in range(4)]
        ps_y = [pb(f"ps_y{i}", [P, BANK]) for i in range(4)]

        acc_in = [sem(f"acc_in{g}") for g in range(TG)]
        acc_out = [sem(f"acc_out{g}") for g in range(TG)]
        w_hi_ok = [sem(f"wfhi_ok{i}") for i in range(2)]
        w_lo_ok = [sem(f"wflo_ok{i}") for i in range(2)]
        w2g_ok = sem("w2g_ok")
        gate_d = sem("gatef_d")
        gate_m = sem("gatef_m")
        gate_ok = sem("gatef_ok")
        mh_ok = sem("mh_ok")
        r_ok = sem("r_ok")
        g_ok = sem("g_ok")
        ghi_ok = sem("ghi_ok")
        glo_ok = sem("glo_ok")
        y_ok = sem("yf_ok")
        add_ok = sem("add_ok")

        YB = UB * NB
        x1_v = scr.x1.rearrange("(t p) d -> t p d", p=P)
        out_v = out[0].rearrange("(t p) d -> t p d", p=P)
        raw, w_in, h_in = ahead.raw, ahead.w_in, ahead.h_in
        hi = [w1_hi, w2_hi]
        lo = [w1_lo, w2_lo]

        def rounds(eng, head, body):
            PAIRS = CHUNKS // 2
            head()
            for half in range(HALVES):
                with eng.Fori(half * PAIRS, (half + 1) * PAIRS - 1) as pair:
                    for e in range(2):
                        body(half, half, pair * 2 + e, e, False)
                i0 = half * CHUNKS
                body(half, half, i0 + CHUNKS - 2, 0, False)
                body(half, half + 1, i0 + CHUNKS - 1, 1, half == HALVES - 1)

        with nc.Block() as block:
            @block.sync
            def _(sp):
                def load_w(i, f):
                    sp.wait_ge(w_lo_ok[0], i + 1)
                    settle(sp, keep.passed)
                    ahead.load_w1(sp, f)
                    sp.wait_ge(w_lo_ok[1], i + 1)
                    settle(sp, keep.passed)
                    ahead.load_w2(sp, f)

                def load_h(half, g):
                    if half:
                        sp.wait_ge(mh_ok, (half * CHUNKS - 1) * TG * FB + (g + 1) * FB)
                    load_h2(sp, scr, ahead, g, h_hi[g], h_lo[g], half * HT + g * BANK)

                def load_acc(half, g):
                    for t in range(g * UB, (g + 1) * UB):
                        sp.dma_start(acc[:, t], x1_v[half * HB + t]).then_inc(acc_in[g], 16)

                def store_acc(half, g):
                    for t in range(g * UB, (g + 1) * UB):
                        unit = ((half + 1) * CHUNKS - 1) * TG + g
                        sp.wait_ge(add_ok, unit * YB + (t % UB + 1) * NB + 4)
                        sp.dma_start(out_v[half * HB + t], acc[:, t]).then_inc(acc_out[g], 16)

                sp.sem_inc(w_lo_ok[0], 1)
                sp.sem_inc(w_lo_ok[1], 1)
                sp.sem_inc(g_ok, 4)
                sp.sem_inc(glo_ok, 2)
                sp.sem_inc(add_ok, 4)
                sp.sem_inc(y_ok, 2 * YB)
                load_h(0, 1)
                for g in range(TG):
                    load_acc(0, g)
                load_w(1, 1)
                for half in range(HALVES):
                    with sp.Fori(2, CHUNKS) as f:
                        load_w(half * CHUNKS + f, f)
                    if half < HALVES - 1:
                        then = (half + 1) * CHUNKS
                        load_h(half + 1, 0)
                        load_w(then, 0)
                        load_h(half + 1, 1)
                        load_w(then + 1, 1)
                    for g in range(TG):
                        store_acc(half, g)
                        if half < HALVES - 1:
                            sp.wait_ge(acc_out[g], UB * 16 * (half + 1))
                            load_acc(half + 1, g)
                for g in range(TG):
                    sp.wait_ge(acc_out[g], UB * 16 * HALVES)

            @block.gpsimd
            def _(pool):
                def w2_gate(i):
                    pool.wait_ge(w_in[1], i * 16 + 16)
                    for b in range(FB):
                        g = nc.gpsimd.tensor_tensor(raw[1][:, b], raw[1][:, b], gate[:], ALU.mult)
                    g.then_inc(w2g_ok, 1)

                def unit_lo(i, g):
                    for fb in range(FB):
                        b = (i * TG + g) * FB + fb
                        pool.wait_ge(ghi_ok, b + 1)
                        nc.gpsimd.tensor_tensor(g_lo[:, g, fb], r[:, fb], f32(g_hi[:, g, fb]), ALU.subtract).then_inc(glo_ok, 1)

                def head():
                    w2_gate(0)
                    unit_lo(0, 0)

                def body(half, then, i, parity, last):
                    if not last:
                        w2_gate(i + 1)
                    unit_lo(i, 1)
                    if not last:
                        unit_lo(i + 1, 0)

                pool.wait_ge(gate_ok, NB)
                rounds(pool, head, body)

            @block.scalar
            def _(act):
                def split(i, parity, more=0):
                    act.wait_ge(y_ok, i * (TG * YB) + more)
                    for m in range(2):
                        if m == 0:
                            act.wait_ge(w_in[0], i * 16 + 16)
                        else:
                            act.wait_ge(w2g_ok, i + 1)
                        nc.scalar.copy(hi[m][:, parity], raw[m]).then_inc(w_hi_ok[m], 1)

                def unit(i, g):
                    for fb in range(FB):
                        b = (i * TG + g) * FB + fb
                        act.wait_ge(mh_ok, b + 1)
                        act.wait_ge(glo_ok, b + 1)
                        nc.scalar.activation(r[:, fb], ps_h[g * FB + fb][:], ACT.Relu).then_inc(r_ok, 1)
                        act.wait_ge(g_ok, b + 5)
                        act.wait_ge(y_ok, (i * TG + g + 1) * YB)
                        nc.scalar.copy(g_hi[:, g, fb], r[:, fb]).then_inc(ghi_ok, 1)

                def head():
                    split(0, 0, more=1)
                    unit(0, 0)

                def body(half, then, i, parity, last):
                    if not last:
                        split(i + 1, 1 - parity)
                    unit(i, 1)
                    if not last:
                        unit(i + 1, 0)

                rounds(act, head, body)

            @block.vector
            def _(dve):
                def split(i, parity):
                    for m in range(2):
                        dve.wait_ge(w_hi_ok[m], i + 1)
                        nc.vector.tensor_tensor(lo[m][:, parity], raw[m], f32(hi[m][:, parity]), ALU.subtract).then_inc(
                            w_lo_ok[m], 1)

                def squares(i, g):
                    for fb in range(FB):
                        b = (i * TG + g) * FB + fb
                        dve.wait_ge(r_ok, b + 1)
                        nc.vector.scalar_tensor_tensor(out=r[:, fb], in0=ps_h[g * FB + fb][:], scalar=0.0, in1=r[:, fb],
                                                       op0=ALU.max, op1=ALU.mult).then_inc(g_ok, 1)

                def adds(half, i, g):
                    for k in range(YB):
                        n = (i * TG + g) * YB + k
                        t = g * UB + k // NB
                        at = slice((k % NB) * BANK, (k % NB + 1) * BANK)
                        if k == 0:
                            dve.wait_ge(acc_in[g], half * (UB * 16) + UB * 16)
                        dve.wait_ge(y_ok, n + 2 * YB + 1)
                        nc.vector.tensor_tensor(acc[:, t, at], ps_y[k % 4][:], acc[:, t, at], ALU.add).then_inc(add_ok, 1)

                def head():
                    split(0, 0)
                    squares(0, 0)

                def body(half, then, i, parity, last):
                    if not last:
                        split(i + 1, 1 - parity)
                    squares(i, 1)
                    adds(half, i, 0)
                    if not last:
                        squares(i + 1, 0)
                    adds(half, i, 1)

                nc.vector.memset(ones[:], 1.0)
                diagonals(nc, keep, diag, 5 * DB).then_inc(gate_d, 1)
                dve.wait_ge(gate_m, NB)
                for n in range(NB):
                    nc.vector.tensor_copy(gate[:, n * BANK:(n + 1) * BANK], ps_y[n][:]).then_inc(gate_ok, 1)
                rounds(dve, head, body)

            @block.tensor
            def _(pe):
                def hidden(half, i, g, parity):
                    if g == 0:
                        pe.wait_ge(w_lo_ok[0], i + 2)
                    pe.wait_ge(h_in[g], half * 32 + 32)
                    for fb in range(FB):
                        b = (i * TG + g) * FB + fb
                        pe.wait_ge(g_ok, b + 1)
                        ps = ps_h[g * FB + fb][:]
                        fs = slice(fb * P, (fb + 1) * P)
                        for d in range(DB):
                            nc.tensor.matmul(ps, w1_hi[:, parity, d, fs], h_hi[g][:, d], start=(d == 0), stop=False)
                            nc.tensor.matmul(ps, w1_hi[:, parity, d, fs], h_lo[g][:, d], start=False, stop=False)
                            mm = nc.tensor.matmul(ps, w1_lo[:, parity, d, fs], h_hi[g][:, d], start=False, stop=(d == DB - 1))
                        mm.then_inc(mh_ok, 1)

                def products(i, g, parity):
                    if g == 0:
                        pe.wait_ge(w_lo_ok[1], i + 2)
                    pe.wait_ge(glo_ok, (i * TG + g) * FB + FB + 2)
                    for k in range(YB):
                        n = (i * TG + g) * YB + k
                        pe.wait_ge(add_ok, n + 1)
                        ts = slice((k // NB) * P, (k // NB + 1) * P)
                        at = slice((k % NB) * BANK, (k % NB + 1) * BANK)
                        for fb in range(FB):
                            nc.tensor.matmul(ps_y[k % 4][:], g_hi[:, g, fb, ts], w2_hi[:, parity, fb, at], start=(fb == 0), stop=False)
                            nc.tensor.matmul(ps_y[k % 4][:], g_hi[:, g, fb, ts], w2_lo[:, parity, fb, at], start=False, stop=False)
                            mm = nc.tensor.matmul(ps_y[k % 4][:], g_lo[:, g, fb, ts], w2_hi[:, parity, fb, at], start=False,
                                                  stop=(fb == FB - 1))
                        mm.then_inc(y_ok, 1)

                def head():
                    hidden(0, 0, 0, 0)

                def body(half, then, i, parity, last):
                    hidden(half, i, 1, parity)
                    products(i, 0, parity)
                    if not last:
                        hidden(then, i + 1, 0, 1 - parity)
                    products(i, 1, parity)

                pe.wait_ge(gate_d, 1)
                for n in range(NB):
                    nc.tensor.matmul(ps_y[n][:], ones[:], diag[:, 4 * n:4 * n + 4].rearrange("p b n -> p (b n)"),
                                     start=True, stop=True).then_inc(gate_m, 1)
                pe.wait_ge(gate_ok, NB)
                rounds(pe, head, body)


def decoder_layer(nc, ins, out):
    scr = Scratch(nc)
    with ExitStack() as ctx:
        keep = Persist(nc, ctx)
        with ExitStack() as both:
            over = Handover(nc, both)
            modulate(nc, ins, keep, scr, over)
            project(nc, ins, keep, scr, over)
        attend(nc, keep, scr)
        ahead = Ahead(nc, ctx, ins)
        mix(nc, ins, keep, scr, ahead)
        mlp(nc, keep, scr, ahead, out)


_INS = ["x", "c", "rel_bias", "w_ada", "b_ada", "norm_mix", "norm_mlp", "mlp_w1", "mlp_w2", "da_w_qkv", "da_w_o",
        "da_q_gain", "da_k_gain", "da_lam_q1", "da_lam_k1", "da_lam_q2", "da_lam_k2", "da_sub_gain"]


def kernel(**inputs):
    import concourse.bacc as bacc
    from concourse.bass_utils import run_bass_kernel_spmd

    nc = bacc.Bacc("TRN2", target_bir_lowering=False, num_devices=1)
    arrays, ins = {}, {}
    for name in _INS:
        a = np.ascontiguousarray(inputs[name])
        arrays[f"in_{name}"] = a
        ins[name] = nc.dram_tensor(f"in_{name}", a.shape, mybir.dt.from_np(a.dtype), kind="ExternalInput").ap()
    table = bucket_table()
    arrays["in_buckets"] = table
    ins["buckets"] = nc.dram_tensor("in_buckets", table.shape, F32, kind="ExternalInput").ap()
    out = nc.dram_tensor("out", (1, S, D), F32, kind="ExternalOutput").ap()
    decoder_layer(nc, ins, out)
    r = run_bass_kernel_spmd(nc, [arrays], core_ids=[0])
    return r.results[0]["out"]
```
